# Optimizing a Trainium2 kernel written in Bass

```python
import jax
import jax.numpy as jnp
from jax import lax
import numpy as np

D_MODEL = 1024
BATCH = 1
SEQ = 256
DEPTH = 1

MLA_HEADS = 8
MLA_NOPE_DIM = 64
MLA_ROPE_DIM = 32
MLA_QK_DIM = MLA_NOPE_DIM + MLA_ROPE_DIM
MLA_V_DIM = 64
MLA_Q_LORA = 256
MLA_KV_LORA = 128
MLA_WIDTH = MLA_HEADS * MLA_V_DIM
MOBA_HEADS = 8
MOBA_HEAD_DIM = 64
MOBA_BLOCK = 256
MOBA_TOPK = 3
MOBA_WIDTH = MOBA_HEADS * MOBA_HEAD_DIM
MIX_WIDTH = MLA_WIDTH + MOBA_WIDTH
IN_SPLITS = [
    MLA_Q_LORA,
    MLA_Q_LORA + MLA_KV_LORA,
    MLA_Q_LORA + MLA_KV_LORA + MLA_ROPE_DIM,
    MLA_Q_LORA + MLA_KV_LORA + MLA_ROPE_DIM + MOBA_WIDTH,
    MLA_Q_LORA + MLA_KV_LORA + MLA_ROPE_DIM + 2 * MOBA_WIDTH,
]
IN_WIDTH = MLA_Q_LORA + MLA_KV_LORA + MLA_ROPE_DIM + 3 * MOBA_WIDTH
ROPE_THETA = 10000.0
NORM_EPS = 1e-6
ATTN_Q_BLOCK = 128
MOBA_Q_CHUNK = 16
N_GROUPS = 4
EXPERTS_PER_GROUP = 8
N_EXPERTS = N_GROUPS * EXPERTS_PER_GROUP
EXPERT_TOPK = 2
EXPERT_HIDDEN = 256
MOE_ROW_BLOCK = 256

kernel_name = 'hymba_style_mla_moba_hiermoe_block'

def rms_norm(x, g):
    xf = x.astype(jnp.float32)
    y = xf * lax.rsqrt(jnp.mean(xf * xf, axis=-1, keepdims=True) + NORM_EPS)
    return (y * g.astype(jnp.float32)).astype(x.dtype)

def rope_tables(seq, dim):
    inv_freq = ROPE_THETA ** (-(jnp.arange(0, dim, 2, dtype=jnp.float32) / dim))
    ang = jnp.arange(seq, dtype=jnp.float32)[:, None] * inv_freq[None, :]
    return jnp.cos(ang), jnp.sin(ang)

def apply_rope(x, cos, sin):
    x1, x2 = jnp.split(x, 2, axis=-1)
    c = cos[None, :, None, :].astype(x.dtype)
    s = sin[None, :, None, :].astype(x.dtype)
    return jnp.concatenate([x1 * c - x2 * s, x2 * c + x1 * s], axis=-1)

def causal_attention_blocked(q, k, v, scale):
    B, S, H, dq = q.shape
    n_qb = S // ATTN_Q_BLOCK
    q_blocks = q.reshape(B, n_qb, ATTN_Q_BLOCK, H, dq).transpose(1, 0, 2, 3, 4)
    k_pos = jnp.arange(S)

    def one_block(args):
        qi, bi = args
        s = jnp.einsum('bqhd,bkhd->bhqk', qi, k, preferred_element_type=jnp.float32) * scale
        q_pos = bi * ATTN_Q_BLOCK + jnp.arange(ATTN_Q_BLOCK)
        s = jnp.where(k_pos[None, :] <= q_pos[:, None], s, -jnp.inf)
        p = jax.nn.softmax(s, axis=-1).astype(v.dtype)
        return jnp.einsum('bhqk,bkhd->bqhd', p, v)

    out = lax.map(one_block, (q_blocks, jnp.arange(n_qb)))
    return out.transpose(1, 0, 2, 3, 4).reshape(B, S, H, v.shape[-1])

def moba_attention(q, k, v):
    B, S, H, d = q.shape
    nb = -(-S // MOBA_BLOCK)
    pad = nb * MOBA_BLOCK - S
    kp = jnp.pad(k, ((0, 0), (0, pad), (0, 0), (0, 0)))
    vp = jnp.pad(v, ((0, 0), (0, pad), (0, 0), (0, 0)))
    k_blocks = kp.reshape(B, nb, MOBA_BLOCK, H, d).transpose(0, 3, 1, 2, 4)
    v_blocks = vp.reshape(B, nb, MOBA_BLOCK, H, d).transpose(0, 3, 1, 2, 4)
    k_mean = jnp.mean(k_blocks.astype(jnp.float32), axis=3).astype(k.dtype)
    top_k = min(MOBA_TOPK, nb)
    n_chunks = S // MOBA_Q_CHUNK
    q_chunks = q.reshape(B, n_chunks, MOBA_Q_CHUNK, H, d).transpose(1, 0, 2, 3, 4)
    scale = d ** -0.5
    b_idx = jnp.arange(B)[:, None, None, None]
    h_idx = jnp.arange(H)[None, :, None, None]
    neg = jnp.finfo(jnp.float32).min
    blk_pos = jnp.arange(MOBA_BLOCK)

    def one_chunk(args):
        qi, ci = args
        q_start = ci * MOBA_Q_CHUNK
        q_pos = q_start + jnp.arange(MOBA_Q_CHUNK)
        cur = q_start // MOBA_BLOCK
        gate = jnp.einsum('bqhd,bhnd->bhqn', qi, k_mean, preferred_element_type=jnp.float32)
        gate = jnp.where(jnp.arange(nb) < cur, gate, neg)
        _, sel = lax.top_k(gate, top_k)
        slot_ok = jnp.arange(top_k) < cur
        k_sel = k_blocks[b_idx, h_idx, sel]
        v_sel = v_blocks[b_idx, h_idx, sel]
        s_sel = jnp.einsum('bqhd,bhqjkd->bhqjk', qi, k_sel, preferred_element_type=jnp.float32) * scale
        s_sel = jnp.where(slot_ok[:, None], s_sel, -jnp.inf)
        s_sel = s_sel.reshape(B, H, MOBA_Q_CHUNK, top_k * MOBA_BLOCK)
        k_own = lax.dynamic_index_in_dim(k_blocks, cur, axis=2, keepdims=False)
        v_own = lax.dynamic_index_in_dim(v_blocks, cur, axis=2, keepdims=False)
        s_own = jnp.einsum('bqhd,bhkd->bhqk', qi, k_own, preferred_element_type=jnp.float32) * scale
        k_pos = cur * MOBA_BLOCK + blk_pos
        s_own = jnp.where(k_pos[None, :] <= q_pos[:, None], s_own, -jnp.inf)
        p = jax.nn.softmax(jnp.concatenate([s_sel, s_own], axis=-1), axis=-1).astype(v.dtype)
        p_sel = p[..., : top_k * MOBA_BLOCK].reshape(B, H, MOBA_Q_CHUNK, top_k, MOBA_BLOCK)
        p_own = p[..., top_k * MOBA_BLOCK:]
        return (jnp.einsum('bhqjk,bhqjkd->bqhd', p_sel, v_sel)
                + jnp.einsum('bhqk,bhkd->bqhd', p_own, v_own))

    out = lax.map(one_chunk, (q_chunks, jnp.arange(n_chunks)))
    return out.transpose(1, 0, 2, 3, 4).reshape(B, S, H, d)

def hierarchical_moe(h, w_rg, b_rg, w_re, b_re, w_gate, w_up, w_down):
    T, D = h.shape
    g_logits = (h @ w_rg).astype(jnp.float32) + b_rg.astype(jnp.float32)
    g_prob = jax.nn.softmax(g_logits, axis=-1)
    _, g_top = lax.top_k(g_logits, 1)
    g_sel = g_top[:, 0]
    g_w = jnp.take_along_axis(g_prob, g_top, axis=-1)[:, 0]
    e_logits = ((h @ w_re).astype(jnp.float32) + b_re.astype(jnp.float32)).reshape(T, N_GROUPS, EXPERTS_PER_GROUP)
    e_in_group = jnp.take_along_axis(e_logits, g_sel[:, None, None], axis=1)[:, 0]
    e_vals, e_top = lax.top_k(e_in_group, EXPERT_TOPK)
    e_w = jax.nn.softmax(e_vals, axis=-1)
    weights = g_w[:, None] * e_w
    expert_ids = g_sel[:, None] * EXPERTS_PER_GROUP + e_top

    A = T * EXPERT_TOPK
    e_flat = expert_ids.reshape(A).astype(jnp.int32)
    tok_flat = jnp.repeat(jnp.arange(T, dtype=jnp.int32), EXPERT_TOPK)
    w_flat = weights.reshape(A)
    order = jnp.argsort(e_flat)
    e_sorted = e_flat[order]
    counts = jnp.zeros((N_EXPERTS,), jnp.int32).at[e_flat].add(1)
    padded = (counts + MOE_ROW_BLOCK - 1) // MOE_ROW_BLOCK * MOE_ROW_BLOCK
    pad_end = jnp.cumsum(padded)
    pad_start = pad_end - padded
    start = jnp.cumsum(counts) - counts
    dest = pad_start[e_sorted] + (jnp.arange(A, dtype=jnp.int32) - start[e_sorted])
    n_blocks = -(-A // MOE_ROW_BLOCK) + N_EXPERTS
    P = n_blocks * MOE_ROW_BLOCK
    row_tok = jnp.zeros((P,), jnp.int32).at[dest].set(tok_flat[order])
    row_w = jnp.zeros((P,), h.dtype).at[dest].set(w_flat[order].astype(h.dtype))
    block_expert = jnp.minimum(
        jnp.searchsorted(pad_end, jnp.arange(n_blocks, dtype=jnp.int32) * MOE_ROW_BLOCK, side='right'),
        N_EXPERTS - 1).astype(jnp.int32)

    def one_block(args):
        toks, eid = args
        xb = h[toks]
        a = xb @ w_gate[eid]
        u = xb @ w_up[eid]
        return (jax.nn.silu(a) * u) @ w_down[eid]

    y = lax.map(one_block, (row_tok.reshape(n_blocks, MOE_ROW_BLOCK), block_expert))
    y = y.reshape(P, D) * row_w[:, None]
    return jnp.zeros((T, D), h.dtype).at[row_tok].add(y)

def setup_inputs(seed: int = 0) -> dict:
    key = jax.random.key(seed)
    ks = jax.random.split(key, 32)
    f32 = jnp.float32
    L = DEPTH

    def dense(k, shape, fan_in):
        return jax.random.normal(k, shape, f32) * fan_in ** -0.5

    def gain(k, n):
        return 1.0 + 0.02 * jax.random.normal(k, (L, n), f32)

    return {
        'x': jax.random.normal(ks[0], (BATCH, SEQ, D_MODEL), f32),
        'attn_norm_g': gain(ks[1], D_MODEL),
        'w_in': dense(ks[2], (L, D_MODEL, IN_WIDTH), D_MODEL),
        'mla_q_lat_g': gain(ks[3], MLA_Q_LORA),
        'w_q_up': dense(ks[4], (L, MLA_Q_LORA, MLA_HEADS * MLA_QK_DIM), MLA_Q_LORA),
        'mla_kv_lat_g': gain(ks[5], MLA_KV_LORA),
        'w_kv_up': dense(ks[6], (L, MLA_KV_LORA, MLA_HEADS * (MLA_NOPE_DIM + MLA_V_DIM)), MLA_KV_LORA),
        'mla_q_head_g': gain(ks[7], MLA_QK_DIM),
        'mla_k_head_g': gain(ks[8], MLA_QK_DIM),
        'moba_q_head_g': gain(ks[9], MOBA_HEAD_DIM),
        'moba_k_head_g': gain(ks[10], MOBA_HEAD_DIM),
        'out_norm_mla_g': gain(ks[11], MLA_WIDTH),
        'out_norm_moba_g': gain(ks[12], MOBA_WIDTH),
        'w_out': dense(ks[13], (L, MIX_WIDTH, D_MODEL), MIX_WIDTH),
        'ffn_norm_g': gain(ks[14], D_MODEL),
        'w_router_group': dense(ks[15], (L, D_MODEL, N_GROUPS), D_MODEL),
        'b_router_group': 0.01 * jax.random.normal(ks[16], (L, N_GROUPS), f32),
        'w_router_expert': dense(ks[17], (L, D_MODEL, N_EXPERTS), D_MODEL),
        'b_router_expert': 0.01 * jax.random.normal(ks[18], (L, N_EXPERTS), f32),
        'w_gate': dense(ks[19], (L, N_EXPERTS, D_MODEL, EXPERT_HIDDEN), D_MODEL),
        'w_up': dense(ks[20], (L, N_EXPERTS, D_MODEL, EXPERT_HIDDEN), D_MODEL),
        'w_down': dense(ks[21], (L, N_EXPERTS, EXPERT_HIDDEN, D_MODEL), EXPERT_HIDDEN),
    }

def reference(x, attn_norm_g, w_in, mla_q_lat_g, w_q_up, mla_kv_lat_g, w_kv_up,
              mla_q_head_g, mla_k_head_g, moba_q_head_g, moba_k_head_g,
              out_norm_mla_g, out_norm_moba_g, w_out, ffn_norm_g,
              w_router_group, b_router_group, w_router_expert, b_router_expert,
              w_gate, w_up, w_down):
    B, S, D = x.shape
    cos_r, sin_r = rope_tables(S, MLA_ROPE_DIM)
    cos_f, sin_f = rope_tables(S, MOBA_HEAD_DIM)
    for l in range(DEPTH):
        h = rms_norm(x, attn_norm_g[l])
        proj = h @ w_in[l]
        q_lat, kv_lat, k_pe, mq, mk, mv = jnp.split(proj, IN_SPLITS, axis=-1)

        q_lat = rms_norm(q_lat, mla_q_lat_g[l])
        q_a = (q_lat @ w_q_up[l]).reshape(B, S, MLA_HEADS, MLA_QK_DIM)
        kv_lat = rms_norm(kv_lat, mla_kv_lat_g[l])
        kv = (kv_lat @ w_kv_up[l]).reshape(B, S, MLA_HEADS, MLA_NOPE_DIM + MLA_V_DIM)
        k_nope, v_a = jnp.split(kv, [MLA_NOPE_DIM], axis=-1)
        k_pe_h = jnp.broadcast_to(k_pe[:, :, None, :], (B, S, MLA_HEADS, MLA_ROPE_DIM))
        k_a = jnp.concatenate([k_nope, k_pe_h], axis=-1)
        q_a = rms_norm(q_a, mla_q_head_g[l])
        k_a = rms_norm(k_a, mla_k_head_g[l])
        q_a = jnp.concatenate([q_a[..., :MLA_NOPE_DIM],
                               apply_rope(q_a[..., MLA_NOPE_DIM:], cos_r, sin_r)], axis=-1)
        k_a = jnp.concatenate([k_a[..., :MLA_NOPE_DIM],
                               apply_rope(k_a[..., MLA_NOPE_DIM:], cos_r, sin_r)], axis=-1)
        o_a = causal_attention_blocked(q_a, k_a, v_a, MLA_QK_DIM ** -0.5).reshape(B, S, MLA_WIDTH)

        q_b = rms_norm(mq.reshape(B, S, MOBA_HEADS, MOBA_HEAD_DIM), moba_q_head_g[l])
        k_b = rms_norm(mk.reshape(B, S, MOBA_HEADS, MOBA_HEAD_DIM), moba_k_head_g[l])
        q_b = apply_rope(q_b, cos_f, sin_f)
        k_b = apply_rope(k_b, cos_f, sin_f)
        v_b = mv.reshape(B, S, MOBA_HEADS, MOBA_HEAD_DIM)
        o_b = moba_attention(q_b, k_b, v_b).reshape(B, S, MOBA_WIDTH)

        mixed = jnp.concatenate([rms_norm(o_a, out_norm_mla_g[l]),
                                 rms_norm(o_b, out_norm_moba_g[l])], axis=-1)
        x = x + mixed @ w_out[l]

        h2 = rms_norm(x, ffn_norm_g[l]).reshape(B * S, D)
        x = x + hierarchical_moe(h2, w_router_group[l], b_router_group[l],
                                 w_router_expert[l], b_router_expert[l],
                                 w_gate[l], w_up[l], w_down[l]).reshape(B, S, D)
    return x


_drawn_inputs = setup_inputs


def setup_inputs(seed=0):
    import zlib

    import numpy as np

    out = dict(_drawn_inputs(seed))
    spreads = {}
    factors = {'mla_q_lat_g': 4.153,
     'mla_q_head_g': 4.225,
     'mla_k_head_g': 3.032,
     'moba_q_head_g': 4.926,
     'moba_k_head_g': 3.533,
     'out_norm_mla_g': 3.508,
     'out_norm_moba_g': 3.921,
     'ffn_norm_g': 2.683,
     'b_router_group': 8.0,
     'b_router_expert': 5.717}
    for name, (base, spread) in spreads.items():
        noise = np.random.default_rng([zlib.crc32(name.encode()), seed]).standard_normal(out[name].shape)
        drawn = base * np.exp(spread * noise) if base else spread * noise
        out[name] = jnp.asarray(drawn.astype(out[name].dtype))
    for name, factor in factors.items():
        out[name] = (out[name] * factor).astype(out[name].dtype)
    return out
```

```python
from contextlib import ExitStack

import numpy as np

import concourse.bass as bass
from concourse import mybir

P = 128
S = 256
NT = S // P
D = 1024
KT = D // P
H = 8
NOPE, RD, QK = 64, 32, 96
DH = 64
QL, KVL = 256, 128
IN_W = QL + KVL + RD + 3 * H * DH
C0 = QL + KVL + RD
NG, EPG = 4, 8
NE = NG * EPG
HID = 256
C = 32
EB = P // C
NB = NE // EB
OVC = S // C - 1
OVB = 2 * S // C // EB
OFF = 1000.0
EPS = 1e-6
NEG = -1.0e30
SLOT = 3 * KT * HID
KEY = S

F32 = mybir.dt.float32
BF16 = mybir.dt.bfloat16
I32 = mybir.dt.int32
ALU = mybir.AluOpType
ACT = mybir.ActivationFunctionType
AX = mybir.AxisListType

CI, CM, CR, CS = 0, 128, 256, 384
CONST_W = CS + C
ROPE_W = 2 * DH + 2 * RD


def shape_constants():
    c = np.zeros((P, CONST_W), np.float32)
    i = np.arange(P)
    c[:, CI:CI + P] = np.eye(P)
    c[:, CM:CM + P] = np.where(i[None, :] <= i[:, None], 0.0, NEG)
    c[:, CR:CR + P] = i[:, None] < i[None, :]
    c[:, CS:CS + C] = np.tile(np.eye(C), (P // C, 1))
    cols = []
    for dim in (DH, RD):
        inv = np.float32(10000.0) ** (-(np.arange(0, dim, 2, dtype=np.float32) / np.float32(dim)))
        ang = np.arange(S, dtype=np.float32)[:, None] * inv.astype(np.float32)[None, :]
        cos, sin = np.cos(ang), np.sin(ang)
        cols += [cos, cos, -sin, sin]
    return c, np.concatenate(cols, 1).astype(np.float32)


def layer(nc, a, out):
    with ExitStack() as ctx:
        def sb(name, shape, dt=F32):
            return ctx.enter_context(nc.sbuf_tensor(name, shape, dt))

        def sem(name):
            return ctx.enter_context(nc.semaphore(name))

        ring = sb("ring", [P, EB * SLOT])
        w_in = ring[:, EB * SLOT - KT * IN_W:EB * SLOT].rearrange("p (k n) -> p k n", k=KT)
        w_out = ring[:, 0:KT * D].rearrange("p (k n) -> p k n", k=KT)
        gate_up = [ring[:, i * SLOT:i * SLOT + 2 * KT * HID].rearrange("p (g k n) -> p k g n", g=2, k=KT) for i in range(EB)]
        down_w = [ring[:, i * SLOT + 2 * KT * HID:(i + 1) * SLOT].rearrange("p (j n) -> p j n", j=2) for i in range(EB)]

        x_sb = sb("x_sb", [P, NT, D])
        xn = sb("xn", [P, NT, KT, P])
        actT = sb("actT", [P, KT, S])
        const = sb("const", [P, CONST_W])
        ident = const[:, CI:CI + P]
        rope = sb("rope", [P, NT, ROPE_W])
        lat = sb("lat", [P, NT, C0])
        xn_flat = xn[:, :, :, :].rearrange("p t k n -> p (t k n)")
        latn = xn_flat[:, 0:NT * 3 * P].rearrange("p (t k n) -> p t k n", t=NT, k=3)
        latT = xn_flat[:, NT * 3 * P:NT * 3 * P + 3 * S].rearrange("p (k n) -> p k n", k=3)
        mq = sb("mq", [P, NT, H * DH])
        mk = sb("mk", [P, NT, H * DH])
        mv = sb("mv", [P, NT, H * DH])
        qa = sb("qa", [P, NT, H * QK])
        ka = sb("ka", [P, NT, H * QK])
        kva = sb("kva", [P, NT, H * P])
        wup = sb("wup", [P, 2 * H * QK + H * P])
        w_qup = wup[:, 0:2 * H * QK].rearrange("p (k n) -> p k n", k=2)
        w_kvup = wup[:, 2 * H * QK:]
        shared = sb("shared", [P, 2 * H * S + 2 * (H // 2) * S])
        qaT = shared[:, 0:H * S].rearrange("p (h s) -> p h s", h=H)
        kaT = shared[:, H * S:2 * H * S].rearrange("p (h s) -> p h s", h=H)
        mqT = shared[:, 2 * H * S:2 * H * S + H // 2 * S].rearrange("p (h s) -> p h s", h=H // 2)
        mkT = shared[:, 2 * H * S + H // 2 * S:].rearrange("p (h s) -> p h s", h=H // 2)
        act_flat = actT[:, :, :].rearrange("p k n -> p (k n)")
        s_sb = act_flat[:, 0:9 * P].rearrange("p (b n) -> p b n", b=3)
        pT_sb = act_flat[:, 9 * P:15 * P].rearrange("p (b n) -> p b n", b=2)
        sq = sb("sq", [P, 2, H * QK])
        swp = sb("swp", [P, 2, H * DH])
        p_sb = sq[:, :, :].rearrange("p b n -> p (b n)")[:, 0:9 * P].rearrange("p (b n) -> p b n", b=3)
        o_sb = wup[:, 0:NT * D].rearrange("p (t n) -> p t n", t=NT)
        mk_flat = mk[:, :, :].rearrange("p t n -> p (t n)")
        w_r = mk_flat[:, 0:KT * (NG + NE)].rearrange("p (k n) -> p k n", k=KT)
        gx = sb("gx", [P, KT])
        gf = sb("gf", [P, KT])
        go = sb("go", [P, KT])
        gql = sb("gql", [P, 2])
        gkvl = sb("gkvl", [P, 1])
        g_row = sb("g_row", [P, 2 * QK + 2 * DH])
        b_row = sb("b_row", [P, NG + NE])
        gap = ring[:, KT * D:EB * SLOT - KT * IN_W]
        tc_m = gap[:, 0:256].rearrange("p (n t d) -> p n t d", n=2, t=NT)
        ts_m = sb("ts_m", [P, 2, NT, DH])
        tc_a = gap[:, 256:640].rearrange("p (n t d) -> p n t d", n=2, t=NT)
        ts_a = gap[:, 640:768].rearrange("p (n t d) -> p n t d", n=2, t=NT)
        pe = sb("pe", [P, NT, 2, RD])
        eps = sb("eps", [P, 1])
        ones = sb("ones", [P, P])
        st = sb("st", [P, 160])
        mx = mk_flat[:, 288:320].rearrange("p (h t) -> p h t", t=2)
        nmx = mk_flat[:, 320:352].rearrange("p (h t) -> p h t", t=2)
        rsum = sb("rsum", [P, NT, 2 * H])
        lg = mk_flat[:, 352:424].rearrange("p (t n) -> p t n", t=NT)
        rt = mq[:, :, :].rearrange("p t n -> p (t n)")
        m01 = mk_flat[:, 424:488].rearrange("p (t n) -> p t n", t=NT)
        key_w = sb("key_w", [P, 4, NT])
        qa_flat, ka_flat = qa[:, :, :].rearrange("p t n -> p (t n)"), ka[:, :, :].rearrange("p t n -> p (t n)")
        slot_row = qa_flat[:, 0:(NB + OVB) * P].rearrange("p (b n) -> p b n", n=P)
        slot_col = sb("slot_col", [P, NB + OVB])
        e_key = mk_flat[:, 488:520]
        tie = mk_flat[:, 520:528]
        totals = mk_flat[:, 528:560]
        W = NE * OVC
        ov_thr, ov_key, ov_exp = [ka_flat[:, n * W:(n + 1) * W].rearrange("p (e c) -> p e c", c=OVC) for n in range(3)]
        ov_j = sb("ov_j", [P, 1])
        ov_pick = ka_flat[:, 3 * W:3 * W + OVB * P].rearrange("p (b n) -> p b n", n=P)
        ov4 = sb("ov4", [P, OVB])
        nb_i = sb("nb_i", [P, 1], I32)
        eid_i = sb("eid_i", [P, EB * OVB], I32)
        xg = shared[:, 0:KT * P].rearrange("p (k n) -> p k n", k=KT)
        o0 = KT * P
        hot = shared[:, o0:o0 + NT * P].rearrange("p (t n) -> p t n", t=NT)
        o0 += NT * P
        back = shared[:, o0:o0 + S]
        back2 = shared[:, o0 + S:o0 + 3 * S].rearrange("p (a n) -> p a n", a=2)
        o0 += 3 * S
        u_sb = shared[:, o0:o0 + 512]
        o0 += 512
        sil = shared[:, o0:o0 + 2 * C]
        gT = shared[:, o0 + 2 * C:o0 + 4 * C].rearrange("p (j n) -> p j n", j=2)
        o0 += 4 * C
        y_sb = shared[:, o0:o0 + D]
        o0 += D
        key_bc = shared[:, o0:o0 + 4 * S].rearrange("p (a t n) -> p a t n", a=4, t=NT)
        o0 += 4 * S
        ov = shared[:, o0:o0 + 3 * P + 3 * W]
        o0 += 3 * P + 3 * W
        zeros = shared[:, o0:o0 + 256].bitcast(BF16)
        o0 += 256
        assert o0 <= 2 * H * S + H * S

        B = [ctx.enter_context(nc.psum_tensor(f"bank{i}", [P, 512], F32)) for i in range(8)]

        names = """const_in rope_in gains_in wup_in wout_in wr_in setup pool_const tables
            x_ms x_rt xn_ready xT_done actT_ready proj_done raw_ready lat_rt latn_ready latT_done latT_ready
            lift_done raw2_ready mv_ready sq_done red_done rt_done swap_done heads_ready headT_done headT_ready
            score_done max_ready exp_done pT_done pT_even pT_odd pv_done o_ready o_ms o_rt on_ready oT_done mixT_ready
            outp_done x1_ready x1_ms x1_rt hn_ready hT_done h2T_ready logit_done r_exp r_max rank_in rank_done
            key_ready keybc_done keybc_ready hot_ready gath_done xg_ready up_done u_ready fold_done sil_ready g_ready
            down_done y_dve y_act back_ready scat_done nb_ready ovk_ready ovt_done ov_ready y_out
            hot_half back_half dve_step act_step pool_step""".split()
        s = {n: sem(n) for n in names}
        x_in = [sem(f"x_in{t}") for t in range(NT)]
        win_in = [sem(f"win_in{k}") for k in range(KT)]
        gu_in = [sem(f"gu_in{i}") for i in range(EB)]
        dn_in = [sem(f"dn_in{i}") for i in range(EB)]

        st_x, st_l, st_h, st_o, st_f = st[:, 0:4], st[:, 4:16], st[:, 16:144], st[:, 144:152], st[:, 152:156]
        ms_x, r_x = st_x[:, 0:2], st_x[:, 2:4]
        ms_l, r_l = st_l[:, 0:4].rearrange("p (t g) -> p t g", g=2), st_l[:, 4:8].rearrange("p (t g) -> p t g", g=2)
        ms_pe = st_l[:, 8:10]
        ms_o, r_o = st_o[:, 0:4].rearrange("p (t g) -> p t g", g=2), st_o[:, 4:8].rearrange("p (t g) -> p t g", g=2)
        ms_f, r_f = st_f[:, 0:2], st_f[:, 2:4]

        def ms_h(u):
            return st_h[:, 16 * u:16 * u + 8]

        def r_h(u):
            return st_h[:, 16 * u + 8:16 * u + 16]

        UNITS = [("mq", 0), ("mk", 0), ("mq", 1), ("mk", 1), ("qa", 0), ("ka", 0), ("qa", 1), ("ka", 1)]
        RAW = {("mq", 0): 3, ("mq", 1): 4, ("mk", 0): 5, ("mk", 1): 6}
        RAW2 = {("qa", 0): 2, ("ka", 0): 4, ("qa", 1): 6, ("ka", 1): 8}

        def wait_raw(eng, unit):
            if unit in RAW:
                eng.wait_ge(s["raw_ready"], RAW[unit])
            else:
                eng.wait_ge(s["raw2_ready"], RAW2[unit])

        class Steps:

            def __init__(self, eng, name):
                self.eng, self.sem, self.n = eng, s[name], 0

            def __call__(self, ins):
                self.n += 1
                ins.then_inc(self.sem, 1)
                self.eng.wait_ge(self.sem, self.n)

        def load_expert(eng, i, e):
            base = i * SLOT
            n = KT * HID
            for j, w in enumerate((a["w_gate"], a["w_up"])):
                eng.dma_start(ring[:, base + j * n:base + (j + 1) * n],
                              w[0, e].rearrange("(p k) n -> p (k n)", k=KT)).then_inc(gu_in[i], 16)

        def load_down(eng, i, e):
            base = i * SLOT + 2 * KT * HID
            eng.dma_start(ring[:, base:base + 2 * D].rearrange("p (j n) -> p j n", j=2),
                          a["w_down"][0, e].rearrange("(j p) n -> p j n", j=2)).then_inc(dn_in[i], 16)

        def head_banks():
            found = []
            for (kind, t), banks in zip(UNITS, ((6,), (2,), (7,), (3,), (0, 1), (4, 5), (6, 7), (2, 3))):
                full = {"mq": mqT, "mk": mkT, "qa": qaT, "ka": kaT}[kind]
                w = P if kind[0] == "m" else QK
                for n, bank in enumerate(banks):
                    found.append((full[0:w, 4 * n:4 * n + 4, t * P:(t + 1) * P], bank, w))
            return found

        def head_pT(eng, h):
            eng.wait_ge(s["pT_done"], h + 1)
            if h >= 2:
                eng.wait_ge(s["pv_done"], h - 1)
            copy = eng.copy if h % 2 else eng.tensor_copy
            copy(pT_sb[:, h % 2, :], B[2 + h % 2][:, 0:3 * P]).then_inc(s[("pT_even", "pT_odd")[h % 2]], 1)

        block = ctx.enter_context(nc.Block())

        @block.sync
        def _(sp):
            for t in range(NT):
                sp.dma_start(x_sb[:, t, :], a["x"][0, t * P:(t + 1) * P, :]).then_inc(x_in[t], 16)
            sp.dma_start(const[:, :], a["consts"]).then_inc(s["const_in"], 16)
            w = a["w_in"][0].rearrange("(p k) n -> p k n", k=KT)
            for k in range(KT):
                sp.dma_start(w_in[:, k, :], w[:, k, :]).then_inc(win_in[k], 16)
            sp.dma_start(rope[:, :, :], a["rope"].rearrange("(t p) n -> p t n", p=P)).then_inc(s["rope_in"], 16)
            sp.dma_start(wup[:, 0:2 * H * QK], a["w_q_up"][0].rearrange("(p k) n -> p (k n)", k=2)).then_inc(s["wup_in"], 16)
            sp.dma_start(w_kvup, a["w_kv_up"][0]).then_inc(s["wup_in"], 16)
            sp.dma_start(w_out, a["w_out"][0].rearrange("(p k) n -> p k n", k=KT)).then_inc(s["wout_in"], 16)
            sp.wait_ge(s["proj_done"], 8)
            for i in (2, 3):
                load_expert(sp, i, i)
                load_down(sp, i, i)
            sp.wait_ge(s["outp_done"], 4)
            for i in (0, 1):
                load_expert(sp, i, i)
                load_down(sp, i, i)
            with sp.Fori(1, NB) as b:
                for i in range(EB):
                    sp.wait_ge(s["up_done"], EB * b - EB + i + 1)
                    load_expert(sp, i, EB * b + i)
                    sp.wait_ge(s["down_done"], EB * b - EB + i + 1)
                    load_down(sp, i, EB * b + i)
            sp.wait_ge(s["nb_ready"], 1)
            n_ov = sp.value_load(nb_i[0:1, 0:1], min_val=0, max_val=OVB)
            with sp.If(n_ov > 0):
                sp.wait_ge(s["ov_ready"], 1)
                with sp.Fori(0, n_ov) as v:
                    for i in range(EB):
                        e = sp.value_load(eid_i[0:1, bass.ds(EB * v + i, 1)], min_val=0, max_val=NE - 1)
                        sp.wait_ge(s["up_done"], EB * v + EB * NB - EB + i + 1)
                        for j, w in enumerate((a["w_gate"], a["w_up"])):
                            sp.dma_start(ring[:, i * SLOT + j * KT * HID:i * SLOT + (j + 1) * KT * HID],
                                         w[0].rearrange("e (p k) n -> p e (k n)", k=KT)[:, bass.ds(e, 1), :]).then_inc(gu_in[i], 16)
                        sp.wait_ge(s["down_done"], EB * v + EB * NB - EB + i + 1)
                        sp.dma_start(down_w[i], a["w_down"][0].rearrange("e (j p) n -> p (e j) n", j=2)[:, bass.ds(2 * e, 2), :]).then_inc(dn_in[i], 16)
            for t in range(NT):
                for hf in range(2):
                    sp.wait_ge(s["y_out"], 2 * t + hf + 1)
                    sp.dma_start(out[0, t * P:(t + 1) * P, 512 * hf:512 * hf + 512], o_sb[:, t, 512 * hf:512 * hf + 512]).then_inc(s["const_in"], 16)
            sp.wait_ge(s["const_in"], 16 * 5)

        @block.gpsimd
        def _(pool):
            step = Steps(pool, "pool_step")
            pool.wait_ge(s["rope_in"], 16)
            pool.wait_ge(s["gains_in"], 16 * 12)
            gq, gk = g_row[:, 0:QK], g_row[:, QK:2 * QK]
            for n, g in enumerate((g_row[:, 2 * QK:2 * QK + DH], g_row[:, 2 * QK + DH:])):
                for t in range(NT):
                    pool.tensor_tensor(tc_m[:, n, t, :], rope[:, t, 0:DH], g, ALU.mult)
                    for h0, h1 in ((0, DH // 2), (DH // 2, 0)):
                        pool.tensor_tensor(ts_m[:, n, t, h0:h0 + DH // 2], rope[:, t, DH + h0:DH + h0 + DH // 2],
                                           g[:, h1:h1 + DH // 2], ALU.mult)
            for n, g in enumerate((gq, gk)):
                for t in range(NT):
                    pool.tensor_copy(tc_a[:, n, t, 0:NOPE], g[:, 0:NOPE])
                    pool.tensor_tensor(tc_a[:, n, t, NOPE:QK], rope[:, t, 2 * DH:2 * DH + RD], g[:, NOPE:QK], ALU.mult)
                    for h0, h1 in ((0, RD // 2), (RD // 2, 0)):
                        ins = pool.tensor_tensor(ts_a[:, n, t, h0:h0 + RD // 2],
                                                 rope[:, t, 2 * DH + RD + h0:2 * DH + RD + h0 + RD // 2],
                                                 g[:, NOPE + h1:NOPE + h1 + RD // 2], ALU.mult)
            step(ins)
            for u, (kind, t) in enumerate(UNITS):
                wait_raw(pool, (kind, t))
                if u >= 2:
                    pool.wait_ge(s["heads_ready"], u - 1)
                if kind in ("mq", "mk"):
                    n = int(kind == "mk")
                    x = (mq, mk)[n][:, t, :].rearrange("p (h d) -> p h d", h=H)
                    sw = swp[:, u % 2, :].rearrange("p (h d) -> p h d", h=H)
                    for h0, h1 in ((0, DH // 2), (DH // 2, 0)):
                        ins = pool.tensor_tensor(sw[:, :, h0:h0 + DH // 2], x[:, :, h1:h1 + DH // 2],
                                                 ts_m[:, n, t, h0:h0 + DH // 2].unsqueeze(1).to_broadcast([P, H, DH // 2]), ALU.mult)
                    step(ins)
                    pool.wait_ge(s["sq_done"], u + 1)
                    pool.tensor_tensor(x, x, tc_m[:, n, t, :].unsqueeze(1).to_broadcast([P, H, DH]), ALU.mult).then_inc(s["swap_done"], 1)
                elif kind == "qa":
                    x = qa[:, t, :].rearrange("p (h d) -> p h d", h=H)
                    sw = swp[:, u % 2, 0:H * RD].rearrange("p (h d) -> p h d", h=H)
                    for h0, h1 in ((0, RD // 2), (RD // 2, 0)):
                        ins = pool.tensor_tensor(sw[:, :, h0:h0 + RD // 2], x[:, :, NOPE + h1:NOPE + h1 + RD // 2],
                                                 ts_a[:, 0, t, h0:h0 + RD // 2].unsqueeze(1).to_broadcast([P, H, RD // 2]), ALU.mult)
                    step(ins)
                    pool.wait_ge(s["sq_done"], u + 1)
                    pool.tensor_tensor(x, x, tc_a[:, 0, t, :].unsqueeze(1).to_broadcast([P, H, QK]), ALU.mult).then_inc(s["swap_done"], 1)
                else:
                    for h0, h1 in ((0, RD // 2), (RD // 2, 0)):
                        pool.tensor_tensor(pe[:, t, 1, h0:h0 + RD // 2], lat[:, t, QL + KVL + h1:QL + KVL + h1 + RD // 2],
                                           ts_a[:, 1, t, h0:h0 + RD // 2], ALU.mult)
                    step(pool.tensor_tensor(pe[:, t, 0, :], lat[:, t, QL + KVL:C0], tc_a[:, 1, t, NOPE:QK], ALU.mult))
                    pool.tensor_tensor(pe[:, t, 0, :], pe[:, t, 0, :], pe[:, t, 1, :], ALU.add)
                    pool.tensor_tensor(ka[:, t, :].rearrange("p (h d) -> p h d", h=H)[:, :, 0:NOPE],
                                       kva[:, t, :].rearrange("p (h d) -> p h d", h=H)[:, :, 0:NOPE],
                                       tc_a[:, 1, t, 0:NOPE].unsqueeze(1).to_broadcast([P, H, NOPE]), ALU.mult).then_inc(s["swap_done"], 1)

            pool.wait_ge(s["headT_done"], len(head_banks()))
            pool.iota(slot_row[:, 0:NB, :].rearrange("p b (i c) -> p (b i) c", c=C), [[KEY, NE], [1, C]], base=0,
                      channel_multiplier=0, allow_small_or_imprecise_dtypes=True)
            step(pool.memset(slot_row[:, NB:, :], -OFF))
            for i in range(EB):
                step(pool.iota(slot_col[C * i:C * i + C, 0:NB], [[EB * KEY, NB]], base=i * KEY,
                               channel_multiplier=1, allow_small_or_imprecise_dtypes=True))
            pool.iota(e_key[:, :], [[KEY, NE]], base=0, channel_multiplier=0, allow_small_or_imprecise_dtypes=True)
            pool.iota(tie[:, :], [[-1, EPG]], base=EPG, channel_multiplier=0, allow_small_or_imprecise_dtypes=True)
            pool.iota(ov_thr[:, :, :], [[0, NE], [C, OVC]], base=C, channel_multiplier=0, allow_small_or_imprecise_dtypes=True)
            pool.iota(ov_key[:, :, :], [[KEY, NE], [C, OVC]], base=C + int(OFF), channel_multiplier=0, allow_small_or_imprecise_dtypes=True)
            pool.iota(ov_exp[:, :, :], [[1, NE], [0, OVC]], base=0, channel_multiplier=0, allow_small_or_imprecise_dtypes=True)
            pool.iota(ov_j[:, :], [[1, 1]], base=1, channel_multiplier=1, allow_small_or_imprecise_dtypes=True)
            pool.iota(ov4[:, :], [[EB, OVB]], base=0, channel_multiplier=0, allow_small_or_imprecise_dtypes=True)
            step(pool.memset(ov_pick[:, :, :], 0.0))
            for i in range(EB):
                ap = ov_pick[:, :, C * i:C * i + C]
                ins = pool.affine_select(out=ap, in_=ap, compare_op=ALU.not_equal, fill=1.0, base=-i,
                                         pattern=[[-EB, OVB], [0, C]], channel_multiplier=1)
            ins.then_inc(s["pool_const"], 1)
        @block.scalar
        def _(act):
            step = Steps(act, "act_step")
            gains = [(gx[:, :], a["attn_norm_g"][0].rearrange("(p k) -> p k", k=KT)),
                     (gql[:, :], a["mla_q_lat_g"][0].rearrange("(p k) -> p k", k=2)),
                     (gkvl[:, :], a["mla_kv_lat_g"][0].rearrange("(p k) -> p k", k=1)),
                     (go[0:P // 2, :], a["out_norm_mla_g"][0].rearrange("(p k) -> p k", k=KT)),
                     (go[P // 2:P, :], a["out_norm_moba_g"][0].rearrange("(p k) -> p k", k=KT)),
                     (gf[:, :], a["ffn_norm_g"][0].rearrange("(p k) -> p k", k=KT)),
                     (g_row[:, 0:QK], a["mla_q_head_g"].to_broadcast([P, QK])),
                     (g_row[:, QK:2 * QK], a["mla_k_head_g"].to_broadcast([P, QK])),
                     (g_row[:, 2 * QK:2 * QK + DH], a["moba_q_head_g"].to_broadcast([P, DH])),
                     (g_row[:, 2 * QK + DH:], a["moba_k_head_g"].to_broadcast([P, DH])),
                     (b_row[:, 0:NG], a["b_router_group"].to_broadcast([P, NG])),
                     (b_row[:, NG:], a["b_router_expert"].to_broadcast([P, NE]))]
            for dst, src in gains:
                act.dma_start(dst, src).then_inc(s["gains_in"], 16)
            act.wait_ge(s["setup"], 1)
            for t in range(NT):
                act.wait_ge(x_in[t], 16)
                ins = act.activation(xn[:, t, :, :].rearrange("p k n -> p (k n)"), x_sb[:, t, :], ACT.Square,
                                     scale=D ** -0.5, accum_out=ms_x[:, t:t + 1])
                step(ins)
            act.activation(ms_x, ms_x, ACT.Sqrt, bias=eps[:, 0:1]).then_inc(s["x_rt"], 1)
            for t in range(NT):
                act.wait_ge(s["proj_done"], t + 1)
                act.copy(lat[:, t, :], B[4 + t][:, 0:C0]).then_inc(s["raw_ready"], 1)
                act.wait_ge(s["raw_ready"], t + 1)
                act.activation(sq[:, t, 0:QL], lat[:, t, 0:QL], ACT.Square, scale=QL ** -0.5, accum_out=ms_l[:, t, 0:1])
                act.activation(sq[:, t, QL:QL + KVL], lat[:, t, QL:QL + KVL], ACT.Square, scale=KVL ** -0.5, accum_out=ms_l[:, t, 1:2])
                step(act.activation(sq[:, t, QL + KVL:C0], lat[:, t, QL + KVL:C0], ACT.Square, scale=QK ** -0.5,
                                    accum_out=ms_pe[:, t:t + 1]))
            act.activation(st_l[:, 0:4], st_l[:, 0:4], ACT.Sqrt, bias=eps[:, 0:1]).then_inc(s["lat_rt"], 1)
            for t in range(NT):
                act.wait_ge(s["proj_done"], 3 + t)
                act.copy(mq[:, t, :], B[6 + t][:, :]).then_inc(s["raw_ready"], 1)

            def square(u):
                kind, t = UNITS[u]
                if u >= 2:
                    act.wait_ge(s["red_done"], u - 1)
                d = DH if kind[0] == "m" else QK
                x = {"mq": mq, "mk": mk, "qa": qa, "ka": kva}[kind][:, t, :].rearrange("p (h d) -> p h d", h=H)
                w = NOPE if kind == "ka" else d
                wait_raw(act, (kind, t))
                act.activation(sq[:, u % 2, 0:H * w].rearrange("p (h d) -> p h d", h=H), x[:, :, 0:w], ACT.Square,
                               scale=d ** -0.5).then_inc(s["sq_done"], 1)

            def root(u):
                act.wait_ge(s["red_done"], u + 1)
                act.activation(ms_h(u), ms_h(u), ACT.Sqrt, bias=eps[:, 0:1]).then_inc(s["rt_done"], 1)

            square(0)
            for t in range(NT):
                act.wait_ge(s["proj_done"], 5 + t)
                act.copy(mk[:, t, :], B[t][:, :]).then_inc(s["raw_ready"], 1)
            square(1)
            root(0)
            square(2)
            root(1)
            square(3)
            root(2)
            root(3)
            lifted = [(qa, 4), (qa, 5), (kva, 2), (kva, 3), (qa, 6), (qa, 7), (kva, 0), (kva, 1)]
            for n, (dst, bank) in enumerate(lifted):
                act.wait_ge(s["lift_done"], n + 1)
                t, hf = n // 4, n % 2
                w = H * QK // 2 if dst is qa else 512
                act.copy(dst[:, t, hf * w:hf * w + w], B[bank][:, 0:w]).then_inc(s["raw2_ready"], 1)
                if n == 3:
                    square(4)
                    square(5)
                    root(4)
                    root(5)
            square(6)
            square(7)
            root(6)
            root(7)
            for t in range(NT):
                act.wait_ge(s["proj_done"], 7 + t)
                act.copy(mv[:, t, :], B[4 + t][:, :]).then_inc(s["mv_ready"], 1)
            for n, (dst, bank, w) in enumerate(head_banks()):
                act.wait_ge(s["headT_done"], n + 1)
                act.copy(dst, B[bank][0:w, :].rearrange("p (h s) -> p h s", h=4)).then_inc(s["headT_ready"], 1)
            for dst, src in ((w_r[:, :, 0:NG], a["w_router_group"]), (w_r[:, :, NG:], a["w_router_expert"])):
                act.dma_start(dst, src[0].rearrange("(p k) n -> p k n", k=KT)).then_inc(s["wr_in"], 16)
            for i in range(2 * H + 2):
                if i < 2 * H:
                    scale = (DH if i < H else QK) ** -0.5
                    act.wait_ge(s["max_ready"], i + 1)
                    if i >= 3:
                        act.wait_ge(s["pT_done"], i - 2)
                    for t in range(NT):
                        ins = act.activation(p_sb[:, i % 3, t * P:(2 * t + 1) * P], s_sb[:, i % 3, t * P:(2 * t + 1) * P],
                                             ACT.Exp, bias=nmx[:, i, t:t + 1], scale=scale, accum_out=rsum[:, t, i:i + 1])
                    ins.then_inc(s["exp_done"], 1)
                if i >= 2 and i % 2:
                    head_pT(act, i - 2)
            for n, (t, g) in enumerate(((0, 1), (1, 1), (0, 0), (1, 0))):
                act.wait_ge(s["o_ready"], n + 1)
                ins = act.activation(xn[:, t, 4 * g:4 * g + 4, :].rearrange("p k n -> p (k n)"), o_sb[:, t, 512 * g:512 * g + 512],
                                     ACT.Square, scale=512 ** -0.5, accum_out=ms_o[:, t, g:g + 1])
            step(ins)
            act.activation(st_o[:, 0:4], st_o[:, 0:4], ACT.Sqrt, bias=eps[:, 0:1]).then_inc(s["o_rt"], 1)
            for t in range(NT):
                act.wait_ge(s["x1_ready"], 2 * t + 2)
                ins = act.activation(o_sb[:, t, :], x_sb[:, t, :], ACT.Square, scale=D ** -0.5, accum_out=ms_f[:, t:t + 1])
            step(ins)
            act.activation(ms_f, ms_f, ACT.Sqrt, bias=eps[:, 0:1]).then_inc(s["x1_rt"], 1)
            act.wait_ge(s["r_max"], 1)
            act.activation(rt[:, 32:40], rt[:, 24:32], ACT.Exp).then_inc(s["r_exp"], 1)
            act.wait_ge(s["r_max"], 2)
            act.activation(rt[:, 212:214], rt[:, 210:212], ACT.Exp).then_inc(s["r_exp"], 1)
            act.wait_ge(s["keybc_done"], 1)
            act.copy(key_bc[:, 0:2, :, :].rearrange("p a t n -> p (a t n)"), B[4][:, :])
            act.wait_ge(s["keybc_done"], 2)
            act.copy(key_bc[:, 2:4, :, :].rearrange("p a t n -> p (a t n)"), B[5][:, :]).then_inc(s["keybc_ready"], 1)

            def batch(b, first):
                for i in range(EB):
                    act.wait_ge(s["up_done"], EB * b + i + 1)
                    if not (first and i == 0):
                        act.wait_ge(s["fold_done"], EB * b + i)
                    act.copy(u_sb, B[5][:, :]).then_inc(s["u_ready"], 1)
                    act.wait_ge(s["fold_done"], EB * b + i + 1)
                    if not (first and i == 0):
                        act.wait_ge(s["g_ready"], EB * b + i)
                    act.activation(sil, B[6][:, 0:2 * C], ACT.Silu).then_inc(s["sil_ready"], 1)
                    act.wait_ge(s["down_done"], EB * b + i + 1)
                    if i == 0 and not first:
                        act.wait_ge(s["scat_done"], b)
                    for q in (2, 3):
                        ins = act.copy(y_sb[C * i:C * i + C, 256 * q:256 * q + 256], B[7][C * q:C * q + C, 0:256])
                    ins.then_inc(s["y_act"], 1)

            batch(0, True)
            with act.Fori(1, NB) as b:
                batch(b, False)
            act.wait_ge(s["nb_ready"], 1)
            n_ov = act.value_load(nb_i[0:1, 0:1], min_val=0, max_val=OVB)
            with act.If(n_ov > 0):
                with act.Fori(0, n_ov) as v:
                    batch(v + NB, False)

        @block.tensor
        def _(pe_):
            def transposes(src, ready, done):
                for t in range(NT):
                    pe_.wait_ge(s[ready], t + 1)
                    for hf in range(2):
                        for k in range(4):
                            ins = pe_.transpose(B[2 * t + hf][:, k * P:(k + 1) * P], src[:, t, 4 * hf + k, :], ident)
                        ins.then_inc(s[done], 1)

            pe_.wait_ge(s["const_in"], 16)
            transposes(xn, "xn_ready", "xT_done")
            pe_.wait_ge(s["actT_ready"], 4)
            col = [0, C0, C0 + 512, C0 + 1024, IN_W]
            for k in range(KT):
                pe_.wait_ge(win_in[k], 16)
                for c in range(2):
                    for t in range(NT):
                        ins = pe_.matmul(B[4 + 2 * c + t][:, 0:col[c + 1] - col[c]], actT[:, k, t * P:(t + 1) * P],
                                         w_in[:, k, col[c]:col[c + 1]], start=(k == 0), stop=(k == KT - 1))
                        if k == KT - 1:
                            ins.then_inc(s["proj_done"], 1)

            def project(c, banks):
                for t in range(NT):
                    for k in range(KT):
                        ins = pe_.matmul(B[banks[t]][:, :], actT[:, k, t * P:(t + 1) * P],
                                         w_in[:, k, col[c]:col[c + 1]], start=(k == 0), stop=(k == KT - 1))
                    ins.then_inc(s["proj_done"], 1)

            project(2, (0, 1))
            pe_.wait_ge(s["latn_ready"], 1)
            for k in range(2):
                for t in range(NT):
                    ins = pe_.transpose(B[2][:, k * S + t * P:k * S + (t + 1) * P], latn[:, t, k, :], ident)
            ins.then_inc(s["latT_done"], 1)
            for t in range(NT):
                ins = pe_.transpose(B[3][:, t * P:(t + 1) * P], latn[:, t, 2, :], ident)
            ins.then_inc(s["latT_done"], 1)
            pe_.wait_ge(s["latT_ready"], 2)
            pe_.wait_ge(s["wup_in"], 32)
            for t in range(NT):
                pe_.wait_ge(s["raw_ready"], (2, 4)[t])
                for hf in range(2):
                    for k in range(2):
                        ins = pe_.matmul(B[4 + 2 * t + hf][:, 0:384], latT[:, k, t * P:(t + 1) * P],
                                         w_qup[:, k, 384 * hf:384 * hf + 384], start=(k == 0), stop=(k == 1))
                    ins.then_inc(s["lift_done"], 1)
                if t:
                    pe_.wait_ge(s["raw_ready"], 6)
                for hf in range(2):
                    pe_.matmul(B[(2, 0)[t] + hf][:, :], latT[:, 2, t * P:(t + 1) * P], w_kvup[:, 512 * hf:512 * hf + 512],
                               start=True, stop=True).then_inc(s["lift_done"], 1)
            pe_.wait_ge(s["raw2_ready"], 2)
            project(3, (4, 5))
            heads = head_banks()
            n = 0
            for u, (kind, t) in enumerate(UNITS):
                pe_.wait_ge(s["heads_ready"], u + 1)
                if u == 0:
                    pe_.wait_ge(s["raw2_ready"], 8)
                if u == 5:
                    pe_.wait_ge(s["mv_ready"], 2)
                if u == 6:
                    pe_.wait_ge(s["headT_ready"], 4)
                if kind[0] == "m":
                    src = (mq if kind == "mq" else mk)[:, t, :].rearrange("p (h d) -> p h d", d=P)
                else:
                    src = (qa if kind == "qa" else ka)[:, t, :].rearrange("p (h d) -> p h d", d=QK)
                for j in range(src.shape[1]):
                    _, bank, w = heads[n]
                    ins = pe_.transpose(B[bank][0:w, (j % 4) * P:(j % 4 + 1) * P], src[:, j, :], ident)
                    if j % 4 == 3:
                        ins.then_inc(s["headT_done"], 1)
                        n += 1
            pe_.wait_ge(s["headT_ready"], len(heads))

            def scores(h):
                if h >= 2:
                    pe_.wait_ge(s["max_ready"], h - 1)
                if h < H:
                    p0 = 64 * (h % 2)
                    q, k = mqT[p0:p0 + DH, h // 2, :], mkT[p0:p0 + DH, h // 2, :]
                else:
                    q, k = qaT[0:QK, h - H, :], kaT[0:QK, h - H, :]
                for t in range(NT):
                    ins = pe_.matmul(B[h % 2][:, t * P:(2 * t + 1) * P], q[:, t * P:(t + 1) * P], k[:, 0:(t + 1) * P], start=True, stop=True)
                ins.then_inc(s["score_done"], 1)

            def turn(h):
                pe_.wait_ge(s["exp_done"], h + 1)
                if h >= 2:
                    pe_.wait_ge(s[("pT_even", "pT_odd")[h % 2]], h // 2)
                for j in range(3):
                    ins = pe_.transpose(B[2 + h % 2][:, j * P:(j + 1) * P], p_sb[:, h % 3, j * P:(j + 1) * P], ident)
                ins.then_inc(s["pT_done"], 1)

            def values(h):
                pe_.wait_ge(s[("pT_even", "pT_odd")[h % 2]], h // 2 + 1)
                g, hh = h // H, h % H
                v = [mv[:, t, DH * hh:DH * hh + DH] if g == 0 else kva[:, t, P * hh + NOPE:P * hh + P] for t in range(NT)]
                o = [B[4 + 2 * g + t][:, DH * hh:DH * hh + DH] for t in range(NT)]
                pe_.matmul(o[0], pT_sb[:, h % 2, 0:P], v[0], start=True, stop=True)
                pe_.matmul(o[1], pT_sb[:, h % 2, P:2 * P], v[0], start=True, stop=False)
                pe_.matmul(o[1], pT_sb[:, h % 2, 2 * P:3 * P], v[1], start=False, stop=True).then_inc(s["pv_done"], 1)

            for i in range(2 * H + 3):
                if i < 2 * H:
                    scores(i)
                if 2 <= i < 2 * H + 2:
                    turn(i - 2)
                if i >= 3:
                    values(i - 3)
            transposes(xn, "on_ready", "oT_done")
            pe_.wait_ge(s["wout_in"], 16)
            for t in range(NT):
                pe_.wait_ge(s["mixT_ready"], 2 * t + 2)
                for hf in range(2):
                    for k in range(KT):
                        ins = pe_.matmul(B[4 + 2 * t + hf][:, :], actT[:, k, t * P:(t + 1) * P],
                                         w_out[:, k, 512 * hf:512 * hf + 512], start=(k == 0), stop=(k == KT - 1))
                    ins.then_inc(s["outp_done"], 1)
            transposes(xn, "hn_ready", "hT_done")
            pe_.wait_ge(s["wr_in"], 32)
            pe_.wait_ge(s["x1_ready"], 4)
            for t in range(NT):
                pe_.wait_ge(s["h2T_ready"], 2 * t + 2)
                for k in range(KT):
                    ins = pe_.matmul(B[4 + t][:, 0:NG + NE], actT[:, k, t * P:(t + 1) * P], w_r[:, k, :], start=(k == 0), stop=(k == KT - 1))
                ins.then_inc(s["logit_done"], 1)
            pe_.wait_ge(s["rank_in"], 1)
            tri = const[:, CR:CR + P]
            pe_.matmul(B[6][:, 0:NE], tri, m01[:, 0, :], start=True, stop=True)
            pe_.matmul(B[6][:, NE:2 * NE], ones[:, :], m01[:, 0, :], start=True, stop=False)
            pe_.matmul(B[6][:, NE:2 * NE], tri, m01[:, 1, :], start=False, stop=True)
            pe_.matmul(B[6][:, 2 * NE:3 * NE], ones[:, :], m01[:, 0, :], start=True, stop=False)
            pe_.matmul(B[6][:, 2 * NE:3 * NE], ones[:, :], m01[:, 1, :], start=False, stop=True).then_inc(s["rank_done"], 1)

            acc = [[B[2 * t + hf] for hf in range(2)] for t in range(NT)]

            def gather(part):
                for k in range(4):
                    for t in range(NT):
                        ins = pe_.matmul(B[4 + part][:, k * P:(k + 1) * P], xn[:, t, 4 * part + k, :], hot[:, t, :],
                                         start=(t == 0), stop=(t == NT - 1))
                ins.then_inc(s["gath_done"], 1)

            pe_.wait_ge(s["hot_ready"], 1)
            pe_.wait_ge(s["logit_done"], 2)
            gather(0)
            gather(1)
            pe_.wait_ge(s["xg_ready"], 2)
            pe_.wait_ge(s["key_ready"], 1)
            for n in range(2):
                for m in range(2):
                    for t in range(NT):
                        ins = pe_.matmul(B[4 + n][:, (2 * m + t) * P:(2 * m + t + 1) * P],
                                         key_w[:, 2 * n + m, t:t + 1].to_broadcast([P, P]), ident, start=True, stop=True)
                ins.then_inc(s["keybc_done"], 1)
            pe_.wait_ge(s["setup"], 2)
            for t in range(NT):
                for hf in range(2):
                    pe_.matmul(acc[t][hf][:, :], zeros[:, 0:P], zeros, start=True, stop=False, skip_group_check=True)
            pe_.wait_ge(s["keybc_ready"], 1)

            def batch(b, first, ahead):
                if not ahead:
                    pe_.wait_ge(s["hot_ready"], b + 2)
                    gather(0)
                    gather(1)
                for i in range(EB):
                    n = EB * b + i
                    pe_.wait_ge(gu_in[i], 32 * b + 32)
                    if i == 0:
                        pe_.wait_ge(s["xg_ready"], 2 * b + 2 if ahead else 2 * b + 4)
                    else:
                        pe_.wait_ge(s["u_ready"], n)
                    for k in range(KT):
                        j = k % EB
                        ins = pe_.matmul(B[5][C * j:C * j + C, :].rearrange("p (g n) -> p g n", g=2), xg[:, k, C * i:C * i + C],
                                         gate_up[i][:, k, :, :], start=(k < EB), stop=(k >= EB), skip_group_check=True)
                    ins.then_inc(s["up_done"], 1)
                    if i == EB - 1 and ahead:
                        pe_.wait_ge(s["hot_ready"], b + 2)
                        gather(0)
                        pe_.wait_ge(s["u_ready"], n + 1)
                        gather(1)
                    pe_.wait_ge(s["u_ready"], n + 1)
                    if not (first and i == 0):
                        pe_.wait_ge(s["g_ready"], n)
                    for c in range(4):
                        ins = pe_.matmul(B[6][:, C * c:C * c + C], u_sb[:, P * c:P * c + P], const[:, CS:CS + C], start=True, stop=True)
                    ins.then_inc(s["fold_done"], 1)
                    pe_.wait_ge(s["g_ready"], n + 1)
                    pe_.wait_ge(dn_in[i], 16 * b + 16)
                    if not (first and i == 0):
                        pe_.wait_ge(s["y_dve"], n)
                        pe_.wait_ge(s["y_act"], n)
                    for j in range(2):
                        for q in range(4):
                            ins = pe_.matmul(B[7][C * q:C * q + C, 0:256], gT[:, j, :], down_w[i][:, j, 256 * q:256 * q + 256],
                                             start=(j == 0), stop=(j == 1), skip_group_check=True)
                    ins.then_inc(s["down_done"], 1)
                pe_.wait_ge(s["y_dve"], EB * b + EB)
                pe_.wait_ge(s["y_act"], EB * b + EB)
                pe_.wait_ge(s["back_ready"], b + 1)
                for t in range(NT):
                    for hf in range(2):
                        ins = pe_.matmul(acc[t][hf][:, :], back[:, t * P:(t + 1) * P], y_sb[:, 512 * hf:512 * hf + 512],
                                         start=False, stop=False, skip_group_check=True)
                ins.then_inc(s["scat_done"], 1)

            batch(0, True, True)
            with pe_.Fori(1, NB) as b:
                batch(b, False, True)
            pe_.wait_ge(s["nb_ready"], 1)
            n_ov = pe_.value_load(nb_i[0:1, 0:1], min_val=0, max_val=OVB)
            with pe_.If(n_ov > 0):
                pe_.wait_ge(s["ovk_ready"], 1)
                pe_.wait_ge(s["xg_ready"], 2 * NB + 2)
                pe_.matmul(B[4][:, :], ov[:, 0:P], ov_pick[:, :, :].rearrange("p b n -> p (b n)"), start=True, stop=True)
                for b in range(OVB):
                    pe_.matmul(B[6][:, b:b + 1], ov_pick[:, b, :], ov[:, P:P + 1], start=True, stop=True)
                pe_.matmul(B[6][:, P:P + EB * OVB], ov[:, 2 * P:3 * P], const[:, CI:CI + EB * OVB], start=True, stop=True).then_inc(s["ovt_done"], 1)
                with pe_.Fori(0, n_ov) as v:
                    batch(v + NB, False, False)

        @block.vector
        def _(dve):
            step = Steps(dve, "dve_step")
            dve.memset(eps[:, :], EPS)
            dve.memset(ones[:, :], 1.0).then_inc(s["setup"], 1)

            def turned(gain, done, ready):
                for n in range(4):
                    dve.wait_ge(s[done], n + 1)
                    t, hf = n // 2, n % 2
                    dve.tensor_tensor(actT[:, 4 * hf:4 * hf + 4, t * P:(t + 1) * P], B[n][:, :].rearrange("p (k n) -> p k n", k=4),
                                      gain[:, 4 * hf:4 * hf + 4].unsqueeze(2).to_broadcast([P, 4, P]), ALU.mult).then_inc(s[ready], 1)

            def permuted(x):
                return x.rearrange("p (n k) -> p k n", k=KT)

            dve.wait_ge(s["x_rt"], 1)
            step(dve.reciprocal(r_x, ms_x))
            for t in range(NT):
                dve.tensor_scalar(xn[:, t, :, :], permuted(x_sb[:, t, :]), r_x[:, t:t + 1], None, ALU.mult).then_inc(s["xn_ready"], 1)
            dve.wait_ge(s["gains_in"], 16 * 12)
            turned(gx, "xT_done", "actT_ready")
            dve.wait_ge(s["lat_rt"], 1)
            step(dve.reciprocal(st_l[:, 4:8], st_l[:, 0:4]))
            for t in range(NT):
                dve.tensor_scalar(latn[:, t, 0:2, :], lat[:, t, 0:QL].rearrange("p (n k) -> p k n", k=2), r_l[:, t, 0:1], None, ALU.mult)
                ins = dve.tensor_scalar(latn[:, t, 2, :], lat[:, t, QL:QL + KVL], r_l[:, t, 1:2], None, ALU.mult)
            ins.then_inc(s["latn_ready"], 1)

            def head_norm(u):
                kind, t = UNITS[u]
                d = DH if kind[0] == "m" else QK
                w = NOPE if kind == "ka" else d
                dve.wait_ge(s["sq_done"], u + 1)
                ins = dve.tensor_reduce(ms_h(u), sq[:, u % 2, 0:H * w].rearrange("p (h d) -> p h d", h=H), AX.X, ALU.add)
                if kind == "ka":
                    step(ins)
                    ins = dve.tensor_scalar(ms_h(u), ms_h(u), ms_pe[:, t:t + 1], None, ALU.add)
                ins.then_inc(s["red_done"], 1)

            def head_scale(u):
                kind, t = UNITS[u]
                dve.wait_ge(s["rt_done"], u + 1)
                dve.wait_ge(s["swap_done"], u + 1)
                if kind[0] == "m":
                    x = (mq if kind == "mq" else mk)[:, t, :].rearrange("p (h d) -> p h d", h=H)
                    dve.tensor_tensor(x, x, swp[:, u % 2, :].rearrange("p (h d) -> p h d", h=H), ALU.add)
                    d = DH
                elif kind == "qa":
                    x = qa[:, t, :].rearrange("p (h d) -> p h d", h=H)
                    dve.tensor_tensor(x[:, :, NOPE:QK], x[:, :, NOPE:QK],
                                      swp[:, u % 2, 0:H * RD].rearrange("p (h d) -> p h d", h=H), ALU.add)
                    d = QK
                else:
                    x = ka[:, t, :].rearrange("p (h d) -> p h d", h=H)
                    dve.tensor_copy(x[:, :, NOPE:QK], pe[:, t, 0, :].unsqueeze(1).to_broadcast([P, H, RD]))
                    d = QK
                step(dve.reciprocal(r_h(u), ms_h(u)))
                dve.tensor_tensor(x, x, r_h(u).unsqueeze(2).to_broadcast([P, H, d]), ALU.mult).then_inc(s["heads_ready"], 1)

            head_norm(0)
            for n, (lo, gain) in enumerate(((0, gql), (2, gkvl))):
                dve.wait_ge(s["latT_done"], n + 1)
                m = 2 - n
                dve.tensor_tensor(latT[:, lo:lo + m, :], B[2 + n][:, 0:m * S].rearrange("p (k n) -> p k n", k=m),
                                  gain[:, :].unsqueeze(2).to_broadcast([P, m, S]), ALU.mult).then_inc(s["latT_ready"], 1)
            head_norm(1)
            for u in range(len(UNITS)):
                head_scale(u)
                if u + 2 < len(UNITS):
                    head_norm(u + 2)

            def mask_max(h):
                scale = (DH if h < H else QK) ** -0.5
                dve.wait_ge(s["score_done"], h + 1)
                if h >= 3:
                    dve.wait_ge(s["exp_done"], h - 2)
                tri = const[:, CM:CM + P]
                sc, dst = B[h % 2], s_sb[:, h % 3, :]
                dve.tensor_tensor_reduce(dst[:, 0:P], sc[:, 0:P], tri, 1.0, NEG, ALU.add, ALU.max, mx[:, h, 0:1])
                step(dve.tensor_tensor_reduce(dst[:, P:3 * P], sc[:, P:3 * P], wide_mask(), 1.0, NEG, ALU.add, ALU.max, mx[:, h, 1:2]))
                dve.tensor_scalar(nmx[:, h, :], mx[:, h, :], -scale, None, ALU.mult).then_inc(s["max_ready"], 1)

            def wide_mask():
                return rt[:, 768:1024]

            def outputs(g):
                dve.wait_ge(s["pv_done"], H * g + H)
                step(dve.reciprocal(rsum[:, :, H * g:H * g + H], rsum[:, :, H * g:H * g + H]))
                for t in range(NT):
                    dve.tensor_tensor(o_sb[:, t, 512 * (1 - g):512 * (1 - g) + 512].rearrange("p (h d) -> p h d", h=H),
                                      B[4 + 2 * g + t][:, :].rearrange("p (h d) -> p h d", h=H),
                                      rsum[:, t, H * g:H * g + H].unsqueeze(2).to_broadcast([P, H, DH]), ALU.mult).then_inc(s["o_ready"], 1)

            dve.wait_ge(s["headT_done"], 4)
            dve.memset(wide_mask()[:, 0:P], 0.0)
            step(dve.tensor_copy(wide_mask()[:, P:2 * P], const[:, CM:CM + P]))
            for i in range(2 * H + 2):
                if i < 2 * H:
                    mask_max(i)
                if i >= 2 and i % 2 == 0:
                    head_pT(dve, i - 2)
                if i == H + 4:
                    outputs(0)
            outputs(1)
            dve.wait_ge(s["o_rt"], 1)
            step(dve.reciprocal(st_o[:, 4:8], st_o[:, 0:4]))
            for t in range(NT):
                for g in range(2):
                    ins = dve.tensor_scalar(xn[:, t, :, 64 * g:64 * g + 64], permuted(o_sb[:, t, 512 * g:512 * g + 512]),
                                            r_o[:, t, g:g + 1], None, ALU.mult)
                ins.then_inc(s["on_ready"], 1)
            turned(go, "oT_done", "mixT_ready")
            for t in range(NT):
                for hf in range(2):
                    dve.wait_ge(s["outp_done"], 2 * t + hf + 1)
                    x = x_sb[:, t, 512 * hf:512 * hf + 512]
                    dve.tensor_tensor(x, x, B[4 + 2 * t + hf][:, :], ALU.add).then_inc(s["x1_ready"], 1)
            dve.wait_ge(s["x1_rt"], 1)
            step(dve.reciprocal(r_f, ms_f))
            for t in range(NT):
                dve.tensor_scalar(xn[:, t, :, :], permuted(x_sb[:, t, :]), r_f[:, t:t + 1], None, ALU.mult).then_inc(s["hn_ready"], 1)
            turned(gf, "hT_done", "h2T_ready")

            dve.memset(zeros, 0.0).then_inc(s["setup"], 1)

            dve.wait_ge(s["pool_const"], 1)
            for t in range(NT):
                dve.wait_ge(s["logit_done"], t + 1)
                ins = dve.tensor_tensor(lg[:, t, :], B[4 + t][:, 0:NG + NE], b_row[:, :], ALU.add)
            step(ins)

            def first_of(dst, x, n, tmp, top):
                step(dve.tensor_tensor(tmp, x, top.to_broadcast([P, NT, n]), ALU.is_equal))
                step(dve.tensor_tensor(tmp, tmp, tie[:, 0:n].unsqueeze(1).to_broadcast([P, NT, n]), ALU.mult))
                step(dve.tensor_reduce(best, tmp, AX.X, ALU.max))
                step(dve.tensor_tensor(dst, tmp, best.to_broadcast([P, NT, n]), ALU.is_equal))

            def view(lo, n):
                return rt[:, lo:lo + NT * n].rearrange("p (t n) -> p t n", t=NT)

            gl = lg[:, :, 0:NG]
            gmax, tmp4, best, ghot = view(0, 1), view(4, NG), view(2, 1), view(16, NG)
            shifted, gexp, gsum = view(24, NG), view(32, NG), view(40, 1)
            step(dve.tensor_reduce(gmax, gl, AX.X, ALU.max))
            step(dve.tensor_tensor(shifted, gl, gmax.to_broadcast([P, NT, NG]), ALU.subtract))
            dve.tensor_copy(rt[:, 42:43], rt[:, 0:1]).then_inc(s["r_max"], 1)
            first_of(ghot, gl, NG, tmp4, gmax)
            prod = rt[:, 256:256 + NT * NE].rearrange("p (t g e) -> p t g e", t=NT, g=NG)
            for t in range(NT):
                ins = dve.tensor_tensor(prod[:, t], lg[:, t, NG:].rearrange("p (g e) -> p g e", g=NG),
                                        ghot[:, t, :].unsqueeze(2).to_broadcast([P, NG, EPG]), ALU.mult)
            step(ins)
            el, e2, tmp8 = view(64, EPG), view(80, EPG), view(96, EPG)
            v1, v2, h1, h2 = view(44, 1), view(46, 1), view(112, EPG), view(128, EPG)
            for t in range(NT):
                ins = dve.tensor_reduce(el[:, t, :], prod[:, t].rearrange("p g e -> p e g"), AX.X, ALU.add)
            step(ins)
            step(dve.tensor_reduce(v1, el, AX.X, ALU.max))
            first_of(h1, el, EPG, tmp8, v1)
            for t in range(NT):
                ins = dve.scalar_tensor_tensor(out=e2[:, t, :], in0=h1[:, t, :], scalar=NEG, in1=el[:, t, :], op0=ALU.mult, op1=ALU.add)
            step(ins)
            step(dve.tensor_reduce(v2, e2, AX.X, ALU.max))
            first_of(h2, e2, EPG, tmp8, v2)
            step(dve.tensor_tensor(rt[:, 210:212], rt[:, 46:48], rt[:, 44:46], ALU.subtract))
            dve.tensor_copy(rt[:, 43:44], rt[:, 210:211]).then_inc(s["r_max"], 1)
            hot1 = rt[:, 320:320 + NT * NE].rearrange("p (t g e) -> p t g e", t=NT, g=NG)
            hot2 = rt[:, 384:384 + NT * NE].rearrange("p (t g e) -> p t g e", t=NT, g=NG)
            for dst, src in ((hot1, h1), (hot2, h2)):
                for t in range(NT):
                    ins = dve.tensor_tensor(dst[:, t], ghot[:, t, :].unsqueeze(2).to_broadcast([P, NG, EPG]),
                                            src[:, t, :].unsqueeze(1).to_broadcast([P, NG, EPG]), ALU.mult)
            step(ins)
            dve.tensor_tensor(m01[:, :, :].rearrange("p t e -> p (t e)"), rt[:, 320:384], rt[:, 384:448], ALU.add).then_inc(s["rank_in"], 1)
            dve.wait_ge(s["r_exp"], 2)
            step(dve.tensor_reduce(gsum, gexp, AX.X, ALU.add))
            step(dve.tensor_scalar(rt[:, 214:216], rt[:, 212:214], 1.0, None, ALU.add))
            step(dve.tensor_tensor(rt[:, 216:218], rt[:, 214:216], rt[:, 40:42], ALU.mult))
            step(dve.reciprocal(key_w[:, 2, :], rt[:, 216:218]))
            step(dve.tensor_tensor(key_w[:, 3, :], key_w[:, 2, :], rt[:, 212:214], ALU.mult))
            dve.wait_ge(s["rank_done"], 1)
            dve.tensor_copy(totals, B[6][:, 2 * NE:3 * NE])
            keys = rt[:, 448:448 + NT * NE].rearrange("p (t e) -> p t e", t=NT)
            step(dve.tensor_tensor(keys, B[6][:, 0:NT * NE].rearrange("p (t e) -> p t e", t=NT),
                                   e_key[:, :].unsqueeze(1).to_broadcast([P, NT, NE]), ALU.add))
            picked = rt[:, 512:512 + 2 * NT * NE].rearrange("p (a t e) -> p a t e", a=2, t=NT)
            for n, hot_n in enumerate((rt[:, 320:384], rt[:, 384:448])):
                ins = dve.tensor_tensor(picked[:, n].rearrange("p t e -> p (t e)"), hot_n, rt[:, 448:512], ALU.mult)
            step(ins)
            for n in range(2):
                ins = dve.tensor_reduce(key_w[:, n, :].unsqueeze(2), picked[:, n], AX.X, ALU.add)
            ins.then_inc(s["key_ready"], 1)
            dve.wait_ge(s["key_ready"], 1)

            def one_hot(b):
                row = slot_row[:, bass.ds(b, 1), :].rearrange("p b n -> p (b n)")
                for t in range(NT):
                    dve.tensor_scalar(hot[:, t, :], row, key_w[:, 0, t:t + 1], None, ALU.is_equal)
                return row

            def one_hot_add(row, count):
                for t in range(NT):
                    ins = dve.scalar_tensor_tensor(out=hot[:, t, :], in0=row, scalar=key_w[:, 1, t:t + 1], in1=hot[:, t, :],
                                                   op0=ALU.is_equal, op1=ALU.add)
                ins.then_inc(s["hot_ready"], 1)

            row = one_hot(0)
            step(dve.tensor_copy(rt[:, 43:44], rt[:, 210:211]))
            one_hot_add(row, 0)

            def gathered_out(part, value):
                dve.wait_ge(s["gath_done"], value)
                dve.tensor_tensor(xg[:, 4 * part:4 * part + 4, :], B[4 + part][:, :].rearrange("p (k n) -> p k n", k=4),
                                  gf[:, 4 * part:4 * part + 4].unsqueeze(2).to_broadcast([P, 4, P]), ALU.mult).then_inc(s["xg_ready"], 1)

            gathered_out(0, 1)
            gathered_out(1, 2)
            there, place, scratch = [ov[:, 3 * P + n * W:3 * P + (n + 1) * W] for n in range(3)]
            small = rt[:, 220:240]
            step(dve.tensor_tensor(there.rearrange("p (e c) -> p e c", c=OVC), totals.unsqueeze(2).to_broadcast([P, NE, OVC]),
                                   ov_thr[:, :, :], ALU.is_gt))
            step(dve.memset(scratch, 1.0))
            step(dve.tensor_tensor_scan(place, scratch, there, 0.0, ALU.mult, ALU.add))
            step(dve.tensor_scalar(small[:, 0:OVB], ov4[:, :], place[:, W - 1:W], None, ALU.is_lt))
            step(dve.tensor_reduce(small[:, 4:5], small[:, 0:OVB], AX.X, ALU.add))
            dve.tensor_copy(nb_i[:, :], small[:, 4:5]).then_inc(s["nb_ready"], 1)
            for n, table in enumerate((ov_key, ov_exp)):
                step(dve.tensor_tensor(scratch, there, table[:, :, :].rearrange("p e c -> p (e c)"), ALU.mult))
                step(dve.scalar_tensor_tensor(out=scratch, in0=place, scalar=ov_j[:, 0:1], in1=scratch, op0=ALU.is_equal,
                                              op1=ALU.mult, accum_out=small[:, 6 + n:7 + n]))
            step(dve.tensor_scalar(small[:, 6:7], small[:, 6:7], -OFF, None, ALU.add))

            def batch(b, first, ahead):
                if ahead:
                    dve.wait_ge(s["gath_done"], 2 * b + 2)
                    row = one_hot(b + 1)
                else:
                    dve.wait_ge(s["gath_done"], 2 * b + 2)
                    row = one_hot(b)
                if not first:
                    dve.wait_ge(s["scat_done"], b)
                for m in range(2):
                    ins = dve.tensor_scalar(back2[:, m, :], key_bc[:, m, :, :].rearrange("p t n -> p (t n)"),
                                            slot_col[:, bass.ds(b, 1)], None, ALU.is_equal)
                ins.then_inc(s["hot_half"], 1)
                dve.wait_ge(s["hot_half"], b + 1)
                one_hot_add(row, b)
                for m in range(2):
                    ins = dve.tensor_tensor(back2[:, m, :], back2[:, m, :], key_bc[:, 2 + m, :, :].rearrange("p t n -> p (t n)"), ALU.mult)
                ins.then_inc(s["back_half"], 1)
                dve.wait_ge(s["back_half"], b + 1)
                dve.tensor_tensor(back, back2[:, 0, :], back2[:, 1, :], ALU.add).then_inc(s["back_ready"], 1)
                if not ahead:
                    gathered_out(0, 2 * b + 3)
                    gathered_out(1, 2 * b + 4)
                for i in range(EB):
                    n = EB * b + i
                    if i == EB - 1 and ahead:
                        gathered_out(0, 2 * b + 3)
                        gathered_out(1, 2 * b + 4)
                    dve.wait_ge(s["sil_ready"], n + 1)
                    if not (first and i == 0):
                        dve.wait_ge(s["down_done"], n)
                    dve.tensor_tensor(gT, sil.rearrange("p (j n) -> p j n", j=2), B[6][:, 2 * C:4 * C].rearrange("p (j n) -> p j n", j=2),
                                      ALU.mult).then_inc(s["g_ready"], 1)
                    dve.wait_ge(s["down_done"], n + 1)
                    if i == 0 and not first:
                        dve.wait_ge(s["scat_done"], b)
                    for q in (0, 1):
                        ins = dve.tensor_copy(y_sb[C * i:C * i + C, 256 * q:256 * q + 256], B[7][C * q:C * q + C, 0:256])
                    ins.then_inc(s["y_dve"], 1)

            dve.wait_ge(s["keybc_ready"], 1)
            batch(0, True, True)
            with dve.Fori(1, NB) as b:
                batch(b, False, True)
            n_ov = dve.value_load(nb_i[0:1, 0:1], min_val=0, max_val=OVB)
            with dve.If(n_ov > 0):
                dve.tensor_scalar(ov[:, 0:P], ones[:, :], small[:, 6:7], None, ALU.mult)
                dve.tensor_scalar(ov[:, 2 * P:3 * P], ones[:, :], small[:, 7:8], None, ALU.mult)
                dve.tensor_copy(ov[:, P:P + 1], small[:, 6:7]).then_inc(s["ovk_ready"], 1)
                dve.wait_ge(s["ovt_done"], 1)
                for b in range(OVB):
                    dve.tensor_tensor(slot_row[:, NB + b, :].rearrange("p (i c) -> p i c", i=EB),
                                      B[4][:, b * P:(b + 1) * P].rearrange("p (i c) -> p i c", i=EB),
                                      slot_row[:, 0, 0:C].unsqueeze(1).to_broadcast([P, EB, C]), ALU.add)
                for i in range(EB):
                    dve.tensor_scalar(slot_col[C * i:C * i + C, NB:], B[6][C * i:C * i + C, 0:OVB],
                                      slot_col[C * i:C * i + C, 0:1], float(-i * KEY), ALU.add, ALU.add)
                dve.tensor_copy(eid_i[:, :], B[6][:, P:P + EB * OVB]).then_inc(s["ov_ready"], 1)
                dve.wait_ge(s["ov_ready"], 1)
                with dve.Fori(0, n_ov) as v:
                    batch(v + NB, False, False)
            dve.wait_ge(s["scat_done"], NB)
            for t in range(NT):
                for hf in range(2):
                    dve.tensor_tensor(o_sb[:, t, 512 * hf:512 * hf + 512], x_sb[:, t, 512 * hf:512 * hf + 512],
                                      B[2 * t + hf][:, :], ALU.add).then_inc(s["y_out"], 1)


_SHAPES = "x attn_norm_g w_in mla_q_lat_g w_q_up mla_kv_lat_g w_kv_up mla_q_head_g mla_k_head_g moba_q_head_g moba_k_head_g out_norm_mla_g out_norm_moba_g w_out ffn_norm_g w_router_group b_router_group w_router_expert b_router_expert w_gate w_up w_down".split()


def kernel(**inputs):
    import concourse.bacc as bacc
    from concourse.bass_utils import run_bass_kernel_spmd

    nc = bacc.Bacc("TRN2", target_bir_lowering=False, num_devices=1)
    arrays = {n: np.ascontiguousarray(inputs[n]) for n in _SHAPES}
    arrays["consts"], arrays["rope"] = shape_constants()
    arrays = {f"in_{n}": v for n, v in arrays.items()}
    aps = {n[3:]: nc.dram_tensor(n, v.shape, mybir.dt.from_np(v.dtype), kind="ExternalInput").ap() for n, v in arrays.items()}
    out = nc.dram_tensor("y", (1, S, D), F32, kind="ExternalOutput").ap()
    layer(nc, aps, out)
    r = run_bass_kernel_spmd(nc, [arrays], core_ids=[0])
    return r.results[0]["y"]
```

```python
from contextlib import ExitStack

import numpy as np

import concourse.bass as bass
from concourse import mybir

P = 128
S = 256
NT = S // P
D = 1024
KT = D // P
H = 8
NOPE, RD, QK = 64, 32, 96
DH = 64
QL, KVL = 256, 128
IN_W = QL + KVL + RD + 3 * H * DH
C0 = QL + KVL + RD
NG, EPG = 4, 8
NE = NG * EPG
HID = 256
C = 32
EB = P // C
NB = NE // EB
OVC = S // C - 1
OVB = 2 * S // C // EB
OFF = 1000.0
EPS = 1e-6
NEG = -1.0e30
SLOT = 3 * KT * HID
KEY = S

F32 = mybir.dt.float32
BF16 = mybir.dt.bfloat16
I32 = mybir.dt.int32
ALU = mybir.AluOpType
ACT = mybir.ActivationFunctionType
AX = mybir.AxisListType

CI, CM, CR, CS = 0, 128, 256, 384
CONST_W = CS + C
ROPE_W = 2 * DH + 2 * RD


def shape_constants():
    c = np.zeros((P, CONST_W), np.float32)
    i = np.arange(P)
    c[:, CI:CI + P] = np.eye(P)
    c[:, CM:CM + P] = np.where(i[None, :] <= i[:, None], 0.0, NEG)
    c[:, CR:CR + P] = i[:, None] < i[None, :]
    c[:, CS:CS + C] = np.tile(np.eye(C), (P // C, 1))
    cols = []
    for dim in (DH, RD):
        inv = np.float32(10000.0) ** (-(np.arange(0, dim, 2, dtype=np.float32) / np.float32(dim)))
        ang = np.arange(S, dtype=np.float32)[:, None] * inv.astype(np.float32)[None, :]
        cos, sin = np.cos(ang), np.sin(ang)
        cols += [cos, cos, -sin, sin]
    return c, np.concatenate(cols, 1).astype(np.float32)


def layer(nc, a, out):
    with ExitStack() as ctx:
        def sb(name, shape, dt=F32):
            return ctx.enter_context(nc.sbuf_tensor(name, shape, dt))

        def sem(name):
            return ctx.enter_context(nc.semaphore(name))

        ring = sb("ring", [P, EB * SLOT])
        w_in = ring[:, EB * SLOT - KT * IN_W:EB * SLOT].rearrange("p (k n) -> p k n", k=KT)
        w_out = ring[:, 0:KT * D].rearrange("p (k n) -> p k n", k=KT)
        gate_up = [ring[:, i * SLOT:i * SLOT + 2 * KT * HID].rearrange("p (g k n) -> p k g n", g=2, k=KT) for i in range(EB)]
        down_w = [ring[:, i * SLOT + 2 * KT * HID:(i + 1) * SLOT].rearrange("p (j n) -> p j n", j=2) for i in range(EB)]

        x_sb = sb("x_sb", [P, NT, D])
        xn = sb("xn", [P, NT, KT, P])
        actT = sb("actT", [P, KT, S])
        hn = actT[:, :, :].rearrange("p k n -> p (k n)").rearrange("p (t k n) -> p t k n", t=NT, k=KT)
        const = sb("const", [P, CONST_W])
        ident = const[:, CI:CI + P]
        rope = sb("rope", [P, NT, ROPE_W])
        zone = sb("zone", [P, 2 * H * QK + 2 * H * QK + H * P + NT * C0 + NT * H * DH + NT * H * P + 2 * H * DH])
        z0 = 0

        def in_zone(n):
            nonlocal z0
            z0 += n
            return zone[:, z0 - n:z0]

        sq = in_zone(2 * H * QK).rearrange("p (b n) -> p b n", b=2)
        wup = in_zone(2 * H * QK + H * P)
        lat = in_zone(NT * C0).rearrange("p (t n) -> p t n", t=NT)
        mv = in_zone(NT * H * DH).rearrange("p (t n) -> p t n", t=NT)
        kva = in_zone(NT * H * P).rearrange("p (t n) -> p t n", t=NT)
        swp = in_zone(2 * H * DH).rearrange("p (b n) -> p b n", b=2)
        xn_flat = xn[:, :, :, :].rearrange("p t k n -> p (t k n)")
        latn = xn_flat[:, 0:NT * 3 * P].rearrange("p (t k n) -> p t k n", t=NT, k=3)
        latT = xn_flat[:, NT * 3 * P:NT * 3 * P + 3 * S].rearrange("p (k n) -> p k n", k=3)
        mq = sb("mq", [P, NT, H * DH])
        mk = sb("mk", [P, NT, H * DH])
        qa = sb("qa", [P, NT, H * QK])
        ka = sb("ka", [P, NT, H * QK])
        w_qup = wup[:, 0:2 * H * QK].rearrange("p (k n) -> p k n", k=2)
        w_kvup = wup[:, 2 * H * QK:]
        shared = sb("shared", [P, 2 * H * S + 2 * (H // 2) * S])
        spares = (zone[:, 0:SLOT], shared[:, 0:SLOT])
        spare_gate_up = [m[:, 0:2 * KT * HID].rearrange("p (g k n) -> p k g n", g=2, k=KT) for m in spares]
        spare_down = [m[:, 2 * KT * HID:].rearrange("p (j n) -> p j n", j=2) for m in spares]
        staged = zone[:, 0:NT * D].rearrange("p (t n) -> p t n", t=NT)
        qaT = shared[:, 0:H * S].rearrange("p (h s) -> p h s", h=H)
        kaT = shared[:, H * S:2 * H * S].rearrange("p (h s) -> p h s", h=H)
        mqT = shared[:, 2 * H * S:2 * H * S + H // 2 * S].rearrange("p (h s) -> p h s", h=H // 2)
        mkT = shared[:, 2 * H * S + H // 2 * S:].rearrange("p (h s) -> p h s", h=H // 2)
        s_sb = wup[:, 0:9 * P].rearrange("p (b n) -> p b n", b=3)
        pT_sb = wup[:, 9 * P:18 * P].rearrange("p (b n) -> p b n", b=3)
        p_sb = sq.rearrange("p b n -> p (b n)").rearrange("p (b n) -> p b n", b=4)
        mk_flat = mk[:, :, :].rearrange("p t n -> p (t n)")
        w_r = mk_flat[:, 0:KT * (NG + NE)].rearrange("p (k n) -> p k n", k=KT)
        gx = sb("gx", [P, KT])
        gf = sb("gf", [P, KT])
        go = sb("go", [P, KT])
        gql = sb("gql", [P, 2])
        gkvl = sb("gkvl", [P, 1])
        g_row = sb("g_row", [P, 2 * QK + 2 * DH])
        b_row = sb("b_row", [P, NG + NE])
        gap = ring[:, KT * D:EB * SLOT - KT * IN_W]
        tc_m = gap[:, 0:256].rearrange("p (n t d) -> p n t d", n=2, t=NT)
        ts_m = sb("ts_m", [P, 2, NT, DH])
        tc_a = gap[:, 256:640].rearrange("p (n t d) -> p n t d", n=2, t=NT)
        ts_a = gap[:, 640:768].rearrange("p (n t d) -> p n t d", n=2, t=NT)
        pe = sb("pe", [P, NT, 2, RD])
        eps = sb("eps", [P, 1])
        ones = sb("ones", [P, P])
        st = sb("st", [P, 160])
        mx = mk_flat[:, 288:320].rearrange("p (h t) -> p h t", t=2)
        nmx = mk_flat[:, 320:352].rearrange("p (h t) -> p h t", t=2)
        rsum = sb("rsum", [P, NT, 2 * H])
        lg = mk_flat[:, 352:424].rearrange("p (t n) -> p t n", t=NT)
        rt = mq[:, :, :].rearrange("p t n -> p (t n)")
        m01 = mk_flat[:, 424:488].rearrange("p (t n) -> p t n", t=NT)
        key_w = sb("key_w", [P, 4, NT])
        qa_flat, ka_flat = qa[:, :, :].rearrange("p t n -> p (t n)"), ka[:, :, :].rearrange("p t n -> p (t n)")
        slot_row = qa_flat[:, 0:(NB + OVB) * P].rearrange("p (b n) -> p b n", n=P)
        slot_col = sb("slot_col", [P, NB + OVB])
        e_key = mk_flat[:, 488:520]
        e_num, g_num = mk_flat[:, 520:552], mk_flat[:, 552:584].rearrange("p (g e) -> p g e", g=NG)
        totals = mk_flat[:, 584:616]
        W = NE * OVC
        ov_thr, ov_key, ov_exp = [ka_flat[:, n * W:(n + 1) * W].rearrange("p (e c) -> p e c", c=OVC) for n in range(3)]
        ov_j = sb("ov_j", [P, 1])
        ov_pick = ka_flat[:, 3 * W:3 * W + OVB * P].rearrange("p (b n) -> p b n", n=P)
        ov4 = sb("ov4", [P, OVB])
        nb_i = sb("nb_i", [P, 1], I32)
        eid_i = sb("eid_i", [P, EB * OVB], I32)
        def scratch_of(lo, n):
            return rt[:, lo:lo + NT * n].rearrange("p (t n) -> p t n", t=NT)

        glog, top, masked, keys = scratch_of(0, 8), scratch_of(16, 8), scratch_of(32, NE), scratch_of(96, NE)
        picked = rt[:, 256:256 + 4 * NE].rearrange("p (a e) -> p a e", a=4)
        gexp, enum = scratch_of(160, NG), scratch_of(168, 2)
        top_i = rt[:, 172:188].bitcast(mybir.dt.uint32).rearrange("p (t n) -> p t n", t=NT)
        gneg, eneg, gnum, gsum, eexp, wden = [rt[:, 188 + 2 * n:190 + 2 * n] for n in range(6)]
        junk = swp
        x_flat = x_sb[:, :, :].rearrange("p t n -> p (t n)")
        xg = x_flat[:, 0:KT * P].rearrange("p (k n) -> p k n", k=KT)
        key_bc = x_flat[:, KT * P:KT * P + 4 * S].rearrange("p (a t n) -> p a t n", a=4, t=NT)
        z0 = SLOT
        y_sb, u_sb, back = in_zone(D), in_zone(512), in_zone(S)
        hot = in_zone(NT * P).rearrange("p (t n) -> p t n", t=NT)
        back2 = in_zone(2 * S).rearrange("p (a n) -> p a n", a=2)
        sil, gT = in_zone(2 * C), in_zone(2 * C).rearrange("p (j n) -> p j n", j=2)
        assert z0 <= zone.shape[1]
        zeros = y_sb[:, 0:256].bitcast(BF16)
        ov = mk_flat[:, 616:616 + 3 * P]
        there, place = [rt[:, 384 + n * W:384 + (n + 1) * W] for n in range(2)]
        scratch = ka_flat[:, 3 * W + OVB * P:4 * W + OVB * P]

        B = [ctx.enter_context(nc.psum_tensor(f"bank{i}", [P, 512], F32)) for i in range(8)]

        names = """const_in gains_in wup_in wout_in wr_in setup pool_const tables
            gx_in x_rt rx_ready xT_done actT_ready proj_done raw_ready lat_rt latn_ready latT_done latT_ready
            lift_done raw2_ready mv_ready sq_done red_done rt_done swap_done heads_ready headT_done headT_act headT_dve
            score_done max_ready exp_done pT_done pT_even pT_odd pv_done o_ready o_rt oT_done mixT_ready
            outp_done x1b_ready x1_ready x1_rt hT_done h2T_ready logit_done hn_ready lg_ready r_exp r_max rank_in rank_done
            key_ready keybc_done keybc_ready hot_ready gath_done xg_ready up_done u_ready fold_done sil_ready g_ready
            down_done y_dve y_act back_ready scat_done weight_ready nb_ready ovk_ready ovt_done ov_ready y_out
            act_sq hot_half back_half y_stored dve_step act_step pool_step""".split()
        s = {n: sem(n) for n in names}
        x_in = [sem(f"x_in{t}") for t in range(NT)]
        win_in = [sem(f"win_in{k}") for k in range(KT)]
        gu_in = [sem(f"gu_in{i}") for i in range(EB)]
        dn_in = [sem(f"dn_in{i}") for i in range(EB)]
        gu_spare = [sem(f"gu_spare{j}") for j in range(2)]
        dn_spare = [sem(f"dn_spare{j}") for j in range(2)]

        st_x, st_l, st_h, st_o, st_f = st[:, 0:4], st[:, 4:16], st[:, 16:144], st[:, 144:152], st[:, 152:156]
        ms_x, r_x = st_x[:, 0:2], st_x[:, 2:4]
        ms_l, r_l = st_l[:, 0:4].rearrange("p (t g) -> p t g", g=2), st_l[:, 4:8].rearrange("p (t g) -> p t g", g=2)
        ms_pe = st_l[:, 8:10]
        ms_o, r_o = st_o[:, 0:4].rearrange("p (t g) -> p t g", g=2), st_o[:, 4:8].rearrange("p (t g) -> p t g", g=2)
        ms_f, r_f = st_f[:, 0:2], st_f[:, 2:4]

        def ms_h(u):
            return st_h[:, 16 * u:16 * u + 8]

        def r_h(u):
            return st_h[:, 16 * u + 8:16 * u + 16]

        UNITS = [("mq", 0), ("mk", 0), ("mq", 1), ("mk", 1), ("qa", 0), ("ka", 0), ("qa", 1), ("ka", 1)]
        RAW = {("mq", 0): 3, ("mq", 1): 4, ("mk", 0): 5, ("mk", 1): 6}
        RAW2 = {("qa", 0): 2, ("ka", 0): 4, ("qa", 1): 6, ("ka", 1): 8}

        def wait_raw(eng, unit):
            if unit in RAW:
                eng.wait_ge(s["raw_ready"], RAW[unit])
            else:
                eng.wait_ge(s["raw2_ready"], RAW2[unit])

        class Steps:

            def __init__(self, eng, name):
                self.eng, self.sem, self.n = eng, s[name], 0

            def __call__(self, ins):
                self.n += 1
                ins.then_inc(self.sem, 1)
                self.eng.wait_ge(self.sem, self.n)

        def load_expert(eng, i, e):
            base = i * SLOT
            n = KT * HID
            for j, w in enumerate((a["w_gate"], a["w_up"])):
                eng.dma_start(ring[:, base + j * n:base + (j + 1) * n],
                              w[0, e].rearrange("(p k) n -> p (k n)", k=KT)).then_inc(gu_in[i], 16)

        def load_down(eng, i, e):
            base = i * SLOT + 2 * KT * HID
            eng.dma_start(ring[:, base:base + 2 * D].rearrange("p (j n) -> p j n", j=2),
                          a["w_down"][0, e].rearrange("(j p) n -> p j n", j=2)).then_inc(dn_in[i], 16)

        TURNS = [(u, 0) for u in range(4)] + [(u, n) for u in range(4, 8) for n in range(2)]

        def turn_of(n):
            u, half = TURNS[n]
            kind, t = UNITS[u]
            full = {"mq": mqT, "mk": mkT, "qa": qaT, "ka": kaT}[kind]
            w = P if kind[0] == "m" else QK
            return u, half, full[0:w, 4 * half:4 * half + 4, t * P:(t + 1) * P], (6, 2, 7, 3)[n] if n < 4 else 7

        def head_turned(eng, n):
            _, _, dst, bank = turn_of(n)
            eng.wait_ge(s["headT_done"], n + 1)
            copy = eng.tensor_copy if n % 2 else eng.copy
            copy(dst, B[bank][0:dst.shape[0], :].rearrange("p (h s) -> p h s", h=4)).then_inc(s[("headT_act", "headT_dve")[n % 2]], 1)

        def head_pT(eng, h):
            eng.wait_ge(s["pT_done"], h + 1)
            if h >= 3:
                eng.wait_ge(s["pv_done"], h - 2)
            copy = eng.copy if h % 2 else eng.tensor_copy
            copy(pT_sb[:, h % 3, :], B[2 + h % 2][:, 0:3 * P]).then_inc(s[("pT_even", "pT_odd")[h % 2]], 1)

        block = ctx.enter_context(nc.Block())

        @block.sync
        def _(sp):
            sp.dma_start(x_sb[:, 0, :], a["x"][0, 0:P, :]).then_inc(x_in[0], 16)
            sp.dma_start(const[:, :], a["consts"]).then_inc(s["const_in"], 16)
            sp.dma_start(x_sb[:, 1, :], a["x"][0, P:2 * P, :]).then_inc(x_in[1], 16)
            sp.dma_start(gx[:, :], a["attn_norm_g"][0].rearrange("(p k) -> p k", k=KT)).then_inc(s["gx_in"], 16)
            w = a["w_in"][0].rearrange("(p k) n -> p k n", k=KT)
            for k in range(KT):
                sp.dma_start(w_in[:, k, :], w[:, k, :]).then_inc(win_in[k], 16)
            sp.dma_start(wup[:, 0:2 * H * QK], a["w_q_up"][0].rearrange("(p k) n -> p (k n)", k=2)).then_inc(s["wup_in"], 16)
            sp.dma_start(w_kvup, a["w_kv_up"][0]).then_inc(s["wup_in"], 16)
            for g in range(2):
                sp.dma_start(w_out[:, 4 * g:4 * g + 4, :], a["w_out"][0, 512 * g:512 * g + 512, :].rearrange("(p k) n -> p k n", k=4)).then_inc(s["wout_in"], 16)
            sp.wait_ge(s["proj_done"], 8)
            for i in (2, 3):
                load_expert(sp, i, i - 2)
                load_down(sp, i, i - 2)
            sp.wait_ge(s["headT_done"], 4)
            for dst, src in ((w_r[:, :, 0:NG], a["w_router_group"]), (w_r[:, :, NG:], a["w_router_expert"])):
                sp.dma_start(dst, src[0].rearrange("(p k) n -> p k n", k=KT)).then_inc(s["wr_in"], 16)
            sp.wait_ge(s["pv_done"], 2 * H)
            for x in range(2):
                for j, w in enumerate((a["w_gate"], a["w_up"])):
                    sp.dma_start(spares[x][:, j * KT * HID:(j + 1) * KT * HID], w[0, EB + x].rearrange("(p k) n -> p (k n)", k=KT)).then_inc(gu_spare[x], 16)
                sp.dma_start(spare_down[x], a["w_down"][0, EB + x].rearrange("(j p) n -> p j n", j=2)).then_inc(dn_spare[x], 16)
            sp.wait_ge(s["outp_done"], 8)
            for i in (0, 1):
                load_expert(sp, i, i + 2)
                load_down(sp, i, i + 2)

            def reload(i, last, e):
                sp.wait_ge(s["up_done"], last + 1)
                load_expert(sp, i, e)
                sp.wait_ge(s["down_done"], last + 1)
                load_down(sp, i, e)

            for last, (i, e) in enumerate(((2, EB + 2), (3, EB + 3), (0, 2 * EB), (1, 2 * EB + 1))):
                reload(i, last, e)
            with sp.Fori(2, NB - 1) as b:
                for i in (2, 3):
                    reload(i, EB * b - EB + i, EB * b + i)
                for i in (0, 1):
                    reload(i, EB * b + i, EB * b + EB + i)
            for i in (2, 3):
                reload(i, EB * (NB - 2) + i, EB * (NB - 1) + i)
            sp.wait_ge(s["nb_ready"], 1)
            n_ov = sp.value_load(nb_i[0:1, 0:1], min_val=0, max_val=OVB)
            with sp.If(n_ov > 0):
                sp.wait_ge(s["ov_ready"], 1)
                with sp.Fori(0, n_ov) as v:
                    for i in range(EB):
                        e = sp.value_load(eid_i[0:1, bass.ds(EB * v + i, 1)], min_val=0, max_val=NE - 1)
                        sp.wait_ge(s["up_done"], EB * v + EB * NB - EB + i + 1)
                        for j, w in enumerate((a["w_gate"], a["w_up"])):
                            sp.dma_start(ring[:, i * SLOT + j * KT * HID:i * SLOT + (j + 1) * KT * HID],
                                         w[0].rearrange("e (p k) n -> p e (k n)", k=KT)[:, bass.ds(e, 1), :]).then_inc(gu_in[i], 16)
                        sp.wait_ge(s["down_done"], EB * v + EB * NB - EB + i + 1)
                        sp.dma_start(down_w[i], a["w_down"][0].rearrange("e (j p) n -> p (e j) n", j=2)[:, bass.ds(2 * e, 2), :]).then_inc(dn_in[i], 16)
            for t in range(NT):
                for hf in range(2):
                    sp.wait_ge(s["y_out"], 2 * t + hf + 1)
                    sp.dma_start(out[0, t * P:(t + 1) * P, 512 * hf:512 * hf + 512], staged[:, t, 512 * hf:512 * hf + 512]).then_inc(s["y_stored"], 16)
            sp.wait_ge(s["y_stored"], 16 * 4)

        @block.gpsimd
        def _(pool):
            step = Steps(pool, "pool_step")
            gains = [(gql[:, :], a["mla_q_lat_g"][0].rearrange("(p k) -> p k", k=2)),
                     (gkvl[:, :], a["mla_kv_lat_g"][0].rearrange("(p k) -> p k", k=1)),
                     (g_row[:, 0:QK], a["mla_q_head_g"].to_broadcast([P, QK])),
                     (g_row[:, QK:2 * QK], a["mla_k_head_g"].to_broadcast([P, QK])),
                     (g_row[:, 2 * QK:2 * QK + DH], a["moba_q_head_g"].to_broadcast([P, DH])),
                     (g_row[:, 2 * QK + DH:], a["moba_k_head_g"].to_broadcast([P, DH])),
                     (go[:, 0:4], a["out_norm_mla_g"][0].rearrange("(p k) -> p k", k=4)),
                     (go[:, 4:8], a["out_norm_moba_g"][0].rearrange("(p k) -> p k", k=4)),
                     (gf[:, :], a["ffn_norm_g"][0].rearrange("(p k) -> p k", k=KT)),
                     (b_row[:, 0:NG], a["b_router_group"].to_broadcast([P, NG])),
                     (b_row[:, NG:], a["b_router_expert"].to_broadcast([P, NE])),
                     (rope[:, :, :], a["rope"].rearrange("(t p) n -> p t n", p=P))]
            for dst, src in gains:
                pool.dma_start(dst, src).then_inc(s["gains_in"], 16)
            pool.wait_ge(s["gains_in"], 16 * 12)
            gq, gk = g_row[:, 0:QK], g_row[:, QK:2 * QK]
            for n, g in enumerate((g_row[:, 2 * QK:2 * QK + DH], g_row[:, 2 * QK + DH:])):
                for t in range(NT):
                    pool.tensor_tensor(tc_m[:, n, t, :], rope[:, t, 0:DH], g, ALU.mult)
                    for h0, h1 in ((0, DH // 2), (DH // 2, 0)):
                        pool.tensor_tensor(ts_m[:, n, t, h0:h0 + DH // 2], rope[:, t, DH + h0:DH + h0 + DH // 2],
                                           g[:, h1:h1 + DH // 2], ALU.mult)
            for n, g in enumerate((gq, gk)):
                for t in range(NT):
                    pool.tensor_copy(tc_a[:, n, t, 0:NOPE], g[:, 0:NOPE])
                    pool.tensor_tensor(tc_a[:, n, t, NOPE:QK], rope[:, t, 2 * DH:2 * DH + RD], g[:, NOPE:QK], ALU.mult)
                    for h0, h1 in ((0, RD // 2), (RD // 2, 0)):
                        ins = pool.tensor_tensor(ts_a[:, n, t, h0:h0 + RD // 2],
                                                 rope[:, t, 2 * DH + RD + h0:2 * DH + RD + h0 + RD // 2],
                                                 g[:, NOPE + h1:NOPE + h1 + RD // 2], ALU.mult)
            step(ins)
            for u, (kind, t) in enumerate(UNITS):
                wait_raw(pool, (kind, t))
                if u >= 2:
                    pool.wait_ge(s["heads_ready"], u - 1)
                if kind in ("mq", "mk"):
                    n = int(kind == "mk")
                    x = (mq, mk)[n][:, t, :].rearrange("p (h d) -> p h d", h=H)
                    sw = swp[:, u % 2, :].rearrange("p (h d) -> p h d", h=H)
                    for h0, h1 in ((0, DH // 2), (DH // 2, 0)):
                        ins = pool.tensor_tensor(sw[:, :, h0:h0 + DH // 2], x[:, :, h1:h1 + DH // 2],
                                                 ts_m[:, n, t, h0:h0 + DH // 2].unsqueeze(1).to_broadcast([P, H, DH // 2]), ALU.mult)
                    step(ins)
                    pool.wait_ge(s["sq_done"], u + 1)
                    pool.tensor_tensor(x, x, tc_m[:, n, t, :].unsqueeze(1).to_broadcast([P, H, DH]), ALU.mult).then_inc(s["swap_done"], 1)
                elif kind == "qa":
                    x = qa[:, t, :].rearrange("p (h d) -> p h d", h=H)
                    sw = swp[:, u % 2, 0:H * RD].rearrange("p (h d) -> p h d", h=H)
                    for h0, h1 in ((0, RD // 2), (RD // 2, 0)):
                        ins = pool.tensor_tensor(sw[:, :, h0:h0 + RD // 2], x[:, :, NOPE + h1:NOPE + h1 + RD // 2],
                                                 ts_a[:, 0, t, h0:h0 + RD // 2].unsqueeze(1).to_broadcast([P, H, RD // 2]), ALU.mult)
                    step(ins)
                    pool.wait_ge(s["sq_done"], u + 1)
                    pool.tensor_tensor(x, x, tc_a[:, 0, t, :].unsqueeze(1).to_broadcast([P, H, QK]), ALU.mult).then_inc(s["swap_done"], 1)
                else:
                    for h0, h1 in ((0, RD // 2), (RD // 2, 0)):
                        pool.tensor_tensor(pe[:, t, 1, h0:h0 + RD // 2], lat[:, t, QL + KVL + h1:QL + KVL + h1 + RD // 2],
                                           ts_a[:, 1, t, h0:h0 + RD // 2], ALU.mult)
                    step(pool.tensor_tensor(pe[:, t, 0, :], lat[:, t, QL + KVL:C0], tc_a[:, 1, t, NOPE:QK], ALU.mult))
                    pool.tensor_tensor(pe[:, t, 0, :], pe[:, t, 0, :], pe[:, t, 1, :], ALU.add)
                    pool.tensor_tensor(ka[:, t, :].rearrange("p (h d) -> p h d", h=H)[:, :, 0:NOPE],
                                       kva[:, t, :].rearrange("p (h d) -> p h d", h=H)[:, :, 0:NOPE],
                                       tc_a[:, 1, t, 0:NOPE].unsqueeze(1).to_broadcast([P, H, NOPE]), ALU.mult).then_inc(s["swap_done"], 1)

            pool.wait_ge(s["headT_done"], len(TURNS))
            pool.iota(slot_row[:, 0:NB, :].rearrange("p b (i c) -> p (b i) c", c=C), [[KEY, NE], [1, C]], base=0,
                      channel_multiplier=0, allow_small_or_imprecise_dtypes=True)
            step(pool.memset(slot_row[:, NB:, :], -OFF))
            for i in range(EB):
                step(pool.iota(slot_col[C * i:C * i + C, 0:NB], [[EB * KEY, NB]], base=i * KEY,
                               channel_multiplier=1, allow_small_or_imprecise_dtypes=True))
            pool.iota(e_key[:, :], [[KEY, NE]], base=0, channel_multiplier=0, allow_small_or_imprecise_dtypes=True)
            pool.iota(e_num, [[1, NE]], base=0, channel_multiplier=0, allow_small_or_imprecise_dtypes=True)
            pool.iota(g_num, [[1, NG], [0, EPG]], base=0, channel_multiplier=0, allow_small_or_imprecise_dtypes=True)
            pool.iota(ov_thr[:, :, :], [[0, NE], [C, OVC]], base=C, channel_multiplier=0, allow_small_or_imprecise_dtypes=True)
            pool.iota(ov_key[:, :, :], [[KEY, NE], [C, OVC]], base=C + int(OFF), channel_multiplier=0, allow_small_or_imprecise_dtypes=True)
            pool.iota(ov_exp[:, :, :], [[1, NE], [0, OVC]], base=0, channel_multiplier=0, allow_small_or_imprecise_dtypes=True)
            pool.iota(ov_j[:, :], [[1, 1]], base=1, channel_multiplier=1, allow_small_or_imprecise_dtypes=True)
            pool.iota(ov4[:, :], [[EB, OVB]], base=0, channel_multiplier=0, allow_small_or_imprecise_dtypes=True)
            step(pool.memset(ov_pick[:, :, :], 0.0))
            for i in range(EB):
                ap = ov_pick[:, :, C * i:C * i + C]
                ins = pool.affine_select(out=ap, in_=ap, compare_op=ALU.not_equal, fill=1.0, base=-i,
                                         pattern=[[-EB, OVB], [0, C]], channel_multiplier=1)
            ins.then_inc(s["pool_const"], 1)
        @block.scalar
        def _(act):
            step = Steps(act, "act_step")
            act.wait_ge(s["setup"], 1)
            step(act.activation(st[:, 156:157], eps[:, 0:1], ACT.Sqrt))
            for t in range(NT):
                act.wait_ge(x_in[t], 16)
                ins = act.activation(xn[:, t, :, :].rearrange("p k n -> p (k n)"), x_sb[:, t, :], ACT.Square,
                                     scale=D ** -0.5, accum_out=ms_x[:, t:t + 1])
                step(ins)
            act.activation(ms_x, ms_x, ACT.Sqrt, bias=eps[:, 0:1]).then_inc(s["x_rt"], 1)
            act.wait_ge(s["rx_ready"], 1)

            def projected(dst, bank, t):
                return act.activation(dst, bank, ACT.Copy, scale=r_x[:, t:t + 1])

            for t in range(NT):
                act.wait_ge(s["proj_done"], t + 1)
                projected(lat[:, t, :], B[4 + t][:, 0:C0], t).then_inc(s["raw_ready"], 1)
                act.wait_ge(s["raw_ready"], t + 1)
                act.activation(sq[:, t, 0:QL], lat[:, t, 0:QL], ACT.Square, scale=QL ** -0.5, accum_out=ms_l[:, t, 0:1])
                act.activation(sq[:, t, QL:QL + KVL], lat[:, t, QL:QL + KVL], ACT.Square, scale=KVL ** -0.5, accum_out=ms_l[:, t, 1:2])
                step(act.activation(sq[:, t, QL + KVL:C0], lat[:, t, QL + KVL:C0], ACT.Square, scale=QK ** -0.5,
                                    accum_out=ms_pe[:, t:t + 1]))
            act.activation(st_l[:, 0:4], st_l[:, 0:4], ACT.Sqrt, bias=eps[:, 0:1]).then_inc(s["lat_rt"], 1)
            for t in range(NT):
                act.wait_ge(s["proj_done"], 3 + t)
                projected(mq[:, t, :], B[6 + t][:, :], t).then_inc(s["raw_ready"], 1)

            def square(u):
                kind, t = UNITS[u]
                if u >= 2:
                    act.wait_ge(s["red_done"], u - 1)
                d = DH if kind[0] == "m" else QK
                x = {"mq": mq, "mk": mk, "qa": qa, "ka": kva}[kind][:, t, :].rearrange("p (h d) -> p h d", h=H)
                w = NOPE if kind == "ka" else d
                wait_raw(act, (kind, t))
                act.activation(sq[:, u % 2, 0:H * w].rearrange("p (h d) -> p h d", h=H), x[:, :, 0:w], ACT.Square,
                               scale=d ** -0.5).then_inc(s["sq_done"], 1)

            def root(u):
                act.wait_ge(s["red_done"], u + 1)
                act.activation(ms_h(u), ms_h(u), ACT.Sqrt, bias=eps[:, 0:1]).then_inc(s["rt_done"], 1)

            square(0)
            for t in range(NT):
                act.wait_ge(s["proj_done"], 5 + t)
                projected(mk[:, t, :], B[t][:, :], t).then_inc(s["raw_ready"], 1)
            square(1)
            root(0)
            square(2)
            root(1)
            square(3)
            root(2)
            root(3)
            lifted = [(qa, 4), (qa, 5), (kva, 2), (kva, 3), (qa, 6), (qa, 7), (kva, 0), (kva, 1)]
            for n, (dst, bank) in enumerate(lifted):
                act.wait_ge(s["lift_done"], n + 1)
                t, hf = n // 4, n % 2
                w = H * QK // 2 if dst is qa else 512
                act.copy(dst[:, t, hf * w:hf * w + w], B[bank][:, 0:w]).then_inc(s["raw2_ready"], 1)
                if n == 3:
                    square(4)
                    square(5)
                    root(4)
                    root(5)
            square(6)
            square(7)
            root(6)
            root(7)
            for t in range(NT):
                act.wait_ge(s["proj_done"], 7 + t)
                projected(mv[:, t, :], B[4 + t][:, :], t).then_inc(s["mv_ready"], 1)
            step(act.activation(st[:, 156:157], eps[:, 0:1], ACT.Exp))
            head_turned(act, 0)
            head_turned(act, 2)
            def group_squares(g):
                for t in range(NT):
                    act.wait_ge(s["o_ready"], (3 + t, 1 + t)[g])
                    act.activation(junk[:, t, :], xn[:, t, 4 * g:4 * g + 4, :].rearrange("p k n -> p (k n)"),
                                   ACT.Square, scale=512 ** -0.5, accum_out=ms_o[:, t, g:g + 1]).then_inc(s["act_sq"], 1)

            for i in range(2 * H + 3):
                if i < 2 * H:
                    scale = (DH if i < H else QK) ** -0.5
                    act.wait_ge(s["max_ready"], i + 1)
                    if i >= 4:
                        act.wait_ge(s["pT_done"], i - 3)
                    for t in range(NT):
                        ins = act.activation(p_sb[:, i % 4, t * P:(2 * t + 1) * P], s_sb[:, i % 3, t * P:(2 * t + 1) * P],
                                             ACT.Exp, bias=nmx[:, i, t:t + 1], scale=scale, accum_out=rsum[:, t, i:i + 1])
                    ins.then_inc(s["exp_done"], 1)
                if i < 8 and i % 2 == 0:
                    head_turned(act, 4 + i)
                if i >= 3 and (i - 3) % 2:
                    head_pT(act, i - 3)
                if i == H + 6:
                    group_squares(1)
            step(act.activation(st[:, 156:157], eps[:, 0:1], ACT.Sqrt))
            group_squares(0)
            act.wait_ge(s["act_sq"], 4)
            act.activation(st_o[:, 0:4], st_o[:, 0:4], ACT.Sqrt, bias=eps[:, 0:1]).then_inc(s["o_rt"], 1)
            for t in range(NT):
                act.wait_ge(s["x1_ready"], 2 * t + 2)
                ins = act.activation(x_sb[:, t, :], xn[:, t, :, :].rearrange("p k n -> p (k n)"), ACT.Square, scale=D ** -0.5,
                                     accum_out=ms_f[:, t:t + 1])
                step(ins)
                act.activation(ms_f[:, t:t + 1], ms_f[:, t:t + 1], ACT.Sqrt, bias=eps[:, 0:1]).then_inc(s["x1_rt"], 1)
            step(act.activation(st[:, 156:157], eps[:, 0:1], ACT.Exp))
            act.wait_ge(s["logit_done"], 2)
            act.wait_ge(s["lg_ready"], 1)
            for t in range(NT):
                act.activation(hn[:, t, :, :].rearrange("p k n -> p (k n)"), xn[:, t, :, :].rearrange("p k n -> p (k n)"),
                               ACT.Copy, scale=r_f[:, t:t + 1]).then_inc(s["hn_ready"], 1)
            act.wait_ge(s["r_max"], 1)
            for t in range(NT):
                act.activation(gexp[:, t, :], lg[:, t, 0:NG], ACT.Exp, bias=gneg[:, t:t + 1], accum_out=gsum[:, t:t + 1])
            act.wait_ge(s["r_max"], 2)
            for t in range(NT):
                ins = act.activation(eexp[:, t:t + 1], top[:, t, 1:2], ACT.Exp, bias=eneg[:, t:t + 1])
            ins.then_inc(s["r_exp"], 1)
            step(act.activation(st[:, 156:157], eps[:, 0:1], ACT.Silu))

            def key_rows():
                for n in range(2):
                    act.wait_ge(s["keybc_done"], n + 1)
                    ins = act.copy(key_bc[:, 2 * n:2 * n + 2, :, :].rearrange("p a t n -> p (a t n)"), B[(7, 4)[n]][:, :])
                ins.then_inc(s["keybc_ready"], 1)

            def outputs_down(b, i, first):
                act.wait_ge(s["down_done"], EB * b + i + 1)
                if i == 0 and not first:
                    act.wait_ge(s["scat_done"], 4 * b)
                for q in (2, 3):
                    ins = act.copy(y_sb[C * i:C * i + C, 256 * q:256 * q + 256], B[7][C * q:C * q + C, 0:256])
                ins.then_inc(s["y_act"], 1)

            def batch(b, first):
                for i in range(EB):
                    act.wait_ge(s["up_done"], EB * b + i + 1)
                    if not (first and i == 0):
                        act.wait_ge(s["fold_done"], EB * b + i)
                    act.copy(u_sb, B[5][:, :]).then_inc(s["u_ready"], 1)
                    if first and i == 0:
                        key_rows()
                    if i > 0:
                        outputs_down(b, i - 1, first)
                    act.wait_ge(s["fold_done"], EB * b + i + 1)
                    if not (first and i == 0):
                        act.wait_ge(s["g_ready"], EB * b + i)
                    act.activation(sil, B[6][:, 0:2 * C], ACT.Silu).then_inc(s["sil_ready"], 1)
                outputs_down(b, EB - 1, first)

            batch(0, True)
            with act.Fori(1, NB) as b:
                batch(b, False)
            act.wait_ge(s["nb_ready"], 1)
            n_ov = act.value_load(nb_i[0:1, 0:1], min_val=0, max_val=OVB)
            with act.If(n_ov > 0):
                with act.Fori(0, n_ov) as v:
                    batch(v + NB, False)

        @block.tensor
        def _(pe_):
            pe_.wait_ge(s["const_in"], 16)
            for t in range(NT):
                pe_.wait_ge(x_in[t], 16)
                for hf in range(2):
                    for k in range(4):
                        ins = pe_.transpose(B[2 * t + hf][:, k * P:(k + 1) * P],
                                            x_sb[:, t, :].rearrange("p (n k) -> p k n", k=KT)[:, 4 * hf + k, :], ident)
                    ins.then_inc(s["xT_done"], 1)
            pe_.wait_ge(s["actT_ready"], 4)
            col = [0, C0, C0 + 512, C0 + 1024, IN_W]
            for k in range(KT):
                pe_.wait_ge(win_in[k], 16)
                for c in range(2):
                    for t in range(NT):
                        ins = pe_.matmul(B[4 + 2 * c + t][:, 0:col[c + 1] - col[c]], actT[:, k, t * P:(t + 1) * P],
                                         w_in[:, k, col[c]:col[c + 1]], start=(k == 0), stop=(k == KT - 1))
                        if k == KT - 1:
                            ins.then_inc(s["proj_done"], 1)

            def project(c, banks):
                for t in range(NT):
                    for k in range(KT):
                        ins = pe_.matmul(B[banks[t]][:, :], actT[:, k, t * P:(t + 1) * P],
                                         w_in[:, k, col[c]:col[c + 1]], start=(k == 0), stop=(k == KT - 1))
                    ins.then_inc(s["proj_done"], 1)

            project(2, (0, 1))
            pe_.wait_ge(s["latn_ready"], 1)
            for k in range(2):
                for t in range(NT):
                    ins = pe_.transpose(B[2][:, k * S + t * P:k * S + (t + 1) * P], latn[:, t, k, :], ident)
            ins.then_inc(s["latT_done"], 1)
            for t in range(NT):
                ins = pe_.transpose(B[3][:, t * P:(t + 1) * P], latn[:, t, 2, :], ident)
            ins.then_inc(s["latT_done"], 1)
            pe_.wait_ge(s["latT_ready"], 2)
            pe_.wait_ge(s["wup_in"], 32)
            for t in range(NT):
                pe_.wait_ge(s["raw_ready"], (2, 4)[t])
                for hf in range(2):
                    for k in range(2):
                        ins = pe_.matmul(B[4 + 2 * t + hf][:, 0:384], latT[:, k, t * P:(t + 1) * P],
                                         w_qup[:, k, 384 * hf:384 * hf + 384], start=(k == 0), stop=(k == 1))
                    ins.then_inc(s["lift_done"], 1)
                if t:
                    pe_.wait_ge(s["raw_ready"], 6)
                for hf in range(2):
                    pe_.matmul(B[(2, 0)[t] + hf][:, :], latT[:, 2, t * P:(t + 1) * P], w_kvup[:, 512 * hf:512 * hf + 512],
                               start=True, stop=True).then_inc(s["lift_done"], 1)
            pe_.wait_ge(s["raw2_ready"], 2)
            project(3, (4, 5))
            def head_turn(n):
                u, half, dst, bank = turn_of(n)
                kind, t = UNITS[u]
                pe_.wait_ge(s["heads_ready"], u + 1)
                if n == 0:
                    pe_.wait_ge(s["raw2_ready"], 8)
                if n >= 5:
                    pe_.wait_ge(s[("headT_dve", "headT_act")[n % 2]], (n + 1) // 2)
                if n == 4:
                    pe_.wait_ge(s["headT_act"], 2)
                src = {"mq": mq, "mk": mk, "qa": qa, "ka": ka}[kind][:, t, :].rearrange("p (h d) -> p h d", d=dst.shape[0])
                for j in range(4):
                    ins = pe_.transpose(B[bank][0:dst.shape[0], j * P:(j + 1) * P], src[:, 4 * half + j, :], ident)
                ins.then_inc(s["headT_done"], 1)

            for n in range(4):
                head_turn(n)
            pe_.wait_ge(s["mv_ready"], 2)
            pe_.wait_ge(s["headT_act"], 2)
            pe_.wait_ge(s["headT_dve"], 2)
            score_bank = (0, 1, 6)

            def scores(h):
                if h >= 3:
                    pe_.wait_ge(s["max_ready"], h - 2)
                if h == H:
                    pe_.wait_ge(s["headT_act"], 6)
                    pe_.wait_ge(s["headT_dve"], 6)
                if h < H:
                    p0 = 64 * (h % 2)
                    q, k = mqT[p0:p0 + DH, h // 2, :], mkT[p0:p0 + DH, h // 2, :]
                else:
                    q, k = qaT[0:QK, h - H, :], kaT[0:QK, h - H, :]
                for t in range(NT):
                    ins = pe_.matmul(B[score_bank[h % 3]][:, t * P:(2 * t + 1) * P], q[:, t * P:(t + 1) * P], k[:, 0:(t + 1) * P], start=True, stop=True)
                ins.then_inc(s["score_done"], 1)

            def turn(h):
                pe_.wait_ge(s["exp_done"], h + 1)
                if h >= 2:
                    pe_.wait_ge(s[("pT_even", "pT_odd")[h % 2]], h // 2)
                for j in range(3):
                    ins = pe_.transpose(B[2 + h % 2][:, j * P:(j + 1) * P], p_sb[:, h % 4, j * P:(j + 1) * P], ident)
                ins.then_inc(s["pT_done"], 1)

            def values(h):
                pe_.wait_ge(s[("pT_even", "pT_odd")[h % 2]], h // 2 + 1)
                g, hh = h // H, h % H
                v = [mv[:, t, DH * hh:DH * hh + DH] if g == 0 else kva[:, t, P * hh + NOPE:P * hh + P] for t in range(NT)]
                if h == H:
                    pe_.wait_ge(s["o_ready"], 1)
                o = [B[((4, 5), (7, 4))[g][t]][:, DH * hh:DH * hh + DH] for t in range(NT)]
                pe_.matmul(o[0], pT_sb[:, h % 3, 0:P], v[0], start=True, stop=True)
                pe_.matmul(o[1], pT_sb[:, h % 3, P:2 * P], v[0], start=True, stop=False)
                pe_.matmul(o[1], pT_sb[:, h % 3, 2 * P:3 * P], v[1], start=False, stop=True).then_inc(s["pv_done"], 1)

            def output_turn(n, bank):
                g, t = 1 - n // 2, n % 2
                for k in range(4):
                    ins = pe_.transpose(B[bank][:, k * P:(k + 1) * P], xn[:, t, 4 * g + k, :], ident)
                ins.then_inc(s["oT_done"], 1)

            for i in range(2 * H + 5):
                if i < 2 * H:
                    scores(i)
                if 3 <= i < 2 * H + 3:
                    turn(i - 3)
                if i >= 5:
                    values(i - 5)
                if i < 8:
                    head_turn(4 + i)
                if i == H + 6:
                    pe_.wait_ge(s["o_ready"], 2)
                    output_turn(0, 5)
                if i == H + 8:
                    pe_.wait_ge(s["mixT_ready"], 1)
                    output_turn(1, 5)
            pe_.wait_ge(s["wout_in"], 32)

            def project_out(g, t, banks):
                for hf in range(2):
                    for k in range(4 * g, 4 * g + 4):
                        ins = pe_.matmul(B[banks[hf]][:, :], actT[:, k, t * P:(t + 1) * P], w_out[:, k, 512 * hf:512 * hf + 512],
                                         start=(k == 4 * g), stop=(k == 4 * g + 3))
                    ins.then_inc(s["outp_done"], 1)

            pe_.wait_ge(s["mixT_ready"], 1)
            project_out(1, 0, (0, 1))
            pe_.wait_ge(s["mixT_ready"], 2)
            project_out(1, 1, (6, 5))
            pe_.wait_ge(s["pT_even"], H)
            pe_.wait_ge(s["pT_odd"], H)
            for t in range(NT):
                pe_.wait_ge(s["o_ready"], 3 + t)
                output_turn(2 + t, 2 + t)
            pe_.wait_ge(s["mixT_ready"], 3)
            pe_.wait_ge(s["o_ready"], 4)
            project_out(0, 0, (7, 4))
            pe_.wait_ge(s["mixT_ready"], 4)
            project_out(0, 1, (2, 3))
            for t in range(NT):
                pe_.wait_ge(s["x1_ready"], 2 * t + 2)
                for hf in range(2):
                    for k in range(4):
                        ins = pe_.transpose(B[((0, 1), (6, 5))[t][hf]][:, k * P:(k + 1) * P], xn[:, t, 4 * hf + k, :], ident)
                    ins.then_inc(s["hT_done"], 1)
            pe_.wait_ge(s["wr_in"], 32)
            for t in range(NT):
                pe_.wait_ge(s["h2T_ready"], 2 * t + 2)
                for k in range(KT):
                    ins = pe_.matmul(B[(7, 4)[t]][:, 0:NG + NE], actT[:, k, t * P:(t + 1) * P], w_r[:, k, :], start=(k == 0), stop=(k == KT - 1))
                ins.then_inc(s["logit_done"], 1)
            pe_.wait_ge(s["rank_in"], 1)
            tri = const[:, CR:CR + P]
            pe_.matmul(B[2][:, 0:NE], tri, m01[:, 0, :], start=True, stop=True)
            pe_.matmul(B[2][:, NE:2 * NE], ones[:, :], m01[:, 0, :], start=True, stop=False)
            pe_.matmul(B[2][:, NE:2 * NE], tri, m01[:, 1, :], start=False, stop=True)
            pe_.matmul(B[2][:, 2 * NE:3 * NE], ones[:, :], m01[:, 0, :], start=True, stop=False)
            pe_.matmul(B[2][:, 2 * NE:3 * NE], ones[:, :], m01[:, 1, :], start=False, stop=True).then_inc(s["rank_done"], 1)

            acc = [[B[2 * t + hf] for hf in range(2)] for t in range(NT)]

            def gather(part):
                for k in range(4):
                    for t in range(NT):
                        ins = pe_.matmul(B[5 - part][:, k * P:(k + 1) * P], hn[:, t, 4 * part + k, :], hot[:, t, :],
                                         start=(t == 0), stop=(t == NT - 1))
                ins.then_inc(s["gath_done"], 1)

            pe_.wait_ge(s["hot_ready"], 1)
            pe_.wait_ge(s["hn_ready"], 2)
            gather(0)
            gather(1)

            def key_rows():
                pe_.wait_ge(s["key_ready"], 1)
                pe_.wait_ge(s["weight_ready"], 1)
                for n in range(2):
                    for m in range(2):
                        for t in range(NT):
                            ins = pe_.matmul(B[(7, 4)[n]][:, (2 * m + t) * P:(2 * m + t + 1) * P],
                                             key_w[:, 2 * n + m, t:t + 1].to_broadcast([P, P]), ident, start=True, stop=True)
                    ins.then_inc(s["keybc_done"], 1)
                pe_.wait_ge(s["setup"], 2)
                for t in range(NT):
                    for hf in range(2):
                        pe_.matmul(acc[t][hf][:, :], zeros[:, 0:P], zeros, start=True, stop=False, skip_group_check=True)

            def up(b, i, first, spare):
                if first:
                    weights, place_in, value = gate_up[(i + 2) % EB], gu_in[(i + 2) % EB], 32
                elif spare:
                    weights, place_in, value = spare_gate_up[i], gu_spare[i], 32
                else:
                    weights, place_in, value = gate_up[i], gu_in[i], 32 * b + (0 if i < 2 else 32)
                pe_.wait_ge(place_in, value)
                if i == 0:
                    pe_.wait_ge(s["xg_ready"], 2 * b + 1)
                else:
                    pe_.wait_ge(s["u_ready"], EB * b + i)
                for k in range(KT):
                    j = k % EB
                    if i == 0 and k == EB:
                        pe_.wait_ge(s["xg_ready"], 2 * b + 2)
                    ins = pe_.matmul(B[5][C * j:C * j + C, :].rearrange("p (g n) -> p g n", g=2), xg[:, k, C * i:C * i + C],
                                     weights[:, k, :, :], start=(k < EB), stop=(k >= EB), skip_group_check=True)
                ins.then_inc(s["up_done"], 1)

            def fold(n, first):
                pe_.wait_ge(s["u_ready"], n + 1)
                if not first:
                    pe_.wait_ge(s["g_ready"], n)
                for c in range(4):
                    ins = pe_.matmul(B[6][:, C * c:C * c + C], u_sb[:, P * c:P * c + P], const[:, CS:CS + C], start=True, stop=True)
                ins.then_inc(s["fold_done"], 1)

            def down(b, i, first, spare):
                n = EB * b + i
                if first:
                    weights, place_in, value = down_w[(i + 2) % EB], dn_in[(i + 2) % EB], 16
                elif spare:
                    weights, place_in, value = spare_down[i], dn_spare[i], 16
                else:
                    weights, place_in, value = down_w[i], dn_in[i], 16 * b + (0 if i < 2 else 16)
                pe_.wait_ge(s["g_ready"], n + 1)
                pe_.wait_ge(place_in, value)
                if first and i == 0:
                    pe_.wait_ge(s["keybc_ready"], 1)
                else:
                    pe_.wait_ge(s["y_dve"], n)
                    pe_.wait_ge(s["y_act"], n)
                for j in range(2):
                    for q in range(4):
                        ins = pe_.matmul(B[7][C * q:C * q + C, 0:256], gT[:, j, :], weights[:, j, 256 * q:256 * q + 256],
                                         start=(j == 0), stop=(j == 1), skip_group_check=True)
                ins.then_inc(s["down_done"], 1)

            def scatter(b):
                pe_.wait_ge(s["y_dve"], EB * b + EB)
                pe_.wait_ge(s["y_act"], EB * b + EB)
                pe_.wait_ge(s["back_ready"], b + 1)
                for t in range(NT):
                    for hf in range(2):
                        ins = pe_.matmul(acc[t][hf][:, :], back[:, t * P:(t + 1) * P], y_sb[:, 512 * hf:512 * hf + 512],
                                         start=False, stop=False, skip_group_check=True)
                        ins.then_inc(s["scat_done"], 1)

            def batch(b, first=False, gathered=True, ahead=True, spares_used=False):
                if not gathered:
                    pe_.wait_ge(s["hot_ready"], b + 1)
                    gather(0)
                    gather(1)
                for i in range(EB):
                    n = EB * b + i
                    up(b, i, first, spares_used and i < 2)
                    if i == 0 and first:
                        key_rows()
                    elif i == 0 and gathered:
                        scatter(b - 1)
                    if i > 0:
                        down(b, i - 1, first, spares_used and i - 1 < 2)
                    if i == EB - 1 and ahead:
                        pe_.wait_ge(s["hot_ready"], b + 2)
                        pe_.wait_ge(s["u_ready"], n + 1)
                        gather(0)
                    fold(n, first and i == 0)
                    if i == EB - 1 and ahead:
                        gather(1)
                down(b, EB - 1, first, False)
                if not ahead:
                    scatter(b)

            batch(0, first=True)
            batch(1, spares_used=True)
            with pe_.Fori(2, NB - 1) as b:
                batch(b)
            batch(NB - 1, ahead=False)
            pe_.wait_ge(s["nb_ready"], 1)
            n_ov = pe_.value_load(nb_i[0:1, 0:1], min_val=0, max_val=OVB)
            with pe_.If(n_ov > 0):
                pe_.wait_ge(s["ovk_ready"], 1)
                pe_.wait_ge(s["g_ready"], EB * NB)
                pe_.matmul(B[4][:, :], ov[:, 0:P], ov_pick[:, :, :].rearrange("p b n -> p (b n)"), start=True, stop=True)
                for b in range(OVB):
                    pe_.matmul(B[6][:, b:b + 1], ov_pick[:, b, :], ov[:, P:P + 1], start=True, stop=True)
                pe_.matmul(B[6][:, P:P + EB * OVB], ov[:, 2 * P:3 * P], const[:, CI:CI + EB * OVB], start=True, stop=True).then_inc(s["ovt_done"], 1)
                with pe_.Fori(0, n_ov) as v:
                    batch(v + NB, gathered=False, ahead=False)

        @block.vector
        def _(dve):
            step = Steps(dve, "dve_step")
            dve.memset(eps[:, :], EPS)
            dve.memset(ones[:, :], 1.0).then_inc(s["setup"], 1)

            def turned(n, gain, bank, done, t, k, ready):
                dve.wait_ge(s[done], n + 1)
                dve.tensor_tensor(actT[:, k:k + 4, t * P:(t + 1) * P], B[bank][:, :].rearrange("p (k n) -> p k n", k=4),
                                  gain[:, k:k + 4].unsqueeze(2).to_broadcast([P, 4, P]), ALU.mult).then_inc(s[ready], 1)

            def permuted(x):
                return x.rearrange("p (n k) -> p k n", k=KT)

            dve.wait_ge(s["gx_in"], 16)
            for n in range(4):
                turned(n, gx, n, "xT_done", n // 2, 4 * (n % 2), "actT_ready")
            dve.wait_ge(s["x_rt"], 1)
            dve.reciprocal(r_x, ms_x).then_inc(s["rx_ready"], 1)
            dve.wait_ge(s["gains_in"], 16 * 12)
            dve.wait_ge(s["lat_rt"], 1)
            step(dve.reciprocal(st_l[:, 4:8], st_l[:, 0:4]))
            for t in range(NT):
                dve.tensor_scalar(latn[:, t, 0:2, :], lat[:, t, 0:QL].rearrange("p (n k) -> p k n", k=2), r_l[:, t, 0:1], None, ALU.mult)
                ins = dve.tensor_scalar(latn[:, t, 2, :], lat[:, t, QL:QL + KVL], r_l[:, t, 1:2], None, ALU.mult)
            ins.then_inc(s["latn_ready"], 1)

            def head_norm(u):
                kind, t = UNITS[u]
                d = DH if kind[0] == "m" else QK
                w = NOPE if kind == "ka" else d
                dve.wait_ge(s["sq_done"], u + 1)
                ins = dve.tensor_reduce(ms_h(u), sq[:, u % 2, 0:H * w].rearrange("p (h d) -> p h d", h=H), AX.X, ALU.add)
                if kind == "ka":
                    step(ins)
                    ins = dve.tensor_scalar(ms_h(u), ms_h(u), ms_pe[:, t:t + 1], None, ALU.add)
                ins.then_inc(s["red_done"], 1)

            def head_scale(u):
                kind, t = UNITS[u]
                dve.wait_ge(s["rt_done"], u + 1)
                dve.wait_ge(s["swap_done"], u + 1)
                if kind[0] == "m":
                    x = (mq if kind == "mq" else mk)[:, t, :].rearrange("p (h d) -> p h d", h=H)
                    dve.tensor_tensor(x, x, swp[:, u % 2, :].rearrange("p (h d) -> p h d", h=H), ALU.add)
                    d = DH
                elif kind == "qa":
                    x = qa[:, t, :].rearrange("p (h d) -> p h d", h=H)
                    dve.tensor_tensor(x[:, :, NOPE:QK], x[:, :, NOPE:QK],
                                      swp[:, u % 2, 0:H * RD].rearrange("p (h d) -> p h d", h=H), ALU.add)
                    d = QK
                else:
                    x = ka[:, t, :].rearrange("p (h d) -> p h d", h=H)
                    dve.tensor_copy(x[:, :, NOPE:QK], pe[:, t, 0, :].unsqueeze(1).to_broadcast([P, H, RD]))
                    d = QK
                step(dve.reciprocal(r_h(u), ms_h(u)))
                dve.tensor_tensor(x, x, r_h(u).unsqueeze(2).to_broadcast([P, H, d]), ALU.mult).then_inc(s["heads_ready"], 1)

            head_norm(0)
            for n, (lo, gain) in enumerate(((0, gql), (2, gkvl))):
                dve.wait_ge(s["latT_done"], n + 1)
                m = 2 - n
                dve.tensor_tensor(latT[:, lo:lo + m, :], B[2 + n][:, 0:m * S].rearrange("p (k n) -> p k n", k=m),
                                  gain[:, :].unsqueeze(2).to_broadcast([P, m, S]), ALU.mult).then_inc(s["latT_ready"], 1)
            head_norm(1)
            for u in range(len(UNITS)):
                head_scale(u)
                if u + 2 < len(UNITS):
                    head_norm(u + 2)

            def mask_max(h):
                scale = (DH if h < H else QK) ** -0.5
                dve.wait_ge(s["score_done"], h + 1)
                if h >= 3:
                    dve.wait_ge(s["exp_done"], h - 2)
                tri = const[:, CM:CM + P]
                sc, dst = B[(0, 1, 6)[h % 3]], s_sb[:, h % 3, :]
                dve.tensor_tensor_reduce(dst[:, 0:P], sc[:, 0:P], tri, 1.0, NEG, ALU.add, ALU.max, mx[:, h, 0:1])
                step(dve.tensor_tensor_reduce(dst[:, P:3 * P], sc[:, P:3 * P], wide_mask(), 1.0, NEG, ALU.add, ALU.max, mx[:, h, 1:2]))
                dve.tensor_scalar(nmx[:, h, :], mx[:, h, :], -scale, None, ALU.mult).then_inc(s["max_ready"], 1)

            def wide_mask():
                return rt[:, 768:1024]

            def outputs(g):
                dve.wait_ge(s["pv_done"], H * g + H)
                step(dve.reciprocal(rsum[:, :, H * g:H * g + H], rsum[:, :, H * g:H * g + H]))
                for t in range(NT):
                    dve.tensor_tensor(xn[:, t, 4 * (1 - g):4 * (1 - g) + 4, :].rearrange("p k (h q) -> p k h q", h=H),
                                      B[((4, 5), (7, 4))[g][t]][:, :].rearrange("p (h q k) -> p k h q", h=H, k=4),
                                      rsum[:, t, H * g:H * g + H].unsqueeze(1).unsqueeze(3).to_broadcast([P, 4, H, DH // 4]),
                                      ALU.mult).then_inc(s["o_ready"], 1)

            head_turned(dve, 1)
            head_turned(dve, 3)
            dve.memset(wide_mask()[:, 0:P], 0.0)
            step(dve.tensor_copy(wide_mask()[:, P:2 * P], const[:, CM:CM + P]))
            for i in range(2 * H + 3):
                if i < 2 * H:
                    mask_max(i)
                if i < 8 and i % 2:
                    head_turned(dve, 4 + i)
                if i >= 3 and (i - 3) % 2 == 0:
                    head_pT(dve, i - 3)
                if i == H + 4:
                    outputs(0)
                if i == H + 7:
                    turned(0, go, 5, "oT_done", 0, 4, "mixT_ready")
            turned(1, go, 5, "oT_done", 1, 4, "mixT_ready")
            outputs(1)

            def add_group(g, t, banks, first):
                for hf in range(2):
                    dve.wait_ge(s["outp_done"], first + hf + 1)
                    x = x_sb[:, t, 512 * hf:512 * hf + 512]
                    if g == 1:
                        dve.scalar_tensor_tensor(out=x, in0=B[banks[hf]][:, :], scalar=r_o[:, t, 1:2], in1=x,
                                                 op0=ALU.mult, op1=ALU.add).then_inc(s["x1b_ready"], 1)
                    else:
                        dve.wait_ge(s["x1b_ready"], 2 * t + hf + 1)
                        dve.scalar_tensor_tensor(out=xn[:, t, :, 64 * hf:64 * hf + 64], in0=permuted(B[banks[hf]][:, :]),
                                                 scalar=r_o[:, t, 0:1], in1=permuted(x), op0=ALU.mult, op1=ALU.add).then_inc(s["x1_ready"], 1)

            dve.wait_ge(s["o_rt"], 1)
            step(dve.reciprocal(st_o[:, 4:8], st_o[:, 0:4]))
            add_group(1, 0, (0, 1), 0)
            add_group(1, 1, (6, 5), 2)
            for t in range(NT):
                turned(2 + t, go, 2 + t, "oT_done", t, 0, "mixT_ready")
            add_group(0, 0, (7, 4), 4)
            add_group(0, 1, (2, 3), 6)
            for t in range(NT):
                for hf in range(2):
                    turned(2 * t + hf, gf, ((0, 1), (6, 5))[t][hf], "hT_done", t, 4 * hf, "h2T_ready")
            dve.wait_ge(s["x1_rt"], 2)
            step(dve.reciprocal(r_f, ms_f))
            dve.memset(zeros, 0.0).then_inc(s["setup"], 1)

            dve.memset(glog[:, :, NG:], NEG)
            dve.wait_ge(s["pool_const"], 1)
            for t in range(NT):
                dve.wait_ge(s["logit_done"], t + 1)
                ins = dve.scalar_tensor_tensor(out=lg[:, t, :], in0=B[(7, 4)[t]][:, 0:NG + NE], scalar=r_f[:, t:t + 1],
                                               in1=b_row[:, :], op0=ALU.mult, op1=ALU.add)
            ins.then_inc(s["lg_ready"], 1)
            dve.wait_ge(s["lg_ready"], 1)

            def both(make):
                make(0)
                step(make(1))

            both(lambda t: dve.tensor_copy(glog[:, t, 0:NG], lg[:, t, 0:NG]))
            both(lambda t: dve.max(top[:, t, :], glog[:, t, :]))
            dve.tensor_scalar(gneg, top[:, :, 0], -1.0, None, ALU.mult).then_inc(s["r_max"], 1)
            both(lambda t: dve.max_index(top_i[:, t, :], top[:, t, :], glog[:, t, :]))
            step(dve.tensor_copy(gnum, top_i[:, :, 0]))
            both(lambda t: dve.tensor_scalar(masked[:, t, :], g_num.rearrange("p g e -> p (g e)"), gnum[:, t:t + 1], NEG, ALU.not_equal, ALU.mult))
            step(dve.tensor_tensor(masked, masked, lg[:, :, NG:], ALU.add))
            dve.wait_ge(s["r_max"], 1)
            both(lambda t: dve.max(top[:, t, :], masked[:, t, :]))
            dve.tensor_scalar(eneg, top[:, :, 0], -1.0, None, ALU.mult).then_inc(s["r_max"], 1)
            both(lambda t: dve.max_index(top_i[:, t, :], top[:, t, :], masked[:, t, :]))
            step(dve.tensor_copy(enum, top_i[:, :, 0:2]))
            both(lambda t: dve.tensor_scalar(m01[:, t, :], e_num, enum[:, t, 1:2], None, ALU.is_equal))
            for t in range(NT):
                ins = dve.scalar_tensor_tensor(out=m01[:, t, :], in0=e_num, scalar=enum[:, t, 0:1], in1=m01[:, t, :],
                                               op0=ALU.is_equal, op1=ALU.add)
            ins.then_inc(s["rank_in"], 1)
            dve.wait_ge(s["r_exp"], 1)
            step(dve.tensor_scalar(wden, eexp, 1.0, None, ALU.add))
            step(dve.tensor_tensor(wden, wden, gsum, ALU.mult))
            step(dve.reciprocal(key_w[:, 2, :], wden))
            dve.tensor_tensor(key_w[:, 3, :], key_w[:, 2, :], eexp, ALU.mult).then_inc(s["weight_ready"], 1)
            dve.wait_ge(s["rank_done"], 1)
            dve.tensor_copy(totals, B[2][:, 2 * NE:3 * NE])
            step(dve.tensor_tensor(keys, B[2][:, 0:NT * NE].rearrange("p (t e) -> p t e", t=NT),
                                   e_key.unsqueeze(1).to_broadcast([P, NT, NE]), ALU.add))
            for n in range(2):
                for t in range(NT):
                    ins = dve.scalar_tensor_tensor(out=picked[:, 2 * n + t, :], in0=e_num, scalar=enum[:, t, n:n + 1], in1=keys[:, t, :],
                                                   op0=ALU.is_equal, op1=ALU.mult, accum_out=key_w[:, n, t:t + 1])
            ins.then_inc(s["key_ready"], 1)
            dve.wait_ge(s["key_ready"], 1)

            def one_hot(b):
                row = slot_row[:, bass.ds(b, 1), :].rearrange("p b n -> p (b n)")
                for t in range(NT):
                    dve.tensor_scalar(hot[:, t, :], row, key_w[:, 0, t:t + 1], None, ALU.is_equal)
                return row

            def one_hot_add(row):
                for t in range(NT):
                    ins = dve.scalar_tensor_tensor(out=hot[:, t, :], in0=row, scalar=key_w[:, 1, t:t + 1], in1=hot[:, t, :],
                                                   op0=ALU.is_equal, op1=ALU.add)
                ins.then_inc(s["hot_ready"], 1)

            row = slot_row[:, 0, :]
            both(lambda t: dve.tensor_scalar(hot[:, t, :], row, key_w[:, 0, t:t + 1], None, ALU.is_equal))
            one_hot_add(row)

            def gathered_out(part, value):
                dve.wait_ge(s["gath_done"], value)
                dve.tensor_tensor(xg[:, 4 * part:4 * part + 4, :], B[5 - part][:, :].rearrange("p (k n) -> p k n", k=4),
                                  gf[:, 4 * part:4 * part + 4].unsqueeze(2).to_broadcast([P, 4, P]), ALU.mult).then_inc(s["xg_ready"], 1)

            gathered_out(0, 1)
            gathered_out(1, 2)
            def further_chunks():
                step(dve.tensor_tensor(there.rearrange("p (e c) -> p e c", c=OVC), totals.unsqueeze(2).to_broadcast([P, NE, OVC]),
                                       ov_thr[:, :, :], ALU.is_gt))
                step(dve.memset(scratch, 1.0))
                step(dve.tensor_tensor_scan(place, scratch, there, 0.0, ALU.mult, ALU.add))
                step(dve.tensor_scalar(small[:, 0:OVB], ov4[:, :], place[:, W - 1:W], None, ALU.is_lt))
                step(dve.tensor_reduce(small[:, 4:5], small[:, 0:OVB], AX.X, ALU.add))
                dve.tensor_copy(nb_i[:, :], small[:, 4:5]).then_inc(s["nb_ready"], 1)
                for n, table in enumerate((ov_key, ov_exp)):
                    step(dve.tensor_tensor(scratch, there, table[:, :, :].rearrange("p e c -> p (e c)"), ALU.mult))
                    step(dve.scalar_tensor_tensor(out=scratch, in0=place, scalar=ov_j[:, 0:1], in1=scratch, op0=ALU.is_equal,
                                                  op1=ALU.mult, accum_out=small[:, 6 + n:7 + n]))
                step(dve.tensor_scalar(small[:, 6:7], small[:, 6:7], -OFF, None, ALU.add))

            small = rt[:, 220:240]

            def hot_and_back(b, first, gathered, ahead):
                turn_hot = ahead or not gathered
                if ahead:
                    dve.wait_ge(s["gath_done"], 2 * b + 2)
                    row = one_hot(b + 1)
                elif not gathered:
                    dve.wait_ge(s["gath_done"], 2 * b)
                    row = one_hot(b)
                if first:
                    dve.wait_ge(s["keybc_ready"], 1)
                for m in range(2):
                    ins = dve.tensor_scalar(back2[:, m, :], key_bc[:, m, :, :].rearrange("p t n -> p (t n)"),
                                            slot_col[:, bass.ds(b, 1)], None, ALU.is_equal)
                ins.then_inc(s["hot_half"], 1)
                dve.wait_ge(s["hot_half"], b + 1)
                if turn_hot:
                    one_hot_add(row)
                for m in range(2):
                    ins = dve.tensor_tensor(back2[:, m, :], back2[:, m, :], key_bc[:, 2 + m, :, :].rearrange("p t n -> p (t n)"), ALU.mult)
                ins.then_inc(s["back_half"], 1)
                dve.wait_ge(s["back_half"], b + 1)
                if not first:
                    dve.wait_ge(s["scat_done"], 4 * b)
                dve.tensor_tensor(back, back2[:, 0, :], back2[:, 1, :], ALU.add).then_inc(s["back_ready"], 1)

            def product(n, first):
                dve.wait_ge(s["sil_ready"], n + 1)
                if not first:
                    dve.wait_ge(s["down_done"], n)
                dve.tensor_tensor(gT, sil.rearrange("p (j n) -> p j n", j=2), B[6][:, 2 * C:4 * C].rearrange("p (j n) -> p j n", j=2),
                                  ALU.mult).then_inc(s["g_ready"], 1)

            def outputs_up(b, i):
                dve.wait_ge(s["down_done"], EB * b + i + 1)
                for q in (0, 1):
                    ins = dve.tensor_copy(y_sb[C * i:C * i + C, 256 * q:256 * q + 256], B[7][C * q:C * q + C, 0:256])
                ins.then_inc(s["y_dve"], 1)

            def batch(b, first=False, gathered=True, ahead=True):
                if not first:
                    hot_and_back(b, first, gathered, ahead)
                if not gathered:
                    gathered_out(0, 2 * b + 1)
                    gathered_out(1, 2 * b + 2)
                for i in range(EB):
                    if i > 0:
                        outputs_up(b, i - 1)
                    if i == EB - 1 and ahead:
                        gathered_out(0, 2 * b + 3)
                    product(EB * b + i, first and i == 0)
                    if i == EB - 1 and ahead:
                        gathered_out(1, 2 * b + 4)
                    if i == 0 and first:
                        hot_and_back(b, first, gathered, ahead)
                    if first and i == 1:
                        further_chunks()
                outputs_up(b, EB - 1)

            batch(0, first=True)
            with dve.Fori(1, NB - 1) as b:
                batch(b)
            batch(NB - 1, ahead=False)
            n_ov = dve.value_load(nb_i[0:1, 0:1], min_val=0, max_val=OVB)
            with dve.If(n_ov > 0):
                dve.tensor_scalar(ov[:, 0:P], ones[:, :], small[:, 6:7], None, ALU.mult)
                dve.tensor_scalar(ov[:, 2 * P:3 * P], ones[:, :], small[:, 7:8], None, ALU.mult)
                dve.tensor_copy(ov[:, P:P + 1], small[:, 6:7]).then_inc(s["ovk_ready"], 1)
                dve.wait_ge(s["ovt_done"], 1)
                for b in range(OVB):
                    dve.tensor_tensor(slot_row[:, NB + b, :].rearrange("p (i c) -> p i c", i=EB),
                                      B[4][:, b * P:(b + 1) * P].rearrange("p (i c) -> p i c", i=EB),
                                      slot_row[:, 0, 0:C].unsqueeze(1).to_broadcast([P, EB, C]), ALU.add)
                for i in range(EB):
                    dve.tensor_scalar(slot_col[C * i:C * i + C, NB:], B[6][C * i:C * i + C, 0:OVB],
                                      slot_col[C * i:C * i + C, 0:1], float(-i * KEY), ALU.add, ALU.add)
                dve.tensor_copy(eid_i[:, :], B[6][:, P:P + EB * OVB]).then_inc(s["ov_ready"], 1)
                dve.wait_ge(s["ov_ready"], 1)
                with dve.Fori(0, n_ov) as v:
                    batch(v + NB, gathered=False, ahead=False)
                dve.wait_ge(s["scat_done"], 4 * n_ov + 4 * NB)
                dve.memset(small[:, 9:10], 0.0)
            for t in range(NT):
                for hf in range(2):
                    dve.wait_ge(s["scat_done"], 4 * NB - 3 + 2 * t + hf)
                    dve.tensor_tensor(staged[:, t, 512 * hf:512 * hf + 512].rearrange("p (n k) -> p n k", k=KT),
                                      xn[:, t, :, 64 * hf:64 * hf + 64].rearrange("p k n -> p n k"),
                                      B[2 * t + hf][:, :].rearrange("p (n k) -> p n k", k=KT), ALU.add).then_inc(s["y_out"], 1)


_SHAPES = "x attn_norm_g w_in mla_q_lat_g w_q_up mla_kv_lat_g w_kv_up mla_q_head_g mla_k_head_g moba_q_head_g moba_k_head_g out_norm_mla_g out_norm_moba_g w_out ffn_norm_g w_router_group b_router_group w_router_expert b_router_expert w_gate w_up w_down".split()


def kernel(**inputs):
    import concourse.bacc as bacc
    from concourse.bass_utils import run_bass_kernel_spmd

    nc = bacc.Bacc("TRN2", target_bir_lowering=False, num_devices=1)
    arrays = {n: np.ascontiguousarray(inputs[n]) for n in _SHAPES}
    arrays["consts"], arrays["rope"] = shape_constants()
    arrays = {f"in_{n}": v for n, v in arrays.items()}
    aps = {n[3:]: nc.dram_tensor(n, v.shape, mybir.dt.from_np(v.dtype), kind="ExternalInput").ap() for n, v in arrays.items()}
    out = nc.dram_tensor("y", (1, S, D), F32, kind="ExternalOutput").ap()
    layer(nc, aps, out)
    r = run_bass_kernel_spmd(nc, [arrays], core_ids=[0])
    return r.results[0]["y"]
```

```python
from contextlib import ExitStack

import numpy as np

import concourse.bass as bass
from concourse import mybir

P = 128
S = 256
NT = S // P
D = 1024
KT = D // P
H = 8
NOPE, RD, QK = 64, 32, 96
DH = 64
QL, KVL = 256, 128
IN_W = QL + KVL + RD + 3 * H * DH
C0 = QL + KVL + RD
NG, EPG = 4, 8
NE = NG * EPG
HID = 256
C = 32
EB = P // C
NB = NE // EB
OVC = S // C - 1
OVB = 2 * S // C // EB
OFF = 1000.0
EPS = 1e-6
NEG = -1.0e30
SLOT = 3 * KT * HID
KEY = S

F32 = mybir.dt.float32
I32 = mybir.dt.int32
ALU = mybir.AluOpType
ACT = mybir.ActivationFunctionType
AX = mybir.AxisListType

CI, CM, CR, CS = 0, 128, 256, 384
CONST_W = CS + C
ROPE_W = 2 * DH + 2 * RD


def shape_constants():
    c = np.zeros((P, CONST_W), np.float32)
    i = np.arange(P)
    c[:, CI:CI + P] = np.eye(P)
    c[:, CM:CM + P] = np.where(i[None, :] <= i[:, None], 0.0, NEG)
    c[:, CR:CR + P] = i[:, None] < i[None, :]
    c[:, CS:CS + C] = np.tile(np.eye(C), (P // C, 1))
    cols = []
    for dim in (DH, RD):
        inv = np.float32(10000.0) ** (-(np.arange(0, dim, 2, dtype=np.float32) / np.float32(dim)))
        ang = np.arange(S, dtype=np.float32)[:, None] * inv.astype(np.float32)[None, :]
        cos, sin = np.cos(ang), np.sin(ang)
        cols += [cos, cos, -sin, sin]
    return c, np.concatenate(cols, 1).astype(np.float32)


def layer(nc, a, out):
    with ExitStack() as ctx:
        def sb(name, shape, dt=F32):
            return ctx.enter_context(nc.sbuf_tensor(name, shape, dt))

        def sem(name):
            return ctx.enter_context(nc.semaphore(name))

        ring = sb("ring", [P, EB * SLOT])
        w_in = ring[:, EB * SLOT - KT * IN_W:EB * SLOT].rearrange("p (k n) -> p k n", k=KT)
        w_out = ring[:, 0:KT * D].rearrange("p (k n) -> p k n", k=KT)
        gate_up = [ring[:, i * SLOT:i * SLOT + 2 * KT * HID].rearrange("p (g k n) -> p k g n", g=2, k=KT) for i in range(EB)]
        down_w = [ring[:, i * SLOT + 2 * KT * HID:(i + 1) * SLOT].rearrange("p (j n) -> p j n", j=2) for i in range(EB)]

        x_sb = sb("x_sb", [P, NT, D])
        xn = sb("xn", [P, NT, KT, P])
        actT = sb("actT", [P, KT, S])
        hn = actT[:, :, :].rearrange("p k n -> p (k n)").rearrange("p (t k n) -> p t k n", t=NT, k=KT)
        const = sb("const", [P, CONST_W])
        ident = const[:, CI:CI + P]
        rope = sb("rope", [P, NT, ROPE_W])
        zone = sb("zone", [P, 2 * H * QK + 2 * H * QK + H * P + NT * C0 + NT * H * DH + NT * H * P + 2 * H * DH])
        z0 = 0

        def in_zone(n):
            nonlocal z0
            z0 += n
            return zone[:, z0 - n:z0]

        sq = in_zone(2 * H * QK).rearrange("p (b n) -> p b n", b=2)
        wup = in_zone(2 * H * QK + H * P)
        lat = in_zone(NT * C0).rearrange("p (t n) -> p t n", t=NT)
        mv = in_zone(NT * H * DH).rearrange("p (t n) -> p t n", t=NT)
        kva = in_zone(NT * H * P).rearrange("p (t n) -> p t n", t=NT)
        swp = in_zone(2 * H * DH).rearrange("p (b n) -> p b n", b=2)
        xn_flat = xn[:, :, :, :].rearrange("p t k n -> p (t k n)")
        latn = xn_flat[:, 0:NT * 3 * P].rearrange("p (t k n) -> p t k n", t=NT, k=3)
        latT = xn_flat[:, NT * 3 * P:NT * 3 * P + 3 * S].rearrange("p (k n) -> p k n", k=3)
        mq = sb("mq", [P, NT, H * DH])
        mk = sb("mk", [P, NT, H * DH])
        qa = sb("qa", [P, NT, H * QK])
        ka = sb("ka", [P, NT, H * QK])
        w_qup = wup[:, 0:2 * H * QK].rearrange("p (k n) -> p k n", k=2)
        w_kvup = wup[:, 2 * H * QK:]
        shared = sb("shared", [P, 2 * H * S + 2 * (H // 2) * S])
        spares = (zone[:, 0:SLOT], shared[:, 0:SLOT])
        spare_gate_up = [m[:, 0:2 * KT * HID].rearrange("p (g k n) -> p k g n", g=2, k=KT) for m in spares]
        spare_down = [m[:, 2 * KT * HID:].rearrange("p (j n) -> p j n", j=2) for m in spares]
        staged = zone[:, 0:NT * D].rearrange("p (t n) -> p t n", t=NT)
        qaT = shared[:, 0:H * S].rearrange("p (h s) -> p h s", h=H)
        kaT = shared[:, H * S:2 * H * S].rearrange("p (h s) -> p h s", h=H)
        mqT = shared[:, 2 * H * S:2 * H * S + H // 2 * S].rearrange("p (h s) -> p h s", h=H // 2)
        mkT = shared[:, 2 * H * S + H // 2 * S:].rearrange("p (h s) -> p h s", h=H // 2)
        s_sb = wup[:, 0:9 * P].rearrange("p (b n) -> p b n", b=3)
        pT_sb = wup[:, 9 * P:18 * P].rearrange("p (b n) -> p b n", b=3)
        p_sb = sq.rearrange("p b n -> p (b n)").rearrange("p (b n) -> p b n", b=4)
        mk_flat = mk[:, :, :].rearrange("p t n -> p (t n)")
        w_r = mk_flat[:, 0:KT * (NG + NE)].rearrange("p (k n) -> p k n", k=KT)
        gx = sb("gx", [P, KT])
        gf = sb("gf", [P, KT])
        go = sb("go", [P, KT])
        gql = sb("gql", [P, 2])
        gkvl = sb("gkvl", [P, 1])
        g_row = sb("g_row", [P, 2 * QK + 2 * DH])
        b_row = sb("b_row", [P, NG + NE])
        gap = ring[:, KT * D:EB * SLOT - KT * IN_W]
        tc_m = gap[:, 0:256].rearrange("p (n t d) -> p n t d", n=2, t=NT)
        ts_m = sb("ts_m", [P, 2, NT, DH])
        tc_a = gap[:, 256:640].rearrange("p (n t d) -> p n t d", n=2, t=NT)
        ts_a = gap[:, 640:768].rearrange("p (n t d) -> p n t d", n=2, t=NT)
        pe = sb("pe", [P, NT, 2, RD])
        eps = sb("eps", [P, 1])
        ones = sb("ones", [P, P])
        st = sb("st", [P, 160])
        mx = mk_flat[:, 288:320].rearrange("p (h t) -> p h t", t=2)
        nmx = mk_flat[:, 320:352].rearrange("p (h t) -> p h t", t=2)
        rsum = sb("rsum", [P, NT, 2 * H])
        rt = mq[:, :, :].rearrange("p t n -> p (t n)")
        m01 = mk_flat[:, 424:488].rearrange("p (t n) -> p t n", t=NT)
        key_w = sb("key_w", [P, 4, NT])
        qa_flat, ka_flat = qa[:, :, :].rearrange("p t n -> p (t n)"), ka[:, :, :].rearrange("p t n -> p (t n)")
        slot_row = qa_flat[:, 0:(NB + OVB) * P].rearrange("p (b n) -> p b n", n=P)
        slot_col = sb("slot_col", [P, NB + OVB])
        e_key = mk_flat[:, 488:520]
        e_num, g_num = mk_flat[:, 520:552], mk_flat[:, 552:584].rearrange("p (g e) -> p g e", g=NG)
        totals = mk_flat[:, 584:616]
        W = NE * OVC
        ov_thr, ov_key, ov_exp = [ka_flat[:, n * W:(n + 1) * W].rearrange("p (e c) -> p e c", c=OVC) for n in range(3)]
        ov_j = sb("ov_j", [P, 1])
        ov_pick = ka_flat[:, 3 * W:3 * W + OVB * P].rearrange("p (b n) -> p b n", n=P)
        ov4 = sb("ov4", [P, OVB])
        nb_i = sb("nb_i", [P, 1], I32)
        eid_i = sb("eid_i", [P, EB * OVB], I32)
        def scratch_of(lo, n):
            return rt[:, lo:lo + NT * n].rearrange("p (t n) -> p t n", t=NT)

        lg = scratch_of(832, 8 + NE)
        glog, elog = lg[:, :, 0:8], lg[:, :, 8:]
        top, masked, keys = scratch_of(16, 8), scratch_of(32, NE), scratch_of(96, NE)
        picked = rt[:, 256:256 + 4 * NE].rearrange("p (a e) -> p a e", a=4)
        gexp, enum = scratch_of(160, NG), scratch_of(168, 2)
        top_i = rt[:, 172:188].bitcast(mybir.dt.uint32).rearrange("p (t n) -> p t n", t=NT)
        gneg, eneg, gnum, gsum, eexp, wden = [rt[:, 188 + 2 * n:190 + 2 * n] for n in range(6)]
        junk = swp
        x_flat = x_sb[:, :, :].rearrange("p t n -> p (t n)")
        xg = x_flat[:, 0:KT * P].rearrange("p (k n) -> p k n", k=KT)
        key_bc = x_flat[:, KT * P:KT * P + 4 * S].rearrange("p (a t n) -> p a t n", a=4, t=NT)
        z0 = SLOT
        y_sb, u_sb, back = in_zone(D), in_zone(512), in_zone(S)
        hot = in_zone(NT * P).rearrange("p (t n) -> p t n", t=NT)
        back2 = in_zone(2 * S).rearrange("p (a n) -> p a n", a=2)
        sil, gT = in_zone(2 * C), in_zone(2 * C).rearrange("p (j n) -> p j n", j=2)
        assert z0 <= zone.shape[1]
        gate_spare = xn_flat.rearrange("p (k n) -> p k n", k=KT)
        ov = mk_flat[:, 616:616 + 3 * P]
        there, place = [rt[:, 384 + n * W:384 + (n + 1) * W] for n in range(2)]
        scratch = ka_flat[:, 3 * W + OVB * P:4 * W + OVB * P]

        B = [ctx.enter_context(nc.psum_tensor(f"bank{i}", [P, 512], F32)) for i in range(8)]

        names = """const_in rope_in lat_gains_in late_gains_in wup_in wout_in wr_in setup pool_const
            gx_in x_rt rx_ready xT_done actT_ready proj_done raw_ready lat_rt latn_ready latT_done latT_ready
            lift_done raw2_ready mv_ready sq_done red_done rt_done swap_done heads_ready headT_done headT_act headT_dve
            score_done max_ready exp_done pT_done pT_even pT_odd pv_done o_ready o_rt oT_done mixT_ready
            outp_done x1b_ready x1_ready x1_rt hT_done h2T_ready logit_done hn_ready lg_ready r_exp r_max rank_in rank_done totals_done acc_ready gate_in
            key_ready keybc_done keybc_ready hot_ready gath_done xg_ready up_done u_ready fold_done sil_ready g_ready
            down_done y_dve y_act back_ready scat_done weight_ready nb_ready ovk_ready ovt_done ov_ready y_out
            act_sq hot_half back_half y_stored dve_step act_step pool_step""".split()
        s = {n: sem(n) for n in names}
        x_in = [sem(f"x_in{t}") for t in range(NT)]
        win_in = [sem(f"win_in{k}") for k in range(KT)]
        gu_in = [sem(f"gu_in{i}") for i in range(EB)]
        dn_in = [sem(f"dn_in{i}") for i in range(EB)]
        gu_spare = [sem(f"gu_spare{j}") for j in range(2)]
        dn_spare = [sem(f"dn_spare{j}") for j in range(2)]

        st_x, st_l, st_h, st_o, st_f = st[:, 0:4], st[:, 4:16], st[:, 16:144], st[:, 144:152], st[:, 152:156]
        ms_x, r_x = st_x[:, 0:2], st_x[:, 2:4]
        ms_l, r_l = st_l[:, 0:4].rearrange("p (t g) -> p t g", g=2), st_l[:, 4:8].rearrange("p (t g) -> p t g", g=2)
        ms_pe = st_l[:, 8:10]
        ms_o, r_o = st_o[:, 0:4].rearrange("p (t g) -> p t g", g=2), st_o[:, 4:8].rearrange("p (t g) -> p t g", g=2)
        ms_f, r_f = st_f[:, 0:2], st_f[:, 2:4]

        def ms_h(u):
            return st_h[:, 16 * u:16 * u + 8]

        def r_h(u):
            return st_h[:, 16 * u + 8:16 * u + 16]

        UNITS = [("mq", 0), ("mq", 1), ("mk", 0), ("mk", 1), ("qa", 0), ("ka", 0), ("qa", 1), ("ka", 1)]
        RAW = {("mq", 0): 3, ("mq", 1): 4, ("mk", 0): 5, ("mk", 1): 6}
        RAW2 = {("qa", 0): 2, ("ka", 0): 4, ("qa", 1): 6, ("ka", 1): 8}

        def wait_raw(eng, unit):
            if unit in RAW:
                eng.wait_ge(s["raw_ready"], RAW[unit])
            else:
                eng.wait_ge(s["raw2_ready"], RAW2[unit])

        class Steps:

            def __init__(self, eng, name):
                self.eng, self.sem, self.n = eng, s[name], 0

            def __call__(self, ins):
                self.n += 1
                ins.then_inc(self.sem, 1)
                self.eng.wait_ge(self.sem, self.n)

        def load_expert(eng, i, e, parts=(0, 1)):
            base = i * SLOT
            n = KT * HID
            for j in parts:
                w = (a["w_gate"], a["w_up"])[j]
                eng.dma_start(ring[:, base + j * n:base + (j + 1) * n],
                              w[0, e].rearrange("(p k) n -> p (k n)", k=KT)).then_inc(gu_in[i], 16)

        def load_down(eng, i, e):
            base = i * SLOT + 2 * KT * HID
            eng.dma_start(ring[:, base:base + 2 * D].rearrange("p (j n) -> p j n", j=2),
                          a["w_down"][0, e].rearrange("(j p) n -> p j n", j=2)).then_inc(dn_in[i], 16)

        TURNS = [(u, 0) for u in range(4)] + [(u, n) for n in range(2) for u in range(4, 8)]

        def turn_of(n):
            u, half = TURNS[n]
            kind, t = UNITS[u]
            full = {"mq": mqT, "mk": mkT, "qa": qaT, "ka": kaT}[kind]
            w = P if kind[0] == "m" else QK
            return u, half, full[0:w, 4 * half:4 * half + 4, t * P:(t + 1) * P], (6, 2, 7, 3)[n] if n < 4 else 7

        def head_turned(eng, n):
            _, _, dst, bank = turn_of(n)
            eng.wait_ge(s["headT_done"], n + 1)
            copy = eng.tensor_copy if n % 2 else eng.copy
            copy(dst, B[bank][0:dst.shape[0], :].rearrange("p (h s) -> p h s", h=4)).then_inc(s[("headT_act", "headT_dve")[n % 2]], 1)

        def head_pT(eng, h):
            eng.wait_ge(s["pT_done"], h + 1)
            if h >= 3:
                eng.wait_ge(s["pv_done"], h - 2)
            copy = eng.copy if h % 2 else eng.tensor_copy
            copy(pT_sb[:, h % 3, :], B[2 + h % 2][:, 0:3 * P]).then_inc(s[("pT_even", "pT_odd")[h % 2]], 1)

        block = ctx.enter_context(nc.Block())

        @block.sync
        def _(sp):
            sp.dma_start(x_sb[:, 0, :], a["x"][0, 0:P, :]).then_inc(x_in[0], 16)
            sp.dma_start(const[:, :], a["consts"]).then_inc(s["const_in"], 16)
            sp.dma_start(x_sb[:, 1, :], a["x"][0, P:2 * P, :]).then_inc(x_in[1], 16)
            sp.dma_start(gx[:, :], a["attn_norm_g"][0].rearrange("(p k) -> p k", k=KT)).then_inc(s["gx_in"], 16)
            between = {1: [(rope[:, :, :], a["rope"].rearrange("(t p) n -> p t n", p=P), "rope_in"),
                           (g_row[:, 2 * QK:2 * QK + DH], a["moba_q_head_g"].to_broadcast([P, DH]), "rope_in"),
                           (g_row[:, 2 * QK + DH:], a["moba_k_head_g"].to_broadcast([P, DH]), "rope_in")],
                       3: [(g_row[:, 0:QK], a["mla_q_head_g"].to_broadcast([P, QK]), "rope_in"),
                           (g_row[:, QK:2 * QK], a["mla_k_head_g"].to_broadcast([P, QK]), "rope_in")],
                       5: [(gql[:, :], a["mla_q_lat_g"][0].rearrange("(p k) -> p k", k=2), "lat_gains_in"),
                           (gkvl[:, :], a["mla_kv_lat_g"][0].rearrange("(p k) -> p k", k=1), "lat_gains_in")]}
            w = a["w_in"][0].rearrange("(p k) n -> p k n", k=KT)
            for k in range(KT):
                sp.dma_start(w_in[:, k, :], w[:, k, :]).then_inc(win_in[k], 16)
                for dst, src, signal in between.get(k, ()):
                    sp.dma_start(dst, src).then_inc(s[signal], 16)
            sp.dma_start(wup[:, 0:2 * H * QK], a["w_q_up"][0].rearrange("(p k) n -> p (k n)", k=2)).then_inc(s["wup_in"], 16)
            sp.dma_start(w_kvup, a["w_kv_up"][0]).then_inc(s["wup_in"], 16)
            for g in range(2):
                sp.dma_start(w_out[:, 4 * g:4 * g + 4, :], a["w_out"][0, 512 * g:512 * g + 512, :].rearrange("(p k) n -> p k n", k=4)).then_inc(s["wout_in"], 16)
            for dst, src in ((go[:, 0:4], a["out_norm_mla_g"][0].rearrange("(p k) -> p k", k=4)),
                             (go[:, 4:8], a["out_norm_moba_g"][0].rearrange("(p k) -> p k", k=4)),
                             (gf[:, :], a["ffn_norm_g"][0].rearrange("(p k) -> p k", k=KT)),
                             (b_row[:, 0:NG], a["b_router_group"].to_broadcast([P, NG])),
                             (b_row[:, NG:], a["b_router_expert"].to_broadcast([P, NE]))):
                sp.dma_start(dst, src).then_inc(s["late_gains_in"], 16)
            sp.wait_ge(s["proj_done"], 8)
            for i in (2, 3):
                load_expert(sp, i, i - 2)
                load_down(sp, i, i - 2)
            sp.wait_ge(s["headT_done"], 4)
            for dst, src in ((w_r[:, :, 0:NG], a["w_router_group"]), (w_r[:, :, NG:], a["w_router_expert"])):
                sp.dma_start(dst, src[0].rearrange("(p k) n -> p k n", k=KT)).then_inc(s["wr_in"], 16)
            sp.wait_ge(s["pv_done"], 2 * H)
            for x in range(2):
                for j, w in enumerate((a["w_gate"], a["w_up"])):
                    sp.dma_start(spares[x][:, j * KT * HID:(j + 1) * KT * HID], w[0, EB + x].rearrange("(p k) n -> p (k n)", k=KT)).then_inc(gu_spare[x], 16)
                sp.dma_start(spare_down[x], a["w_down"][0, EB + x].rearrange("(j p) n -> p j n", j=2)).then_inc(dn_spare[x], 16)
            assert 4 * D == 2 * KT * HID and KT * D == SLOT + KT * HID
            sp.wait_ge(s["outp_done"], 4)
            load_down(sp, 0, 2)
            load_expert(sp, 1, 3, (0,))
            sp.wait_ge(s["outp_done"], 8)
            load_expert(sp, 0, 2)
            load_expert(sp, 1, 3, (1,))
            load_down(sp, 1, 3)

            sp.wait_ge(s["acc_ready"], 2 * NT)
            sp.wait_ge(s["hn_ready"], 2)
            sp.dma_start(xn_flat, a["w_gate"][0, EB + 2].rearrange("(p k) n -> p (k n)", k=KT)).then_inc(s["gate_in"], 16)

            def reload(i, last, e):
                sp.wait_ge(s["up_done"], last + 1)
                load_expert(sp, i, e)
                sp.wait_ge(s["down_done"], last + 1)
                load_down(sp, i, e)

            sp.wait_ge(s["up_done"], 1)
            load_expert(sp, 2, EB + 2, (1,))
            sp.wait_ge(s["up_done"], 2)
            load_expert(sp, 3, EB + 3)
            sp.wait_ge(s["down_done"], 2)
            load_down(sp, 2, EB + 2)
            load_down(sp, 3, EB + 3)
            for i in (0, 1):
                reload(i, 2 + i, 2 * EB + i)
            with sp.Fori(2, NB - 1) as b:
                for i in (2, 3):
                    reload(i, EB * b - EB + i, EB * b + i)
                for i in (0, 1):
                    reload(i, EB * b + i, EB * b + EB + i)
            for i in (2, 3):
                reload(i, EB * (NB - 2) + i, EB * (NB - 1) + i)
            sp.wait_ge(s["nb_ready"], 1)
            n_ov = sp.value_load(nb_i[0:1, 0:1], min_val=0, max_val=OVB)
            with sp.If(n_ov > 0):
                sp.wait_ge(s["ov_ready"], 1)
                with sp.Fori(0, n_ov) as v:
                    for i in range(EB):
                        e = sp.value_load(eid_i[0:1, bass.ds(EB * v + i, 1)], min_val=0, max_val=NE - 1)
                        sp.wait_ge(s["up_done"], EB * v + EB * NB - EB + i + 1)
                        for j, w in enumerate((a["w_gate"], a["w_up"])):
                            sp.dma_start(ring[:, i * SLOT + j * KT * HID:i * SLOT + (j + 1) * KT * HID],
                                         w[0].rearrange("e (p k) n -> p e (k n)", k=KT)[:, bass.ds(e, 1), :]).then_inc(gu_in[i], 16)
                        sp.wait_ge(s["down_done"], EB * v + EB * NB - EB + i + 1)
                        sp.dma_start(down_w[i], a["w_down"][0].rearrange("e (j p) n -> p (e j) n", j=2)[:, bass.ds(2 * e, 2), :]).then_inc(dn_in[i], 16)
            for t in range(NT):
                for hf in range(2):
                    sp.wait_ge(s["y_out"], 2 * t + hf + 1)
                    sp.dma_start(out[0, t * P:(t + 1) * P, 512 * hf:512 * hf + 512], staged[:, t, 512 * hf:512 * hf + 512]).then_inc(s["y_stored"], 16)
            sp.wait_ge(s["y_stored"], 16 * 4)

        @block.gpsimd
        def _(pool):
            step = Steps(pool, "pool_step")
            pool.wait_ge(s["rope_in"], 16 * 5)
            gq, gk = g_row[:, 0:QK], g_row[:, QK:2 * QK]
            for n, g in enumerate((g_row[:, 2 * QK:2 * QK + DH], g_row[:, 2 * QK + DH:])):
                for t in range(NT):
                    pool.tensor_tensor(tc_m[:, n, t, :], rope[:, t, 0:DH], g, ALU.mult)
                    for h0, h1 in ((0, DH // 2), (DH // 2, 0)):
                        pool.tensor_tensor(ts_m[:, n, t, h0:h0 + DH // 2], rope[:, t, DH + h0:DH + h0 + DH // 2],
                                           g[:, h1:h1 + DH // 2], ALU.mult)
            for n, g in enumerate((gq, gk)):
                for t in range(NT):
                    pool.tensor_copy(tc_a[:, n, t, 0:NOPE], g[:, 0:NOPE])
                    pool.tensor_tensor(tc_a[:, n, t, NOPE:QK], rope[:, t, 2 * DH:2 * DH + RD], g[:, NOPE:QK], ALU.mult)
                    for h0, h1 in ((0, RD // 2), (RD // 2, 0)):
                        ins = pool.tensor_tensor(ts_a[:, n, t, h0:h0 + RD // 2],
                                                 rope[:, t, 2 * DH + RD + h0:2 * DH + RD + h0 + RD // 2],
                                                 g[:, NOPE + h1:NOPE + h1 + RD // 2], ALU.mult)
            step(ins)
            for u, (kind, t) in enumerate(UNITS):
                wait_raw(pool, (kind, t))
                if u >= 2:
                    pool.wait_ge(s["heads_ready"], u - 1)
                if kind in ("mq", "mk"):
                    n = int(kind == "mk")
                    x = (mq, mk)[n][:, t, :].rearrange("p (h d) -> p h d", h=H)
                    sw = swp[:, u % 2, :].rearrange("p (h d) -> p h d", h=H)
                    for h0, h1 in ((0, DH // 2), (DH // 2, 0)):
                        ins = pool.tensor_tensor(sw[:, :, h0:h0 + DH // 2], x[:, :, h1:h1 + DH // 2],
                                                 ts_m[:, n, t, h0:h0 + DH // 2].unsqueeze(1).to_broadcast([P, H, DH // 2]), ALU.mult)
                    step(ins)
                    pool.wait_ge(s["sq_done"], u + 1)
                    pool.tensor_tensor(x, x, tc_m[:, n, t, :].unsqueeze(1).to_broadcast([P, H, DH]), ALU.mult).then_inc(s["swap_done"], 1)
                elif kind == "qa":
                    x = qa[:, t, :].rearrange("p (h d) -> p h d", h=H)
                    sw = swp[:, u % 2, 0:H * RD].rearrange("p (h d) -> p h d", h=H)
                    for h0, h1 in ((0, RD // 2), (RD // 2, 0)):
                        ins = pool.tensor_tensor(sw[:, :, h0:h0 + RD // 2], x[:, :, NOPE + h1:NOPE + h1 + RD // 2],
                                                 ts_a[:, 0, t, h0:h0 + RD // 2].unsqueeze(1).to_broadcast([P, H, RD // 2]), ALU.mult)
                    step(ins)
                    pool.wait_ge(s["sq_done"], u + 1)
                    pool.tensor_tensor(x, x, tc_a[:, 0, t, :].unsqueeze(1).to_broadcast([P, H, QK]), ALU.mult).then_inc(s["swap_done"], 1)
                else:
                    for h0, h1 in ((0, RD // 2), (RD // 2, 0)):
                        pool.tensor_tensor(pe[:, t, 1, h0:h0 + RD // 2], lat[:, t, QL + KVL + h1:QL + KVL + h1 + RD // 2],
                                           ts_a[:, 1, t, h0:h0 + RD // 2], ALU.mult)
                    step(pool.tensor_tensor(pe[:, t, 0, :], lat[:, t, QL + KVL:C0], tc_a[:, 1, t, NOPE:QK], ALU.mult))
                    pool.tensor_tensor(pe[:, t, 0, :], pe[:, t, 0, :], pe[:, t, 1, :], ALU.add)
                    pool.tensor_tensor(ka[:, t, :].rearrange("p (h d) -> p h d", h=H)[:, :, 0:NOPE],
                                       kva[:, t, :].rearrange("p (h d) -> p h d", h=H)[:, :, 0:NOPE],
                                       tc_a[:, 1, t, 0:NOPE].unsqueeze(1).to_broadcast([P, H, NOPE]), ALU.mult).then_inc(s["swap_done"], 1)

            pool.wait_ge(s["headT_done"], len(TURNS))
            pool.iota(slot_row[:, 0:NB, :].rearrange("p b (i c) -> p (b i) c", c=C), [[KEY, NE], [1, C]], base=0,
                      channel_multiplier=0, allow_small_or_imprecise_dtypes=True)
            step(pool.memset(slot_row[:, NB:, :], -OFF))
            for i in range(EB):
                step(pool.iota(slot_col[C * i:C * i + C, 0:NB], [[EB * KEY, NB]], base=i * KEY,
                               channel_multiplier=1, allow_small_or_imprecise_dtypes=True))
            pool.iota(e_key[:, :], [[KEY, NE]], base=0, channel_multiplier=0, allow_small_or_imprecise_dtypes=True)
            pool.iota(e_num, [[1, NE]], base=0, channel_multiplier=0, allow_small_or_imprecise_dtypes=True)
            pool.iota(g_num, [[1, NG], [0, EPG]], base=0, channel_multiplier=0, allow_small_or_imprecise_dtypes=True)
            pool.iota(ov_thr[:, :, :], [[0, NE], [C, OVC]], base=C, channel_multiplier=0, allow_small_or_imprecise_dtypes=True)
            pool.iota(ov_key[:, :, :], [[KEY, NE], [C, OVC]], base=C + int(OFF), channel_multiplier=0, allow_small_or_imprecise_dtypes=True)
            pool.iota(ov_exp[:, :, :], [[1, NE], [0, OVC]], base=0, channel_multiplier=0, allow_small_or_imprecise_dtypes=True)
            pool.iota(ov_j[:, :], [[1, 1]], base=1, channel_multiplier=1, allow_small_or_imprecise_dtypes=True)
            pool.iota(ov4[:, :], [[EB, OVB]], base=0, channel_multiplier=0, allow_small_or_imprecise_dtypes=True)
            step(pool.memset(ov_pick[:, :, :], 0.0))
            for i in range(EB):
                ap = ov_pick[:, :, C * i:C * i + C]
                ins = pool.affine_select(out=ap, in_=ap, compare_op=ALU.not_equal, fill=1.0, base=-i,
                                         pattern=[[-EB, OVB], [0, C]], channel_multiplier=1)
            ins.then_inc(s["pool_const"], 1)
        @block.scalar
        def _(act):
            step = Steps(act, "act_step")
            act.wait_ge(s["setup"], 1)
            step(act.activation(st[:, 156:157], eps[:, 0:1], ACT.Sqrt))
            for t in range(NT):
                act.wait_ge(x_in[t], 16)
                ins = act.activation(xn[:, t, :, :].rearrange("p k n -> p (k n)"), x_sb[:, t, :], ACT.Square,
                                     scale=D ** -0.5, accum_out=ms_x[:, t:t + 1])
                step(ins)
            act.activation(ms_x, ms_x, ACT.Sqrt, bias=eps[:, 0:1]).then_inc(s["x_rt"], 1)
            act.wait_ge(s["rx_ready"], 1)

            def projected(dst, bank, t):
                return act.activation(dst, bank, ACT.Copy, scale=r_x[:, t:t + 1])

            for t in range(NT):
                act.wait_ge(s["proj_done"], t + 1)
                projected(lat[:, t, :], B[4 + t][:, 0:C0], t).then_inc(s["raw_ready"], 1)
                act.wait_ge(s["raw_ready"], t + 1)
                act.activation(sq[:, t, 0:QL], lat[:, t, 0:QL], ACT.Square, scale=QL ** -0.5, accum_out=ms_l[:, t, 0:1])
                act.activation(sq[:, t, QL:QL + KVL], lat[:, t, QL:QL + KVL], ACT.Square, scale=KVL ** -0.5, accum_out=ms_l[:, t, 1:2])
                step(act.activation(sq[:, t, QL + KVL:C0], lat[:, t, QL + KVL:C0], ACT.Square, scale=QK ** -0.5,
                                    accum_out=ms_pe[:, t:t + 1]))
            act.activation(st_l[:, 0:4], st_l[:, 0:4], ACT.Sqrt, bias=eps[:, 0:1]).then_inc(s["lat_rt"], 1)
            for t in range(NT):
                act.wait_ge(s["proj_done"], 3 + t)
                projected(mq[:, t, :], B[6 + t][:, :], t).then_inc(s["raw_ready"], 1)

            def square(u):
                kind, t = UNITS[u]
                if u >= 2:
                    act.wait_ge(s["red_done"], u - 1)
                d = DH if kind[0] == "m" else QK
                x = {"mq": mq, "mk": mk, "qa": qa, "ka": kva}[kind][:, t, :].rearrange("p (h d) -> p h d", h=H)
                w = NOPE if kind == "ka" else d
                wait_raw(act, (kind, t))
                act.activation(sq[:, u % 2, 0:H * w].rearrange("p (h d) -> p h d", h=H), x[:, :, 0:w], ACT.Square,
                               scale=d ** -0.5).then_inc(s["sq_done"], 1)

            def root(u):
                act.wait_ge(s["red_done"], u + 1)
                act.activation(ms_h(u), ms_h(u), ACT.Sqrt, bias=eps[:, 0:1]).then_inc(s["rt_done"], 1)

            square(0)
            square(1)
            root(0)
            root(1)
            for t in range(NT):
                act.wait_ge(s["proj_done"], 5 + t)
                projected(mk[:, t, :], B[t][:, :], t).then_inc(s["raw_ready"], 1)
                square(2 + t)
                root(2 + t)
            lifted = [(qa, 4), (qa, 5), (kva, 2), (kva, 3), (qa, 6), (qa, 7), (kva, 0), (kva, 1)]
            for n, (dst, bank) in enumerate(lifted):
                act.wait_ge(s["lift_done"], n + 1)
                t, hf = n // 4, n % 2
                w = H * QK // 2 if dst is qa else 512
                act.copy(dst[:, t, hf * w:hf * w + w], B[bank][:, 0:w]).then_inc(s["raw2_ready"], 1)
                if n == 3:
                    square(4)
                    square(5)
            head_turned(act, 0)
            root(4)
            head_turned(act, 2)
            root(5)
            square(6)
            square(7)
            root(6)
            root(7)
            step(act.activation(st[:, 156:157], eps[:, 0:1], ACT.Exp))
            def moba_v(t):
                act.wait_ge(s["proj_done"], 7 + t)
                projected(mv[:, t, :], B[4 + t][:, :], t).then_inc(s["mv_ready"], 1)

            def group_squares(g):
                for t in range(NT):
                    act.wait_ge(s["o_ready"], (3 + t, 1 + t)[g])
                    act.activation(junk[:, t, :], xn[:, t, 4 * g:4 * g + 4, :].rearrange("p k n -> p (k n)"),
                                   ACT.Square, scale=512 ** -0.5, accum_out=ms_o[:, t, g:g + 1]).then_inc(s["act_sq"], 1)

            moba_v(0)
            head_turned(act, 4)
            for i in range(2 * H + 3):
                if i < 2 * H:
                    scale = (DH if i < H else QK) ** -0.5
                    act.wait_ge(s["max_ready"], i + 1)
                    if i >= 4:
                        act.wait_ge(s["pT_done"], i - 3)
                    for t in range(NT):
                        ins = act.activation(p_sb[:, i % 4, t * P:(2 * t + 1) * P], s_sb[:, i % 3, t * P:(2 * t + 1) * P],
                                             ACT.Exp, bias=nmx[:, i, t:t + 1], scale=scale, accum_out=rsum[:, t, i:i + 1])
                    ins.then_inc(s["exp_done"], 1)
                if i == 4:
                    moba_v(1)
                if 0 < i < 8 and i % 2 == 0:
                    head_turned(act, 4 + i)
                if i >= 3 and (i - 3) % 2:
                    head_pT(act, i - 3)
                if i == H + 6:
                    group_squares(1)
            step(act.activation(st[:, 156:157], eps[:, 0:1], ACT.Sqrt))
            group_squares(0)
            act.wait_ge(s["act_sq"], 4)
            act.activation(st_o[:, 0:4], st_o[:, 0:4], ACT.Sqrt, bias=eps[:, 0:1]).then_inc(s["o_rt"], 1)
            for t in range(NT):
                act.wait_ge(s["x1_ready"], 2 * t + 2)
                ins = act.activation(x_sb[:, t, :], xn[:, t, :, :].rearrange("p k n -> p (k n)"), ACT.Square, scale=D ** -0.5,
                                     accum_out=ms_f[:, t:t + 1])
                step(ins)
                act.activation(ms_f[:, t:t + 1], ms_f[:, t:t + 1], ACT.Sqrt, bias=eps[:, 0:1]).then_inc(s["x1_rt"], 1)
            step(act.activation(st[:, 156:157], eps[:, 0:1], ACT.Exp))
            act.wait_ge(s["logit_done"], 2)
            act.wait_ge(s["lg_ready"], 1)
            for t in range(NT):
                act.activation(hn[:, t, :, :].rearrange("p k n -> p (k n)"), xn[:, t, :, :].rearrange("p k n -> p (k n)"),
                               ACT.Copy, scale=r_f[:, t:t + 1]).then_inc(s["hn_ready"], 1)
            act.wait_ge(s["r_max"], 1)
            for t in range(NT):
                act.activation(gexp[:, t, :], glog[:, t, 0:NG], ACT.Exp, bias=gneg[:, t:t + 1], accum_out=gsum[:, t:t + 1])
            act.wait_ge(s["r_max"], 2)
            for t in range(NT):
                ins = act.activation(eexp[:, t:t + 1], top[:, t, 1:2], ACT.Exp, bias=eneg[:, t:t + 1])
            ins.then_inc(s["r_exp"], 1)
            step(act.activation(st[:, 156:157], eps[:, 0:1], ACT.Silu))

            def key_rows(n):
                act.wait_ge(s["keybc_done"], n + 1)
                act.copy(key_bc[:, 2 * n:2 * n + 2, :, :].rearrange("p a t n -> p (a t n)"), B[(7, 4)[n]][:, :]).then_inc(s["keybc_ready"], 1)

            def outputs_down(b, i, first):
                act.wait_ge(s["down_done"], EB * b + i + 1)
                if i == 0 and not first:
                    act.wait_ge(s["scat_done"], 4 * b)
                for q in (2, 3):
                    ins = act.copy(y_sb[C * i:C * i + C, 256 * q:256 * q + 256], B[7][C * q:C * q + C, 0:256])
                ins.then_inc(s["y_act"], 1)

            def batch(b, first=False, ahead=True):
                for i in range(EB):
                    act.wait_ge(s["up_done"], EB * b + i + 1)
                    if not (first and i == 0):
                        act.wait_ge(s["fold_done"], EB * b + i)
                    act.copy(u_sb, B[5][:, :]).then_inc(s["u_ready"], 1)
                    if first and i < 2:
                        key_rows(i)
                    if i > 0 and ahead:
                        outputs_down(b, i - 1, first)
                    act.wait_ge(s["fold_done"], EB * b + i + 1)
                    if not (first and i == 0):
                        act.wait_ge(s["g_ready"], EB * b + i)
                    act.activation(sil, B[6][:, 0:2 * C], ACT.Silu).then_inc(s["sil_ready"], 1)
                    if not ahead:
                        outputs_down(b, i, first)
                if ahead:
                    outputs_down(b, EB - 1, first)

            batch(0, first=True)
            with act.Fori(1, NB - 1) as b:
                batch(b)
            batch(NB - 1, ahead=False)
            act.wait_ge(s["nb_ready"], 1)
            n_ov = act.value_load(nb_i[0:1, 0:1], min_val=0, max_val=OVB)
            with act.If(n_ov > 0):
                with act.Fori(0, n_ov) as v:
                    batch(v + NB, ahead=False)

        @block.tensor
        def _(pe_):
            def keep_busy(n, bank):
                for _ in range(n):
                    pe_.matmul(B[bank][:, 0:P], ones[:, :], ones[:, :], start=True, stop=True)

            pe_.wait_ge(s["setup"], 1)
            keep_busy(9, 7)
            pe_.wait_ge(s["const_in"], 16)
            for t in range(NT):
                pe_.wait_ge(x_in[t], 16)
                for hf in range(2):
                    for k in range(4):
                        ins = pe_.transpose(B[2 * t + hf][:, k * P:(k + 1) * P],
                                            x_sb[:, t, :].rearrange("p (n k) -> p k n", k=KT)[:, 4 * hf + k, :], ident)
                    ins.then_inc(s["xT_done"], 1)
            pe_.wait_ge(s["actT_ready"], 4)
            col = [0, C0, C0 + 512, C0 + 1024, IN_W]
            for k in range(KT):
                pe_.wait_ge(win_in[k], 16)
                for c in range(2):
                    for t in range(NT):
                        ins = pe_.matmul(B[4 + 2 * c + t][:, 0:col[c + 1] - col[c]], actT[:, k, t * P:(t + 1) * P],
                                         w_in[:, k, col[c]:col[c + 1]], start=(k == 0), stop=(k == KT - 1))
                        if k == KT - 1:
                            ins.then_inc(s["proj_done"], 1)

            def project(c, t, bank, k0=0, k1=KT):
                for k in range(k0, k1):
                    ins = pe_.matmul(B[bank][:, :], actT[:, k, t * P:(t + 1) * P], w_in[:, k, col[c]:col[c + 1]],
                                     start=(k == 0), stop=(k == KT - 1))
                if k1 == KT:
                    ins.then_inc(s["proj_done"], 1)

            project(2, 0, 0)
            pe_.wait_ge(s["latn_ready"], 1)
            for k in range(2):
                for t in range(NT):
                    ins = pe_.transpose(B[2][:, k * S + t * P:k * S + (t + 1) * P], latn[:, t, k, :], ident)
            ins.then_inc(s["latT_done"], 1)
            for t in range(NT):
                ins = pe_.transpose(B[3][:, t * P:(t + 1) * P], latn[:, t, 2, :], ident)
            ins.then_inc(s["latT_done"], 1)
            project(2, 1, 1)
            pe_.wait_ge(s["latT_ready"], 2)
            pe_.wait_ge(s["wup_in"], 32)
            for t in range(NT):
                pe_.wait_ge(s["raw_ready"], (2, 4)[t])
                for hf in range(2):
                    for k in range(2):
                        ins = pe_.matmul(B[4 + 2 * t + hf][:, 0:384], latT[:, k, t * P:(t + 1) * P],
                                         w_qup[:, k, 384 * hf:384 * hf + 384], start=(k == 0), stop=(k == 1))
                    ins.then_inc(s["lift_done"], 1)
                if t:
                    pe_.wait_ge(s["raw_ready"], 6)
                for hf in range(2):
                    pe_.matmul(B[(2, 0)[t] + hf][:, :], latT[:, 2, t * P:(t + 1) * P], w_kvup[:, 512 * hf:512 * hf + 512],
                               start=True, stop=True).then_inc(s["lift_done"], 1)
            pe_.wait_ge(s["raw2_ready"], 1)
            def head_turn(n):
                u, half, dst, bank = turn_of(n)
                kind, t = UNITS[u]
                pe_.wait_ge(s["heads_ready"], u + 1)
                if n == 0:
                    pe_.wait_ge(s["raw2_ready"], 8)
                if n >= 5:
                    pe_.wait_ge(s[("headT_dve", "headT_act")[n % 2]], (n + 1) // 2)
                if n == 4:
                    pe_.wait_ge(s["headT_act"], 2)
                src = {"mq": mq, "mk": mk, "qa": qa, "ka": ka}[kind][:, t, :].rearrange("p (h d) -> p h d", d=dst.shape[0])
                for j in range(4):
                    ins = pe_.transpose(B[bank][0:dst.shape[0], j * P:(j + 1) * P], src[:, 4 * half + j, :], ident)
                ins.then_inc(s["headT_done"], 1)

            project(3, 0, 4, 0, 1)
            for n in range(4):
                head_turn(n)
            project(3, 0, 4, 1, 5)
            pe_.wait_ge(s["headT_act"], 2)
            pe_.wait_ge(s["headT_dve"], 2)
            score_bank = (0, 1, 6)
            V_SLICES = ((0, 4, 5, KT), (1, 5, 0, 2), (1, 5, 2, 4), (1, 5, 4, 6), (1, 5, 6, KT))

            def scores(h):
                if h >= 3:
                    pe_.wait_ge(s["max_ready"], h - 2)
                if h in (H, H + 4):
                    pe_.wait_ge(s["headT_act"], 4 + 2 * (h - H) // 4)
                    pe_.wait_ge(s["headT_dve"], 4 + 2 * (h - H) // 4)
                if h < H:
                    p0 = 64 * (h % 2)
                    q, k = mqT[p0:p0 + DH, h // 2, :], mkT[p0:p0 + DH, h // 2, :]
                else:
                    q, k = qaT[0:QK, h - H, :], kaT[0:QK, h - H, :]
                for t in range(NT):
                    ins = pe_.matmul(B[score_bank[h % 3]][:, t * P:(2 * t + 1) * P], q[:, t * P:(t + 1) * P], k[:, 0:(t + 1) * P], start=True, stop=True)
                ins.then_inc(s["score_done"], 1)

            def turn(h):
                pe_.wait_ge(s["exp_done"], h + 1)
                if h >= 2:
                    pe_.wait_ge(s[("pT_even", "pT_odd")[h % 2]], h // 2)
                for j in range(3):
                    ins = pe_.transpose(B[2 + h % 2][:, j * P:(j + 1) * P], p_sb[:, h % 4, j * P:(j + 1) * P], ident)
                ins.then_inc(s["pT_done"], 1)

            def values(h):
                pe_.wait_ge(s[("pT_even", "pT_odd")[h % 2]], h // 2 + 1)
                g, hh = h // H, h % H
                v = [mv[:, t, DH * hh:DH * hh + DH] if g == 0 else kva[:, t, P * hh + NOPE:P * hh + P] for t in range(NT)]
                if h == H:
                    pe_.wait_ge(s["o_ready"], 1)
                o = [B[((4, 5), (7, 4))[g][t]][:, DH * hh:DH * hh + DH] for t in range(NT)]
                pe_.matmul(o[0], pT_sb[:, h % 3, 0:P], v[0], start=True, stop=True)
                pe_.matmul(o[1], pT_sb[:, h % 3, P:2 * P], v[0], start=True, stop=False)
                pe_.matmul(o[1], pT_sb[:, h % 3, 2 * P:3 * P], v[1], start=False, stop=True).then_inc(s["pv_done"], 1)

            def output_turn(n, bank):
                g, t = 1 - n // 2, n % 2
                for k in range(4):
                    ins = pe_.transpose(B[bank][:, k * P:(k + 1) * P], xn[:, t, 4 * g + k, :], ident)
                ins.then_inc(s["oT_done"], 1)

            for i in range(2 * H + 5):
                if i < 2 * H:
                    scores(i)
                if 3 <= i < 2 * H + 3:
                    turn(i - 3)
                if i == 5:
                    pe_.wait_ge(s["mv_ready"], 2)
                if i >= 5:
                    values(i - 5)
                if i < len(V_SLICES):
                    project(3, *V_SLICES[i])
                if i < 8:
                    head_turn(4 + i)
                if i == H + 6:
                    pe_.wait_ge(s["o_ready"], 2)
                    output_turn(0, 5)
                if i == H + 8:
                    pe_.wait_ge(s["mixT_ready"], 1)
                    output_turn(1, 5)
            pe_.wait_ge(s["wout_in"], 32)

            def project_out(g, t, banks, halves=(0, 1)):
                for hf in halves:
                    for k in range(4 * g, 4 * g + 4):
                        ins = pe_.matmul(B[banks[hf]][:, :], actT[:, k, t * P:(t + 1) * P], w_out[:, k, 512 * hf:512 * hf + 512],
                                         start=(k == 4 * g), stop=(k == 4 * g + 3))
                    ins.then_inc(s["outp_done"], 1)

            pe_.wait_ge(s["mixT_ready"], 1)
            project_out(1, 0, (0, 1))
            pe_.wait_ge(s["mixT_ready"], 2)
            project_out(1, 1, (6, 5), (0,))
            pe_.wait_ge(s["pT_even"], H)
            pe_.wait_ge(s["pT_odd"], H)
            for t in range(NT):
                pe_.wait_ge(s["o_ready"], 3 + t)
                output_turn(2 + t, 2 + t)
            project_out(1, 1, (6, 5), (1,))
            pe_.wait_ge(s["mixT_ready"], 3)
            pe_.wait_ge(s["o_ready"], 4)
            project_out(0, 0, (7, 4))
            pe_.wait_ge(s["mixT_ready"], 4)
            project_out(0, 1, (2, 3))
            for t in range(NT):
                pe_.wait_ge(s["x1_ready"], 2 * t + 2)
                for hf in range(2):
                    for k in range(4):
                        ins = pe_.transpose(B[((0, 1), (6, 5))[t][hf]][:, k * P:(k + 1) * P], xn[:, t, 4 * hf + k, :], ident)
                    ins.then_inc(s["hT_done"], 1)
            pe_.wait_ge(s["wr_in"], 32)
            for t in range(NT):
                pe_.wait_ge(s["h2T_ready"], 2 * t + 2)
                for k in range(KT):
                    ins = pe_.matmul(B[(7, 4)[t]][:, 0:NG + NE], actT[:, k, t * P:(t + 1) * P], w_r[:, k, :], start=(k == 0), stop=(k == KT - 1))
                ins.then_inc(s["logit_done"], 1)
            tri = const[:, CR:CR + P]
            acc = [[B[2 * t + hf] for hf in range(2)] for t in range(NT)]

            def start_output(t, hf):
                pe_.matmul(acc[t][hf][:, :].rearrange("p (n k) -> p n k", k=KT), ident,
                           xn[:, t, :, 64 * hf:64 * hf + 64].rearrange("p k n -> p n k"), start=True, stop=False,
                           skip_group_check=True).then_inc(s["acc_ready"], 1)

            start_output(0, 0)
            start_output(0, 1)
            start_output(1, 0)
            keep_busy(5, 5)
            pe_.wait_ge(s["rank_in"], 1)
            pe_.matmul(B[6][:, 0:NE], tri, m01[:, 0, :], start=True, stop=True)
            pe_.matmul(B[6][:, NE:2 * NE], ones[:, :], m01[:, 0, :], start=True, stop=False)
            pe_.matmul(B[6][:, NE:2 * NE], tri, m01[:, 1, :], start=False, stop=True).then_inc(s["rank_done"], 1)
            pe_.matmul(B[5][:, 0:NE], ones[:, :], m01[:, 0, :], start=True, stop=False)
            pe_.matmul(B[5][:, 0:NE], ones[:, :], m01[:, 1, :], start=False, stop=True).then_inc(s["totals_done"], 1)

            start_output(1, 1)
            keep_busy(5, 4)

            def gather(part):
                for k in range(4):
                    for t in range(NT):
                        ins = pe_.matmul(B[5 - part][:, k * P:(k + 1) * P], hn[:, t, 4 * part + k, :], hot[:, t, :],
                                         start=(t == 0), stop=(t == NT - 1))
                ins.then_inc(s["gath_done"], 1)

            pe_.wait_ge(s["hot_ready"], 1)
            pe_.wait_ge(s["hn_ready"], 2)
            gather(0)
            gather(1)

            def key_rows(n):
                pe_.wait_ge(s[("key_ready", "weight_ready")[n]], 1)
                for m in range(2):
                    for t in range(NT):
                        ins = pe_.matmul(B[(7, 4)[n]][:, (2 * m + t) * P:(2 * m + t + 1) * P],
                                         key_w[:, 2 * n + m, t:t + 1].to_broadcast([P, P]), ident, start=True, stop=True)
                ins.then_inc(s["keybc_done"], 1)

            def up(b, i, first, spare, gate_apart=False):
                if first:
                    weights, place_in, value = gate_up[(i + 2) % EB], gu_in[(i + 2) % EB], 32
                elif spare:
                    weights, place_in, value = spare_gate_up[i], gu_spare[i], 32
                else:
                    weights, place_in, value = gate_up[i], gu_in[i], 32 * b + (0, 0, 16, 32)[i]
                pe_.wait_ge(place_in, value)
                if i == 0:
                    pe_.wait_ge(s["xg_ready"], 2 * b + 1)
                else:
                    pe_.wait_ge(s["u_ready"], EB * b + i)
                if gate_apart:
                    pe_.wait_ge(s["gate_in"], 16)
                    for g, half in enumerate((gate_spare, weights[:, :, 1, :])):
                        for k in range(KT):
                            j = k % EB
                            ins = pe_.matmul(B[5][C * j:C * j + C, HID * g:HID * g + HID], xg[:, k, C * i:C * i + C],
                                             half[:, k, :], start=(k < EB), stop=(k >= EB), skip_group_check=True)
                    ins.then_inc(s["up_done"], 1)
                    return
                for k in range(KT):
                    j = k % EB
                    if i == 0 and k == EB:
                        pe_.wait_ge(s["xg_ready"], 2 * b + 2)
                    ins = pe_.matmul(B[5][C * j:C * j + C, :].rearrange("p (g n) -> p g n", g=2), xg[:, k, C * i:C * i + C],
                                     weights[:, k, :, :], start=(k < EB), stop=(k >= EB), skip_group_check=True)
                ins.then_inc(s["up_done"], 1)

            def fold(n, first):
                pe_.wait_ge(s["u_ready"], n + 1)
                if not first:
                    pe_.wait_ge(s["g_ready"], n)
                for c in range(4):
                    ins = pe_.matmul(B[6][:, C * c:C * c + C], u_sb[:, P * c:P * c + P], const[:, CS:CS + C], start=True, stop=True)
                ins.then_inc(s["fold_done"], 1)

            def down(b, i, first, spare):
                n = EB * b + i
                if first:
                    weights, place_in, value = down_w[(i + 2) % EB], dn_in[(i + 2) % EB], 16
                elif spare:
                    weights, place_in, value = spare_down[i], dn_spare[i], 16
                else:
                    weights, place_in, value = down_w[i], dn_in[i], 16 * b + (0 if i < 2 else 16)
                pe_.wait_ge(s["g_ready"], n + 1)
                pe_.wait_ge(place_in, value)
                if first and i == 0:
                    pe_.wait_ge(s["keybc_ready"], 1)
                else:
                    pe_.wait_ge(s["y_dve"], n)
                    pe_.wait_ge(s["y_act"], n)
                for j in range(2):
                    for q in range(4):
                        ins = pe_.matmul(B[7][C * q:C * q + C, 0:256], gT[:, j, :], weights[:, j, 256 * q:256 * q + 256],
                                         start=(j == 0), stop=(j == 1), skip_group_check=True)
                ins.then_inc(s["down_done"], 1)

            def scatter(b):
                pe_.wait_ge(s["y_dve"], EB * b + EB)
                pe_.wait_ge(s["y_act"], EB * b + EB)
                pe_.wait_ge(s["back_ready"], b + 1)
                for t in range(NT):
                    for hf in range(2):
                        ins = pe_.matmul(acc[t][hf][:, :], back[:, t * P:(t + 1) * P], y_sb[:, 512 * hf:512 * hf + 512],
                                         start=False, stop=False, skip_group_check=True)
                        ins.then_inc(s["scat_done"], 1)

            def batch(b, first=False, gathered=True, ahead=True, spares_used=False):
                if not gathered:
                    pe_.wait_ge(s["hot_ready"], b + 1)
                    gather(0)
                    gather(1)
                for i in range(EB):
                    n = EB * b + i
                    if not ahead and gathered and i >= EB - 2:
                        keep_busy(8, 4)
                    up(b, i, first, spares_used and i < 2, spares_used and i == 2)
                    if i < 2 and first:
                        key_rows(i)
                    elif i == 0 and gathered:
                        scatter(b - 1)
                    if i > 0 and ahead:
                        down(b, i - 1, first, spares_used and i - 1 < 2)
                    if i == EB - 1 and ahead:
                        pe_.wait_ge(s["hot_ready"], b + 2)
                        pe_.wait_ge(s["u_ready"], n + 1)
                        gather(0)
                    fold(n, first and i == 0)
                    if i == EB - 1 and ahead:
                        gather(1)
                    if not ahead:
                        if gathered and i == EB - 1:
                            keep_busy(4, 4)
                        down(b, i, first, False)
                if ahead:
                    down(b, EB - 1, first, False)
                else:
                    if gathered:
                        keep_busy(5, 4)
                    scatter(b)

            batch(0, first=True)
            batch(1, spares_used=True)
            with pe_.Fori(2, NB - 1) as b:
                batch(b)
            batch(NB - 1, ahead=False)
            pe_.wait_ge(s["nb_ready"], 1)
            n_ov = pe_.value_load(nb_i[0:1, 0:1], min_val=0, max_val=OVB)
            with pe_.If(n_ov > 0):
                pe_.wait_ge(s["ovk_ready"], 1)
                pe_.wait_ge(s["g_ready"], EB * NB)
                pe_.matmul(B[4][:, :], ov[:, 0:P], ov_pick[:, :, :].rearrange("p b n -> p (b n)"), start=True, stop=True)
                for b in range(OVB):
                    pe_.matmul(B[6][:, b:b + 1], ov_pick[:, b, :], ov[:, P:P + 1], start=True, stop=True)
                pe_.matmul(B[6][:, P:P + EB * OVB], ov[:, 2 * P:3 * P], const[:, CI:CI + EB * OVB], start=True, stop=True).then_inc(s["ovt_done"], 1)
                with pe_.Fori(0, n_ov) as v:
                    batch(v + NB, gathered=False, ahead=False)

        @block.vector
        def _(dve):
            step = Steps(dve, "dve_step")
            dve.memset(eps[:, :], EPS)
            dve.memset(ones[:, :], 1.0).then_inc(s["setup"], 1)

            def turned(n, gain, bank, done, t, k, ready):
                dve.wait_ge(s[done], n + 1)
                dve.tensor_tensor(actT[:, k:k + 4, t * P:(t + 1) * P], B[bank][:, :].rearrange("p (k n) -> p k n", k=4),
                                  gain[:, k:k + 4].unsqueeze(2).to_broadcast([P, 4, P]), ALU.mult).then_inc(s[ready], 1)

            def permuted(x):
                return x.rearrange("p (n k) -> p k n", k=KT)

            dve.wait_ge(s["gx_in"], 16)
            for n in range(4):
                turned(n, gx, n, "xT_done", n // 2, 4 * (n % 2), "actT_ready")
            dve.wait_ge(s["x_rt"], 1)
            dve.reciprocal(r_x, ms_x).then_inc(s["rx_ready"], 1)
            dve.wait_ge(s["lat_rt"], 1)
            step(dve.reciprocal(st_l[:, 4:8], st_l[:, 0:4]))
            for t in range(NT):
                dve.tensor_scalar(latn[:, t, 0:2, :], lat[:, t, 0:QL].rearrange("p (n k) -> p k n", k=2), r_l[:, t, 0:1], None, ALU.mult)
                ins = dve.tensor_scalar(latn[:, t, 2, :], lat[:, t, QL:QL + KVL], r_l[:, t, 1:2], None, ALU.mult)
            ins.then_inc(s["latn_ready"], 1)

            def head_norm(u):
                kind, t = UNITS[u]
                d = DH if kind[0] == "m" else QK
                w = NOPE if kind == "ka" else d
                dve.wait_ge(s["sq_done"], u + 1)
                ins = dve.tensor_reduce(ms_h(u), sq[:, u % 2, 0:H * w].rearrange("p (h d) -> p h d", h=H), AX.X, ALU.add)
                if kind == "ka":
                    step(ins)
                    ins = dve.tensor_scalar(ms_h(u), ms_h(u), ms_pe[:, t:t + 1], None, ALU.add)
                ins.then_inc(s["red_done"], 1)

            def head_scale(u):
                kind, t = UNITS[u]
                dve.wait_ge(s["rt_done"], u + 1)
                dve.wait_ge(s["swap_done"], u + 1)
                if kind[0] == "m":
                    x = (mq if kind == "mq" else mk)[:, t, :].rearrange("p (h d) -> p h d", h=H)
                    dve.tensor_tensor(x, x, swp[:, u % 2, :].rearrange("p (h d) -> p h d", h=H), ALU.add)
                    d = DH
                elif kind == "qa":
                    x = qa[:, t, :].rearrange("p (h d) -> p h d", h=H)
                    dve.tensor_tensor(x[:, :, NOPE:QK], x[:, :, NOPE:QK],
                                      swp[:, u % 2, 0:H * RD].rearrange("p (h d) -> p h d", h=H), ALU.add)
                    d = QK
                else:
                    x = ka[:, t, :].rearrange("p (h d) -> p h d", h=H)
                    dve.tensor_copy(x[:, :, NOPE:QK], pe[:, t, 0, :].unsqueeze(1).to_broadcast([P, H, RD]))
                    d = QK
                step(dve.reciprocal(r_h(u), ms_h(u)))
                dve.tensor_tensor(x, x, r_h(u).unsqueeze(2).to_broadcast([P, H, d]), ALU.mult).then_inc(s["heads_ready"], 1)

            head_norm(0)
            head_norm(1)
            head_scale(0)
            head_scale(1)
            head_norm(2)
            head_scale(2)
            dve.wait_ge(s["lat_gains_in"], 16 * 2)
            for n, (lo, gain) in enumerate(((0, gql), (2, gkvl))):
                dve.wait_ge(s["latT_done"], n + 1)
                m = 2 - n
                dve.tensor_tensor(latT[:, lo:lo + m, :], B[2 + n][:, 0:m * S].rearrange("p (k n) -> p k n", k=m),
                                  gain[:, :].unsqueeze(2).to_broadcast([P, m, S]), ALU.mult).then_inc(s["latT_ready"], 1)
            head_norm(3)
            head_scale(3)
            head_norm(4)
            head_norm(5)
            head_turned(dve, 1)
            head_scale(4)
            head_norm(6)
            head_turned(dve, 3)
            head_scale(5)
            head_norm(7)
            head_scale(6)
            head_scale(7)

            def mask_max(h):
                scale = (DH if h < H else QK) ** -0.5
                dve.wait_ge(s["score_done"], h + 1)
                if h >= 3:
                    dve.wait_ge(s["exp_done"], h - 2)
                tri = const[:, CM:CM + P]
                sc, dst = B[(0, 1, 6)[h % 3]], s_sb[:, h % 3, :]
                dve.tensor_tensor_reduce(dst[:, 0:P], sc[:, 0:P], tri, 1.0, NEG, ALU.add, ALU.max, mx[:, h, 0:1])
                step(dve.tensor_tensor_reduce(dst[:, P:3 * P], sc[:, P:3 * P], wide_mask(), 1.0, NEG, ALU.add, ALU.max, mx[:, h, 1:2]))
                dve.tensor_scalar(nmx[:, h, :], mx[:, h, :], -scale, None, ALU.mult).then_inc(s["max_ready"], 1)

            def wide_mask():
                return rope[:, :, :].rearrange("p t n -> p (t n)")[:, 0:2 * P]

            def outputs(g):
                dve.wait_ge(s["pv_done"], H * g + H)
                step(dve.reciprocal(rsum[:, :, H * g:H * g + H], rsum[:, :, H * g:H * g + H]))
                for t in range(NT):
                    dve.tensor_tensor(xn[:, t, 4 * (1 - g):4 * (1 - g) + 4, :].rearrange("p k (h q) -> p k h q", h=H),
                                      B[((4, 5), (7, 4))[g][t]][:, :].rearrange("p (h q k) -> p k h q", h=H, k=4),
                                      rsum[:, t, H * g:H * g + H].unsqueeze(1).unsqueeze(3).to_broadcast([P, 4, H, DH // 4]),
                                      ALU.mult).then_inc(s["o_ready"], 1)

            dve.wait_ge(s["late_gains_in"], 16 * 5)
            dve.memset(wide_mask()[:, 0:P], 0.0)
            step(dve.tensor_copy(wide_mask()[:, P:2 * P], const[:, CM:CM + P]))
            for i in range(2 * H + 3):
                if i < 2 * H:
                    mask_max(i)
                if i < 8 and i % 2:
                    head_turned(dve, 4 + i)
                if i >= 3 and (i - 3) % 2 == 0:
                    head_pT(dve, i - 3)
                if i == H + 4:
                    outputs(0)
                if i == H + 7:
                    turned(0, go, 5, "oT_done", 0, 4, "mixT_ready")
            turned(1, go, 5, "oT_done", 1, 4, "mixT_ready")
            outputs(1)

            def add_group(g, t, banks, first, halves=(0, 1)):
                for hf in halves:
                    dve.wait_ge(s["outp_done"], first + hf + 1)
                    x = x_sb[:, t, 512 * hf:512 * hf + 512]
                    if g == 1:
                        dve.scalar_tensor_tensor(out=x, in0=B[banks[hf]][:, :], scalar=r_o[:, t, 1:2], in1=x,
                                                 op0=ALU.mult, op1=ALU.add).then_inc(s["x1b_ready"], 1)
                    else:
                        dve.wait_ge(s["x1b_ready"], 2 * t + hf + 1)
                        dve.scalar_tensor_tensor(out=xn[:, t, :, 64 * hf:64 * hf + 64], in0=permuted(B[banks[hf]][:, :]),
                                                 scalar=r_o[:, t, 0:1], in1=permuted(x), op0=ALU.mult, op1=ALU.add).then_inc(s["x1_ready"], 1)

            dve.wait_ge(s["o_rt"], 1)
            step(dve.reciprocal(st_o[:, 4:8], st_o[:, 0:4]))
            add_group(1, 0, (0, 1), 0)
            add_group(1, 1, (6, 5), 2, (0,))
            for t in range(NT):
                turned(2 + t, go, 2 + t, "oT_done", t, 0, "mixT_ready")
            add_group(1, 1, (6, 5), 2, (1,))
            add_group(0, 0, (7, 4), 4)
            add_group(0, 1, (2, 3), 6)
            for t in range(NT):
                for hf in range(2):
                    turned(2 * t + hf, gf, ((0, 1), (6, 5))[t][hf], "hT_done", t, 4 * hf, "h2T_ready")
            dve.wait_ge(s["x1_rt"], 2)
            step(dve.reciprocal(r_f, ms_f))

            dve.memset(glog[:, :, NG:], NEG)
            dve.wait_ge(s["pool_const"], 1)
            for t in range(NT):
                dve.wait_ge(s["logit_done"], t + 1)
                for dst, c0, c1 in ((glog[:, t, 0:NG], 0, NG), (elog[:, t, :], NG, NG + NE)):
                    ins = dve.scalar_tensor_tensor(out=dst, in0=B[(7, 4)[t]][:, c0:c1], scalar=r_f[:, t:t + 1],
                                                   in1=b_row[:, c0:c1], op0=ALU.mult, op1=ALU.add)
            ins.then_inc(s["lg_ready"], 1)
            dve.wait_ge(s["lg_ready"], 1)

            def both(make):
                make(0)
                step(make(1))

            both(lambda t: dve.max(top[:, t, :], glog[:, t, :]))
            both(lambda t: dve.max_index(top_i[:, t, :], top[:, t, :], glog[:, t, :]))
            dve.tensor_scalar(gneg, top[:, :, 0], -1.0, None, ALU.mult).then_inc(s["r_max"], 1)
            step(dve.tensor_copy(gnum, top_i[:, :, 0]))
            both(lambda t: dve.tensor_scalar(masked[:, t, :], g_num.rearrange("p g e -> p (g e)"), gnum[:, t:t + 1], NEG, ALU.not_equal, ALU.mult))
            step(dve.tensor_tensor(masked, masked, elog, ALU.add))
            dve.wait_ge(s["r_max"], 1)
            both(lambda t: dve.max(top[:, t, :], masked[:, t, :]))
            both(lambda t: dve.max_index(top_i[:, t, :], top[:, t, :], masked[:, t, :]))
            dve.tensor_scalar(eneg, top[:, :, 0], -1.0, None, ALU.mult).then_inc(s["r_max"], 1)
            step(dve.tensor_copy(enum, top_i[:, :, 0:2]))
            both(lambda t: dve.tensor_scalar(m01[:, t, :], e_num, enum[:, t, 1:2], None, ALU.is_equal))
            for t in range(NT):
                ins = dve.scalar_tensor_tensor(out=m01[:, t, :], in0=e_num, scalar=enum[:, t, 0:1], in1=m01[:, t, :],
                                               op0=ALU.is_equal, op1=ALU.add)
            ins.then_inc(s["rank_in"], 1)
            dve.wait_ge(s["r_exp"], 1)
            step(dve.tensor_scalar(wden, eexp, 1.0, None, ALU.add))
            step(dve.tensor_tensor(wden, wden, gsum, ALU.mult))
            step(dve.reciprocal(key_w[:, 2, :], wden))
            dve.tensor_tensor(key_w[:, 3, :], key_w[:, 2, :], eexp, ALU.mult).then_inc(s["weight_ready"], 1)
            dve.wait_ge(s["rank_done"], 1)
            step(dve.tensor_tensor(keys, B[6][:, 0:NT * NE].rearrange("p (t e) -> p t e", t=NT),
                                   e_key.unsqueeze(1).to_broadcast([P, NT, NE]), ALU.add))
            for n in range(2):
                for t in range(NT):
                    ins = dve.scalar_tensor_tensor(out=picked[:, 2 * n + t, :], in0=e_num, scalar=enum[:, t, n:n + 1], in1=keys[:, t, :],
                                                   op0=ALU.is_equal, op1=ALU.mult, accum_out=key_w[:, n, t:t + 1])
            ins.then_inc(s["key_ready"], 1)
            dve.wait_ge(s["key_ready"], 1)

            def one_hot(b):
                row = slot_row[:, bass.ds(b, 1), :].rearrange("p b n -> p (b n)")
                for t in range(NT):
                    dve.tensor_scalar(hot[:, t, :], row, key_w[:, 0, t:t + 1], None, ALU.is_equal)
                return row

            def one_hot_add(row):
                for t in range(NT):
                    ins = dve.scalar_tensor_tensor(out=hot[:, t, :], in0=row, scalar=key_w[:, 1, t:t + 1], in1=hot[:, t, :],
                                                   op0=ALU.is_equal, op1=ALU.add)
                ins.then_inc(s["hot_ready"], 1)

            row = slot_row[:, 0, :]
            both(lambda t: dve.tensor_scalar(hot[:, t, :], row, key_w[:, 0, t:t + 1], None, ALU.is_equal))
            dve.wait_ge(s["totals_done"], 1)
            dve.tensor_copy(totals, B[5][:, 0:NE])
            one_hot_add(row)

            def gathered_out(part, value):
                dve.wait_ge(s["gath_done"], value)
                dve.tensor_tensor(xg[:, 4 * part:4 * part + 4, :], B[5 - part][:, :].rearrange("p (k n) -> p k n", k=4),
                                  gf[:, 4 * part:4 * part + 4].unsqueeze(2).to_broadcast([P, 4, P]), ALU.mult).then_inc(s["xg_ready"], 1)

            gathered_out(0, 1)
            gathered_out(1, 2)
            def further_chunks():
                step(dve.tensor_tensor(there.rearrange("p (e c) -> p e c", c=OVC), totals.unsqueeze(2).to_broadcast([P, NE, OVC]),
                                       ov_thr[:, :, :], ALU.is_gt))
                step(dve.memset(scratch, 1.0))
                step(dve.tensor_tensor_scan(place, scratch, there, 0.0, ALU.mult, ALU.add))
                step(dve.tensor_scalar(small[:, 0:OVB], ov4[:, :], place[:, W - 1:W], None, ALU.is_lt))
                step(dve.tensor_reduce(small[:, 4:5], small[:, 0:OVB], AX.X, ALU.add))
                dve.tensor_copy(nb_i[:, :], small[:, 4:5]).then_inc(s["nb_ready"], 1)
                for n, table in enumerate((ov_key, ov_exp)):
                    step(dve.tensor_tensor(scratch, there, table[:, :, :].rearrange("p e c -> p (e c)"), ALU.mult))
                    step(dve.scalar_tensor_tensor(out=scratch, in0=place, scalar=ov_j[:, 0:1], in1=scratch, op0=ALU.is_equal,
                                                  op1=ALU.mult, accum_out=small[:, 6 + n:7 + n]))
                step(dve.tensor_scalar(small[:, 6:7], small[:, 6:7], -OFF, None, ALU.add))

            small = rt[:, 220:240]

            def hot_and_back(b, first, gathered, ahead):
                turn_hot = ahead or not gathered
                if ahead:
                    dve.wait_ge(s["gath_done"], 2 * b + 2)
                    row = one_hot(b + 1)
                elif not gathered:
                    dve.wait_ge(s["gath_done"], 2 * b)
                    row = one_hot(b)
                if first:
                    dve.wait_ge(s["keybc_ready"], 2)
                for m in range(2):
                    ins = dve.tensor_scalar(back2[:, m, :], key_bc[:, m, :, :].rearrange("p t n -> p (t n)"),
                                            slot_col[:, bass.ds(b, 1)], None, ALU.is_equal)
                ins.then_inc(s["hot_half"], 1)
                dve.wait_ge(s["hot_half"], b + 1)
                if turn_hot:
                    one_hot_add(row)
                for m in range(2):
                    ins = dve.tensor_tensor(back2[:, m, :], back2[:, m, :], key_bc[:, 2 + m, :, :].rearrange("p t n -> p (t n)"), ALU.mult)
                ins.then_inc(s["back_half"], 1)
                dve.wait_ge(s["back_half"], b + 1)
                if not first:
                    dve.wait_ge(s["scat_done"], 4 * b)
                dve.tensor_tensor(back, back2[:, 0, :], back2[:, 1, :], ALU.add).then_inc(s["back_ready"], 1)

            def product(n, first):
                dve.wait_ge(s["sil_ready"], n + 1)
                if not first:
                    dve.wait_ge(s["down_done"], n)
                dve.tensor_tensor(gT, sil.rearrange("p (j n) -> p j n", j=2), B[6][:, 2 * C:4 * C].rearrange("p (j n) -> p j n", j=2),
                                  ALU.mult).then_inc(s["g_ready"], 1)

            def outputs_up(b, i):
                dve.wait_ge(s["down_done"], EB * b + i + 1)
                for q in (0, 1):
                    ins = dve.tensor_copy(y_sb[C * i:C * i + C, 256 * q:256 * q + 256], B[7][C * q:C * q + C, 0:256])
                ins.then_inc(s["y_dve"], 1)

            def batch(b, first=False, gathered=True, ahead=True):
                if not first:
                    hot_and_back(b, first, gathered, ahead)
                if not gathered:
                    gathered_out(0, 2 * b + 1)
                    gathered_out(1, 2 * b + 2)
                for i in range(EB):
                    if i > 0 and ahead:
                        outputs_up(b, i - 1)
                    if i == EB - 1 and ahead:
                        gathered_out(0, 2 * b + 3)
                    product(EB * b + i, first and i == 0)
                    if i == EB - 1 and ahead:
                        gathered_out(1, 2 * b + 4)
                    if i == 1 and first:
                        hot_and_back(b, first, gathered, ahead)
                    if first and i == 2:
                        further_chunks()
                    if not ahead:
                        outputs_up(b, i)
                if ahead:
                    outputs_up(b, EB - 1)

            batch(0, first=True)
            with dve.Fori(1, NB - 1) as b:
                batch(b)
            batch(NB - 1, ahead=False)
            n_ov = dve.value_load(nb_i[0:1, 0:1], min_val=0, max_val=OVB)
            with dve.If(n_ov > 0):
                dve.tensor_scalar(ov[:, 0:P], ones[:, :], small[:, 6:7], None, ALU.mult)
                dve.tensor_scalar(ov[:, 2 * P:3 * P], ones[:, :], small[:, 7:8], None, ALU.mult)
                dve.tensor_copy(ov[:, P:P + 1], small[:, 6:7]).then_inc(s["ovk_ready"], 1)
                dve.wait_ge(s["ovt_done"], 1)
                for b in range(OVB):
                    dve.tensor_tensor(slot_row[:, NB + b, :].rearrange("p (i c) -> p i c", i=EB),
                                      B[4][:, b * P:(b + 1) * P].rearrange("p (i c) -> p i c", i=EB),
                                      slot_row[:, 0, 0:C].unsqueeze(1).to_broadcast([P, EB, C]), ALU.add)
                for i in range(EB):
                    dve.tensor_scalar(slot_col[C * i:C * i + C, NB:], B[6][C * i:C * i + C, 0:OVB],
                                      slot_col[C * i:C * i + C, 0:1], float(-i * KEY), ALU.add, ALU.add)
                dve.tensor_copy(eid_i[:, :], B[6][:, P:P + EB * OVB]).then_inc(s["ov_ready"], 1)
                dve.wait_ge(s["ov_ready"], 1)
                with dve.Fori(0, n_ov) as v:
                    batch(v + NB, gathered=False, ahead=False)
                dve.wait_ge(s["scat_done"], 4 * n_ov + 4 * NB)
                dve.memset(small[:, 9:10], 0.0)
            for t in range(NT):
                for hf in range(2):
                    dve.wait_ge(s["scat_done"], 4 * NB - 3 + 2 * t + hf)
                    dve.tensor_copy(staged[:, t, 512 * hf:512 * hf + 512], B[2 * t + hf][:, :]).then_inc(s["y_out"], 1)


_SHAPES = "x attn_norm_g w_in mla_q_lat_g w_q_up mla_kv_lat_g w_kv_up mla_q_head_g mla_k_head_g moba_q_head_g moba_k_head_g out_norm_mla_g out_norm_moba_g w_out ffn_norm_g w_router_group b_router_group w_router_expert b_router_expert w_gate w_up w_down".split()


def kernel(**inputs):
    import concourse.bacc as bacc
    from concourse.bass_utils import run_bass_kernel_spmd

    nc = bacc.Bacc("TRN2", target_bir_lowering=False, num_devices=1)
    arrays = {n: np.ascontiguousarray(inputs[n]) for n in _SHAPES}
    arrays["consts"], arrays["rope"] = shape_constants()
    arrays = {f"in_{n}": v for n, v in arrays.items()}
    aps = {n[3:]: nc.dram_tensor(n, v.shape, mybir.dt.from_np(v.dtype), kind="ExternalInput").ap() for n, v in arrays.items()}
    out = nc.dram_tensor("y", (1, S, D), F32, kind="ExternalOutput").ap()
    layer(nc, aps, out)
    r = run_bass_kernel_spmd(nc, [arrays], core_ids=[0])
    return r.results[0]["y"]
```
